# Optimizing a Trainium2 kernel written in Bass

```python
import math
import jax, jax.numpy as jnp
from jax import lax
import numpy as np

D_MODEL = 1024
BATCH = 1
SEQ = 256
DEPTH = 2

N_MIXERS = 3
Q_BLK = 128
NORM_EPS = 1e-5
RMS_EPS = 1e-6

REL_BUCKETS = 32
REL_MAX_DIST = 2048
REL_HEADS = 16

A_HEADS = 16
A_HEAD_DIM = 128
A_IDX_HEADS = 8
A_IDX_DIM = 64
A_TOPK_MAX = 256
A_Q = A_HEADS * A_HEAD_DIM
A_SPLITS = (A_Q, A_Q + A_HEAD_DIM, A_Q + 2 * A_HEAD_DIM,
            A_Q + 2 * A_HEAD_DIM + A_IDX_HEADS * A_IDX_DIM,
            A_Q + 2 * A_HEAD_DIM + A_IDX_HEADS * A_IDX_DIM + A_IDX_DIM)
A_IN = A_SPLITS[-1] + A_IDX_HEADS

B_GROUPS = ((128, 1), (512, 4), (2048, 16))
B_HEADS = 16
B_HEAD_DIM = 64
B_IN = len(B_GROUPS) * 3 * B_HEADS * B_HEAD_DIM

C_HEADS = 16
C_Q_RANK = 256
C_KV_RANK = 128
C_NOPE = 64
C_ROPE = 32
C_V = 64
C_IN = C_Q_RANK + C_KV_RANK + C_ROPE
ROPE_BASE = 10000.0

N_EXPERTS = 64
TOP_K = 8
N_GROUPS = 8
TOPK_GROUPS = 4
D_EXPERT = 256
D_SHARED = 256
ROUTED_SCALE = 2.5
MOE_BLK = 256

DN_ALPHA = (2 * DEPTH) ** 0.25
DN_BETA = (8 * DEPTH) ** -0.25
N_A = len(range(0, DEPTH, N_MIXERS))
N_B = len(range(1, DEPTH, N_MIXERS))
N_C = len(range(2, DEPTH, N_MIXERS))

kernel_name = 'hybrid_dsa_dilated_mla_moe_deepnorm'

def layer_norm(x, g, b):
    xf = x.astype(jnp.float32)
    mu = jnp.mean(xf, axis=-1, keepdims=True)
    var = jnp.mean(jnp.square(xf - mu), axis=-1, keepdims=True)
    return ((xf - mu) * lax.rsqrt(var + NORM_EPS) * g.astype(jnp.float32) + b.astype(jnp.float32)).astype(x.dtype)

def rms_norm(x, g):
    xf = x.astype(jnp.float32)
    y = xf * lax.rsqrt(jnp.mean(jnp.square(xf), axis=-1, keepdims=True) + RMS_EPS)
    return (y * g.astype(jnp.float32)).astype(x.dtype)

def rope(x, pos):
    half = x.shape[-1] // 2
    inv = ROPE_BASE ** (-jnp.arange(half, dtype=jnp.float32) / half)
    ang = pos.astype(jnp.float32)[:, None] * inv[None, :]
    cos, sin = jnp.cos(ang)[:, None, :], jnp.sin(ang)[:, None, :]
    xf = x.astype(jnp.float32)
    x1, x2 = xf[..., :half], xf[..., half:]
    return jnp.concatenate([x1 * cos - x2 * sin, x1 * sin + x2 * cos], axis=-1).astype(x.dtype)

def t5_bucket(dist):
    exact = REL_BUCKETS // 2
    d_f = jnp.maximum(dist, 1).astype(jnp.float32)
    large = exact + (jnp.log(d_f / exact) / math.log(REL_MAX_DIST / exact) * (REL_BUCKETS - exact)).astype(jnp.int32)
    return jnp.where(dist < exact, dist, jnp.minimum(large, REL_BUCKETS - 1))

def t5_bias(rel_bias, dist):
    return rel_bias[t5_bucket(dist)]

def to_blocks(a):
    b, s = a.shape[0], a.shape[1]
    return jnp.swapaxes(a.reshape(b, s // Q_BLK, Q_BLK, *a.shape[2:]), 0, 1)

def from_blocks(a):
    a = jnp.swapaxes(a, 0, 1)
    return a.reshape(a.shape[0], a.shape[1] * a.shape[2], *a.shape[3:])

def dsa_mixer(x, w_in, w_o, rel_bias):
    bsz, seq, _ = x.shape
    k_sel = min(A_TOPK_MAX, seq // 4)
    q, k, v, qi, ki, wi = jnp.split(x @ w_in, list(A_SPLITS), axis=-1)
    q = q.reshape(bsz, seq, A_HEADS, A_HEAD_DIM)
    qi = qi.reshape(bsz, seq, A_IDX_HEADS, A_IDX_DIM)
    ki = ki.astype(jnp.float32)
    pos = jnp.arange(seq)
    gather = jax.vmap(lambda a, i: a[i])

    def block(args):
        start, q_b, qi_b, wi_b = args
        t = start + jnp.arange(Q_BLK)
        rel = jax.nn.relu(jnp.einsum('bthe,bse->bhts', qi_b.astype(jnp.float32), ki) * A_IDX_DIM ** -0.5)
        score = jnp.einsum('bth,bhts->bts', wi_b.astype(jnp.float32) * A_IDX_HEADS ** -0.5, rel)
        score = jnp.where(pos[None, :] <= t[:, None], score, -jnp.inf)
        _, idx = lax.top_k(score, k_sel)
        k_g, v_g = gather(k, idx), gather(v, idx)
        logits = jnp.einsum('bthe,btke->bhtk', q_b, k_g).astype(jnp.float32) * A_HEAD_DIM ** -0.5
        dist = t[None, :, None] - idx
        logits = logits + jnp.moveaxis(t5_bias(rel_bias, jnp.maximum(dist, 0)), -1, 1).astype(jnp.float32)
        logits = jnp.where((dist >= 0)[:, None], logits, -jnp.inf)
        p = jax.nn.softmax(logits, axis=-1).astype(v.dtype)
        return jnp.einsum('bhtk,btke->bthe', p, v_g)

    starts = jnp.arange(seq // Q_BLK) * Q_BLK
    o = lax.map(block, (starts, to_blocks(q), to_blocks(qi), to_blocks(wi)))
    return from_blocks(o).reshape(bsz, seq, A_Q) @ w_o

def dilated_group(q, k, v, rel_bias, window, dil):
    bsz, seq, nh, hd = q.shape
    n = window // dil
    span = n * dil
    sp = -(-seq // span) * span
    nb = sp // span

    def split(a):
        a = jnp.pad(a, ((0, 0), (0, sp - seq), (0, 0), (0, 0)))
        return a.reshape(bsz, nb, n, dil, nh, hd)

    def with_prev(a):
        prev = jnp.pad(a, ((0, 0), (1, 0), (0, 0), (0, 0), (0, 0), (0, 0)))[:, :-1]
        return jnp.concatenate([prev, a], axis=2)

    qs = split(q)
    kk, vv = with_prev(split(k)), with_prev(split(v))
    logits = jnp.einsum('bcirhe,bcjrhe->bcrhij', qs, kk).astype(jnp.float32) * hd ** -0.5
    ii = jnp.arange(n)[:, None]
    jj = jnp.arange(2 * n)[None, :]
    delta = n + ii - jj
    band = (delta >= 0) & (delta <= n)
    exists = (jnp.arange(nb)[:, None, None] > 0) | (jj[None] >= n)
    mask = band[None] & exists
    bias = jnp.transpose(t5_bias(rel_bias, jnp.maximum(delta, 0) * dil), (2, 0, 1))
    logits = logits + bias.astype(jnp.float32)
    logits = jnp.where(mask[None, :, None, None], logits, -jnp.inf)
    lse = jax.nn.logsumexp(logits, axis=-1)
    p = jnp.exp(logits - lse[..., None]).astype(v.dtype)
    o = jnp.einsum('bcrhij,bcjrhe->bcirhe', p, vv).reshape(bsz, sp, nh, hd)[:, :seq]
    lse = jnp.transpose(lse, (0, 1, 4, 2, 3)).reshape(bsz, sp, nh)[:, :seq]
    return o, lse

def dilated_mixer(x, w_in, w_o, rel_bias):
    bsz, seq, _ = x.shape
    proj = (x @ w_in).reshape(bsz, seq, len(B_GROUPS), 3, B_HEADS, B_HEAD_DIM)
    outs, lses = [], []
    for g, (window, dil) in enumerate(B_GROUPS):
        o, l = dilated_group(proj[:, :, g, 0], proj[:, :, g, 1], proj[:, :, g, 2], rel_bias, window, dil)
        outs.append(o)
        lses.append(l)
    wts = jax.nn.softmax(jnp.stack(lses, axis=2), axis=2)
    o = jnp.einsum('bsgh,bsghe->bshe', wts.astype(x.dtype), jnp.stack(outs, axis=2))
    return o.reshape(bsz, seq, B_HEADS * B_HEAD_DIM) @ w_o

def mla_mixer(x, w_in, q_norm, kv_norm, w_q_up, w_kv_up, w_o):
    bsz, seq, _ = x.shape
    c_q, c_kv, k_r = jnp.split(x @ w_in, [C_Q_RANK, C_Q_RANK + C_KV_RANK], axis=-1)
    q = (rms_norm(c_q, q_norm) @ w_q_up).reshape(bsz, seq, C_HEADS, C_NOPE + C_ROPE)
    kv = (rms_norm(c_kv, kv_norm) @ w_kv_up).reshape(bsz, seq, C_HEADS, C_NOPE + C_V)
    pos = jnp.arange(seq)
    q_nope, q_rope = q[..., :C_NOPE], rope(q[..., C_NOPE:], pos)
    k_rope = rope(k_r[:, :, None, :], pos)[:, :, 0]
    k_nope, v = kv[..., :C_NOPE], kv[..., C_NOPE:]
    scale = (C_NOPE + C_ROPE) ** -0.5

    def block(args):
        start, qn_b, qr_b = args
        t = start + jnp.arange(Q_BLK)
        logits = (jnp.einsum('bthe,bshe->bhts', qn_b, k_nope)
                  + jnp.einsum('bthe,bse->bhts', qr_b, k_rope)).astype(jnp.float32) * scale
        logits = jnp.where(pos[None, :] <= t[:, None], logits, -jnp.inf)
        p = jax.nn.softmax(logits, axis=-1).astype(v.dtype)
        return jnp.einsum('bhts,bshe->bthe', p, v)

    starts = jnp.arange(seq // Q_BLK) * Q_BLK
    o = lax.map(block, (starts, to_blocks(q_nope), to_blocks(q_rope)))
    return from_blocks(o).reshape(bsz, seq, C_HEADS * C_V) @ w_o

def swiglu(x, w_gate, w_up, w_down):
    return (jax.nn.silu(x @ w_gate) * (x @ w_up)) @ w_down

def grouped_experts(tok, eidx, gate, w_gate, w_up, w_down):
    n_tok, d = tok.shape
    n_asg = n_tok * TOP_K
    flat_e = eidx.reshape(-1)
    order = jnp.argsort(flat_e)
    sorted_e = flat_e[order]
    counts = jnp.bincount(flat_e, length=N_EXPERTS)
    padded = (counts + MOE_BLK - 1) // MOE_BLK * MOE_BLK
    pad_end = jnp.cumsum(padded)
    pad_start = pad_end - padded
    start = jnp.cumsum(counts) - counts
    dest = pad_start[sorted_e] + jnp.arange(n_asg) - start[sorted_e]
    n_blk = -(-n_asg // MOE_BLK) + N_EXPERTS
    n_slot = n_blk * MOE_BLK
    slot_tok = jnp.full((n_slot,), n_tok, jnp.int32).at[dest].set((order // TOP_K).astype(jnp.int32))
    slot_w = jnp.zeros((n_slot,), gate.dtype).at[dest].set(gate.reshape(-1)[order])
    blk_e = jnp.minimum(jnp.searchsorted(pad_end, jnp.arange(n_blk) * MOE_BLK, side='right'), N_EXPERTS - 1)
    tok_pad = jnp.concatenate([tok, jnp.zeros((1, d), tok.dtype)], axis=0)

    def block(args):
        e, rows, wts = args
        xb = tok_pad[rows]
        return swiglu(xb, w_gate[e], w_up[e], w_down[e]) * wts[:, None].astype(xb.dtype)

    out = lax.map(block, (blk_e, slot_tok.reshape(n_blk, MOE_BLK), slot_w.reshape(n_blk, MOE_BLK)))
    return jax.ops.segment_sum(out.reshape(n_slot, d), slot_tok, num_segments=n_tok + 1)[:n_tok]

def moe(h, w_router, e_bias, w_gate, w_up, w_down, ws_gate, ws_up, ws_down):
    bsz, seq, d = h.shape
    tok = h.reshape(-1, d)
    n_tok = tok.shape[0]
    scores = jax.nn.sigmoid((tok @ w_router).astype(jnp.float32))
    choice = scores + e_bias.astype(jnp.float32)
    grp_score = lax.top_k(choice.reshape(n_tok, N_GROUPS, N_EXPERTS // N_GROUPS), 2)[0].sum(-1)
    _, gi = lax.top_k(grp_score, TOPK_GROUPS)
    gmask = jnp.sum(jax.nn.one_hot(gi, N_GROUPS, dtype=jnp.float32), axis=1) > 0
    choice = jnp.where(jnp.repeat(gmask, N_EXPERTS // N_GROUPS, axis=1), choice, -jnp.inf)
    _, eidx = lax.top_k(choice, TOP_K)
    gate = jnp.take_along_axis(scores, eidx, axis=-1)
    gate = gate / jnp.sum(gate, axis=-1, keepdims=True) * ROUTED_SCALE
    routed = grouped_experts(tok, eidx, gate, w_gate, w_up, w_down)
    return (routed + swiglu(tok, ws_gate, ws_up, ws_down)).reshape(bsz, seq, d)

def setup_inputs(seed: int = 0) -> dict:
    key = jax.random.key(seed)
    keys = iter(jax.random.split(key, 32))

    def nrm(shape, fan_in, scale=1.0):
        return jax.random.normal(next(keys), shape, jnp.float32) * (scale * fan_in ** -0.5)

    def gain(shape):
        return 1.0 + 0.02 * jax.random.normal(next(keys), shape, jnp.float32)

    d = D_MODEL
    return {
        'x': jax.random.normal(next(keys), (BATCH, SEQ, d), jnp.float32),
        'rel_bias': 0.2 * jax.random.normal(next(keys), (REL_BUCKETS, REL_HEADS), jnp.float32),
        'a_w_in': nrm((N_A, d, A_IN), d),
        'a_w_o': nrm((N_A, A_Q, d), A_Q, DN_BETA),
        'b_w_in': nrm((N_B, d, B_IN), d),
        'b_w_o': nrm((N_B, B_HEADS * B_HEAD_DIM, d), B_HEADS * B_HEAD_DIM, DN_BETA),
        'c_w_in': nrm((N_C, d, C_IN), d),
        'c_q_norm': gain((N_C, C_Q_RANK)),
        'c_kv_norm': gain((N_C, C_KV_RANK)),
        'c_w_q_up': nrm((N_C, C_Q_RANK, C_HEADS * (C_NOPE + C_ROPE)), C_Q_RANK),
        'c_w_kv_up': nrm((N_C, C_KV_RANK, C_HEADS * (C_NOPE + C_V)), C_KV_RANK),
        'c_w_o': nrm((N_C, C_HEADS * C_V, d), C_HEADS * C_V, DN_BETA),
        'ln_g': gain((DEPTH, 2, d)),
        'ln_b': 0.02 * jax.random.normal(next(keys), (DEPTH, 2, d), jnp.float32),
        'moe_w_router': nrm((DEPTH, d, N_EXPERTS), d),
        'moe_bias': 0.01 * jax.random.normal(next(keys), (DEPTH, N_EXPERTS), jnp.float32),
        'moe_w_gate': nrm((DEPTH, N_EXPERTS, d, D_EXPERT), d),
        'moe_w_up': nrm((DEPTH, N_EXPERTS, d, D_EXPERT), d),
        'moe_w_down': nrm((DEPTH, N_EXPERTS, D_EXPERT, d), D_EXPERT, DN_BETA),
        'moe_ws_gate': nrm((DEPTH, d, D_SHARED), d),
        'moe_ws_up': nrm((DEPTH, d, D_SHARED), d),
        'moe_ws_down': nrm((DEPTH, D_SHARED, d), D_SHARED, DN_BETA),
    }

def reference(x, rel_bias, a_w_in, a_w_o, b_w_in, b_w_o, c_w_in, c_q_norm, c_kv_norm,
              c_w_q_up, c_w_kv_up, c_w_o, ln_g, ln_b, moe_w_router, moe_bias, moe_w_gate,
              moe_w_up, moe_w_down, moe_ws_gate, moe_ws_up, moe_ws_down):
    h = x
    for layer in range(DEPTH):
        kind, slot = layer % N_MIXERS, layer // N_MIXERS
        if kind == 0:
            mix = dsa_mixer(h, a_w_in[slot], a_w_o[slot], rel_bias)
        elif kind == 1:
            mix = dilated_mixer(h, b_w_in[slot], b_w_o[slot], rel_bias)
        else:
            mix = mla_mixer(h, c_w_in[slot], c_q_norm[slot], c_kv_norm[slot],
                            c_w_q_up[slot], c_w_kv_up[slot], c_w_o[slot])
        h = layer_norm(DN_ALPHA * h + mix, ln_g[layer, 0], ln_b[layer, 0])
        ff = moe(h, moe_w_router[layer], moe_bias[layer], moe_w_gate[layer], moe_w_up[layer],
                 moe_w_down[layer], moe_ws_gate[layer], moe_ws_up[layer], moe_ws_down[layer])
        h = layer_norm(DN_ALPHA * h + ff, ln_g[layer, 1], ln_b[layer, 1])
    return h


_drawn_inputs = setup_inputs


def setup_inputs(seed=0):
    import zlib

    import numpy as np

    out = dict(_drawn_inputs(seed))
    spreads = {}
    factors = {}
    for name, (base, spread) in spreads.items():
        noise = np.random.default_rng([zlib.crc32(name.encode()), seed]).standard_normal(out[name].shape)
        drawn = base * np.exp(spread * noise) if base else spread * noise
        out[name] = __import__('jax').numpy.asarray(drawn.astype(out[name].dtype))
    for name, factor in factors.items():
        out[name] = (out[name] * factor).astype(out[name].dtype)
    return out
```

```python
import math
from contextlib import ExitStack

import numpy as np

import concourse.bass as bass
from concourse import mybir

F32 = mybir.dt.float32
F32R = mybir.dt.float32r
ALU = mybir.AluOpType
ACT = mybir.ActivationFunctionType
AX = mybir.AxisListType

D_MODEL, SEQ, DEPTH = 1024, 256, 2
P = 128
KC = D_MODEL // P
TC = SEQ // P
REL_BUCKETS, REL_MAX_DIST, REL_HEADS = 32, 2048, 16
A_HEADS, A_HD, IDX_HEADS, IDX_HD = 16, 128, 8, 64
TOPK_KEYS = min(256, SEQ // 4)
B_GROUPS = ((128, 1), (512, 4), (2048, 16))
B_HEADS, B_HD = 16, 64
N_EXPERTS, TOP_K, N_GROUPS, TOPK_GROUPS, D_EXPERT = 64, 8, 8, 4, 256
GROUP = N_EXPERTS // N_GROUPS
ROUTED_SCALE = 2.5
NORM_EPS = 1e-5
DN_ALPHA = (2 * DEPTH) ** 0.25
MASKED = -1e30
TAKEN = -3e38
LINE = 3 * P
STEPS = A_HEADS // 2
UNIT = KC * D_EXPERT


def wait(eng, sem, value):
    if isinstance(value, int) and value <= 0:
        return
    eng.wait_ge(sem, value)


def build(nc, t, out):
    with ExitStack() as ctx:
        def sem(name):
            return ctx.enter_context(nc.semaphore(name))

        spent = []

        def phase_sems(scope, made):
            before = {s.num for s in spent}

            def f(name):
                s = scope.enter_context(nc.semaphore(name))
                assert s.num not in before
                made.append(s)
                return s
            return f

        def clear_spent(pool, old):
            for s in old:
                pool.sem_clear(s)

        def sb(name, shape, dt=F32):
            return ctx.enter_context(nc.sbuf_tensor(name, shape, dt))

        ident = sb("ident", [P, P])
        h = sb("h", [P, TC, D_MODEL])
        xTh = sb("xTh", [P, KC, SEQ], F32R)
        xTl = sb("xTl", [P, KC, SEQ], F32R)
        gate_rows = sb("gate_rows", [P, 2, SEQ])
        stats = sb("stats", [P, TC, 2, 6])
        mv = sb("mv", [P, TC, 2])
        rstd = sb("rstd", [P, TC])
        raw = sb("raw", [P, 6, UNIT])
        arena_at = nc.sbuf_base
        top = nc.sbuf_usable_end

        class Arena:
            def __init__(self, tag, start=0):
                self.tag, self.at = tag, arena_at + start

            def __call__(self, name, shape, dt=F32):
                size = 4 * int(np.prod(shape[1:]))
                x = nc.alloc_sbuf_tensor_at(f"{self.tag}_{name}", shape, dt, offset=self.at)
                self.at += (size + 31) // 32 * 32
                assert self.at <= top, (self.tag, name, self.at, top)
                return x

        psum = ctx.enter_context(nc.psum_tensor("psum", [P, 8, 512], F32))

        lines_d = nc.dram_tensor("bias_lines", [1 + len(B_GROUPS), REL_HEADS, LINE], F32, kind="Internal").ap()
        gates_d = [nc.dram_tensor(f"gates{l}", [N_EXPERTS, SEQ], F32, kind="Internal").ap() for l in range(DEPTH)]

        def bias_tile(table, nt, j, n):
            base = lines_d[table:table + nt, bass.ds(2 * j, 2) if not isinstance(j, int) else slice(2 * j, 2 * j + 2), :]
            return bass.AP(base.tensor, base.offset,
                           [[1, P], [REL_HEADS * LINE, nt], [LINE, 2], [1, n]])

        def attention(tag, G, scale, xT, pieces, project, load_first, load_loop, load_after, bias_ready, bias_of,
                      q_of, k_of, v_of, evac_piece, o_step, o_chunks, wo_view, wo_units, ar, extra_pool=None):
            PP = pieces
            S = ar("scores", [P, 2, G, LINE])
            pT = ar("pT", [P, 3, LINE])
            smax = ar("smax", [P, 2, TC])
            nmax = ar("nmax", [P, 2, TC])
            ssum = ar("ssum", [P, 2, TC])
            sinv = ar("sinv", [P, 2, TC])
            oT = ar("oT", [P, o_chunks, SEQ])
            wo = ar("wo", [P, 4, 2, D_MODEL])
            prob = ar("prob", [P, 2, G, LINE])

            pr_done, pr_free = sem(tag + "proj_done"), sem(tag + "proj_free")
            qk_done, stt_done = sem(tag + "qk_done"), sem(tag + "logits_done")
            red_done, max_done = sem(tag + "red_done"), sem(tag + "max_done")
            ex_done, rc_done, nrm = sem(tag + "exp_done"), sem(tag + "recip_done"), sem(tag + "norm_done")
            tr_done, pt_ev, pv_done = sem(tag + "tr_done"), sem(tag + "pT_ready"), sem(tag + "pv_done")
            ot_ev, y_done = sem(tag + "oT_ready"), sem(tag + "y_done")
            wo_in = [sem(f"{tag}wo_in{i}") for i in range(4)]
            wo_used = sem(tag + "wo_used")
            SL, ST, OT = psum[:, 2:5, :], psum[:, 5:7, :], psum[:, 7, :]

            def loop(eng, stage):
                stage(0, 0, 0)
                with eng.Fori(0, STEPS // 2 - 1) as it:
                    stage(2 * it + 1, 1, it)
                    stage(2 * it + 2, 0, it + 1)
                stage(STEPS - 1, 1, STEPS // 2 - 1)

            with nc.Block() as block:
                @block.sync
                def _(sp):
                    load_first(sp, pr_done)
                    for u in range(4):
                        sp.dma_start(wo[:, u, :, :], wo_view(u)).then_inc(wo_in[u], 16)
                    load_loop(sp, pr_done, stt_done)
                    sp.wait_ge(pr_done, PP * STEPS)
                    load_after(sp)
                    for u in range(4, wo_units):
                        sp.wait_ge(wo_used, u - 3)
                        sp.dma_start(wo[:, u % 4, :, :], wo_view(u)).then_inc(wo_in[u % 4], 16)

                if extra_pool:
                    @block.gpsimd
                    def _(pool):
                        extra_pool(pool, stt_done)

                @block.tensor
                def _(pe):
                    def piece(j, b, half, i):
                        wait(pe, pr_free, PP * j + i - 1)
                        project(pe, j, b, half, i).then_inc(pr_done, 1)

                    def stage(j, b, half):
                        for c in range(2):
                            r = 2 * j + c
                            pe.wait_ge(pr_free, PP * j + PP)
                            wait(pe, stt_done, r)
                            for g in range(G):
                                bank = psum[:, 2 + (c if G == 1 else g), :]
                                for a in range(TC):
                                    last = pe.matmul(bank[:, a * P:a * P + P * (a + 1)], q_of(b, c, g, a), k_of(b, c, g, a),
                                                     start=True, stop=True)
                            last.then_inc(qk_done, 1)
                            if not (isinstance(j, int) and j == STEPS - 1):
                                for i in range(c * PP // 2, (c + 1) * PP // 2):
                                    nb, nhalf = 1 - b, (half if b == 0 else half + 1)
                                    piece(j + 1, nb, nhalf, i)
                            pe.wait_ge(nrm, 2 * r + 2)

                            def trans(g):
                                w = G * r + g
                                wait(pe, pt_ev, w - 1)
                                for s in range(3):
                                    last = pe.transpose(ST[:, (c * G + g) % 2, s * P:s * P + P], prob[:, c, g, s * P:s * P + P],
                                                        ident[:, :])
                                last.then_inc(tr_done, 1)

                            def pv(g):
                                w = G * r + g
                                pe.wait_ge(pt_ev, w + 1)
                                if c == 0 and g == 0:
                                    wait(pe, ot_ev, j)
                                o = o_step(OT, c)
                                slot = g if G > 1 else c
                                pe.matmul(o[:, 0:SEQ], v_of(b, c, g, 0), pT[:, slot, 0:2 * P], start=(g == 0), stop=False)
                                pe.matmul(o[:, P:SEQ], v_of(b, c, g, 1), pT[:, slot, 2 * P:3 * P], start=False,
                                          stop=(g == G - 1)).then_inc(pv_done, 1)

                            trans(0)
                            for g in range(1, G):
                                trans(g)
                                pv(g - 1)
                            pv(G - 1)

                    for i in range(PP):
                        piece(0, 0, 0, i)
                    loop(pe, stage)
                    pe.wait_ge(ot_ev, STEPS)
                    for u in range(wo_units):
                        pe.wait_ge(wo_in[u % 4], 16 * (u // 4 + 1))
                        for cc in range(2):
                            for a in range(TC):
                                for n in range(2):
                                    last = pe.matmul(psum[:, 2 * a + n, :], oT[:, 2 * u + cc, a * P:a * P + P],
                                                     wo[:, u % 4, cc, n * 512:n * 512 + 512],
                                                     start=(u == 0 and cc == 0), stop=(u == wo_units - 1 and cc == 1))
                        last.then_inc(wo_used, 1)

                @block.scalar
                def _(act):
                    def evac(j, b, i):
                        act.wait_ge(pr_done, PP * j + i + 1)
                        evac_piece(act, b, i).then_inc(pr_free, 1)

                    def stage(j, b, half):
                        for c in range(2):
                            r = 2 * j + c
                            act.wait_ge(max_done, r + 1)
                            wait(act, tr_done, G * (r - 1))
                            for a in range(TC):
                                act.activation(prob[:, c, :, a * P:a * P + P * (a + 1)], S[:, c, :, a * P:a * P + P * (a + 1)],
                                               ACT.Exp, bias=nmax[:, c, a:a + 1],
                                               accum_out=ssum[:, c, a:a + 1]).then_inc(ex_done, 1)
                            if not (isinstance(j, int) and j == STEPS - 1):
                                if c == 0:
                                    wait(act, pv_done, 2 * G * j)
                                for i in range(c * PP // 2, (c + 1) * PP // 2):
                                    evac(j + 1, 1 - b, i)
                            for g in range(G):
                                w = G * r + g
                                act.wait_ge(tr_done, w + 1)
                                wait(act, pv_done, w - (2 if G > 1 else 1))
                                act.activation(pT[:, g if G > 1 else c, :], ST[:, (c * G + g) % 2, 0:LINE], ACT.Copy).then_inc(pt_ev, 1)
                        act.wait_ge(pv_done, 2 * G * (j + 1))
                        o_evac(act, j)

                    def o_evac(act, j):
                        per = o_chunks // STEPS
                        act.activation(oT[:, bass.ds(per * j, per), :] if not isinstance(j, int) else oT[:, per * j:per * j + per, :],
                                       OT[:, 0:per * SEQ].rearrange("p (c t) -> p c t", c=per), ACT.Copy).then_inc(ot_ev, 1)

                    for i in range(PP):
                        evac(0, 0, i)
                    loop(act, stage)

                @block.vector
                def _(dve):
                    def stage(j, b, half):
                        for c in range(2):
                            r = 2 * j + c
                            if c == 0:
                                bias_ready(dve, j, b, half)
                            dve.wait_ge(qk_done, r + 1)
                            wait(dve, ex_done, 2 * (r - 1))
                            src = psum[:, 2 + c, 0:LINE] if G == 1 else SL[:, :, 0:LINE]
                            dst = S[:, c, 0, :] if G == 1 else S[:, c, :, :]
                            dve.scalar_tensor_tensor(out=dst, in0=src, scalar=scale, in1=bias_of(b, c), op0=ALU.mult,
                                                     op1=ALU.add).then_inc(stt_done, 1)
                            dve.wait_ge(stt_done, r + 1)
                            for a in range(TC):
                                dve.tensor_reduce(smax[:, c, a:a + 1], S[:, c, :, a * P:a * P + P * (a + 1)], AX.XY, ALU.max)\
                                   .then_inc(red_done, 1)
                            dve.wait_ge(red_done, 2 * r + 2)
                            dve.tensor_scalar(nmax[:, c, :], smax[:, c, :], -1.0, None, ALU.mult).then_inc(max_done, 1)
                            dve.wait_ge(ex_done, 2 * r + 2)
                            dve.reciprocal(sinv[:, c, :], ssum[:, c, :]).then_inc(rc_done, 1)
                            dve.wait_ge(rc_done, r + 1)
                            for a in range(TC):
                                dve.tensor_scalar(prob[:, c, :, a * P:a * P + P * (a + 1)], prob[:, c, :, a * P:a * P + P * (a + 1)],
                                                  sinv[:, c, a:a + 1], None, ALU.mult).then_inc(nrm, 1)
                    loop(dve, stage)

        def norm(*args, **kw):
            made = []
            with ExitStack() as scope:
                norm_phase(phase_sems(scope, made), tuple(spent), *args, **kw)
            spent[:] = made

        def norm_phase(sem, old, tag, which, xT_full, ar, early_loads=None, router=None, gates=None, final=False):
            gb = ar("ln_gb", [P, 2, D_MODEL])
            ln_in = sem(tag + "ln_in")
            res_done, st_done, ag_done = sem(tag + "res"), sem(tag + "stats"), sem(tag + "mean_var")
            eps_done, sq_done, rs_done = sem(tag + "eps"), sem(tag + "sqrt"), sem(tag + "rstd")
            cn_done, g_done, ln_done = sem(tag + "centered"), sem(tag + "gained"), sem(tag + "ln_done")
            tr_done, xf_done, xh_done, xl_done = sem(tag + "tr"), sem(tag + "xf"), sem(tag + "xh"), sem(tag + "xl")
            out_done = sem(tag + "out")
            if router is not None:
                wr = ar("wr", [P, KC, N_EXPERTS])
                eb = ar("eb", [P, N_EXPERTS])
                tri = ar("tri", [P, N_GROUPS, N_GROUPS])
                rt = {n: ar(n, [P, N_EXPERTS]) for n in
                      ("sc0", "sc1", "ch0", "ch1", "mk0", "mk1", "gt0", "gt1", "gts0", "gts1")}
                m8 = ar("m8", [P, TC, N_GROUPS, 8])
                gs = ar("gs", [P, TC, N_GROUPS])
                gtm = ar("gtm", [P, TC, N_GROUPS, N_GROUPS])
                eqm = ar("eqm", [P, TC, N_GROUPS, N_GROUPS])
                rank = ar("rank", [P, TC, N_GROUPS])
                pen = ar("pen", [P, TC, N_GROUPS])
                top8 = ar("top8", [P, TC, 8])
                gsum = ar("gsum", [P, TC])
                ginv = ar("ginv", [P, TC])
                gT = ar("gT", [N_EXPERTS, SEQ])
                r_in, lg_done, re_done, rc = sem(tag + "router_in"), sem(tag + "router"), sem(tag + "router_exp"), sem(tag + "route")
                gt_done, ge_done, gd_done = sem(tag + "gates_T"), sem(tag + "gates_ev"), sem(tag + "gates_dram")
                w_router, bias_row = router

            with nc.Block() as block:
                @block.sync
                def _(sp):
                    g_row, b_row = which
                    sp.dma_start(gb[:, 0, :], g_row.partition_broadcast(P)).then_inc(ln_in, 16)
                    sp.dma_start(gb[:, 1, :], b_row.partition_broadcast(P)).then_inc(ln_in, 16)
                    if router is not None:
                        sp.dma_start(wr[:, :, :], w_router).then_inc(r_in, 16)
                        sp.dma_start(eb[:, :], bias_row.partition_broadcast(P)).then_inc(r_in, 16)
                        sp.dma_start(tri[:, :, :], t["tri"]).then_inc(r_in, 16)
                    if early_loads:
                        early_loads(sp)
                    if router is not None:
                        sp.wait_ge(ge_done, 1)
                        sp.dma_start(gates, gT[:, :]).then_inc(gd_done, 16)
                        sp.wait_ge(gd_done, 16)
                    if final:
                        for a in range(TC):
                            sp.wait_ge(ln_done, a + 1)
                            sp.dma_start(out[0, a * P:(a + 1) * P, :], h[:, a, :]).then_inc(out_done, 16)
                        sp.wait_ge(out_done, 16 * TC)

                @block.gpsimd
                def _(pool):
                    clear_spent(pool, old)

                @block.vector
                def _(dve):
                    for a in range(TC):
                        for n in range(2):
                            dve.scalar_tensor_tensor(out=h[:, a, n * 512:n * 512 + 512], in0=h[:, a, n * 512:n * 512 + 512],
                                                     scalar=DN_ALPHA, in1=psum[:, 2 * a + n, :], op0=ALU.mult,
                                                     op1=ALU.add).then_inc(res_done, 1)
                    for a in range(TC):
                        for n in range(2):
                            dve.wait_ge(res_done, 2 * a + n + 1)
                            dve.bn_stats(stats[:, a, n, :], h[:, a, n * 512:n * 512 + 512]).then_inc(st_done, 1)
                    for a in range(TC):
                        dve.wait_ge(st_done, 2 * a + 2)
                        dve.bn_aggr(mv[:, a, :], stats[:, a, :, :]).then_inc(ag_done, 1)
                    dve.wait_ge(ag_done, TC)
                    dve.tensor_scalar(rstd[:, :], mv[:, :, 1], NORM_EPS, None, ALU.add).then_inc(eps_done, 1)
                    dve.wait_ge(sq_done, 1)
                    dve.reciprocal(rstd[:, :], rstd[:, :]).then_inc(rs_done, 1)
                    dve.wait_ge(rs_done, 1)
                    for a in range(TC):
                        dve.tensor_scalar(h[:, a, :], h[:, a, :], mv[:, a, 0:1], rstd[:, a:a + 1], ALU.subtract, ALU.mult)\
                           .then_inc(cn_done, 1)
                    dve.wait_ge(ln_in, 32)
                    for a in range(TC):
                        dve.wait_ge(cn_done, a + 1)
                        dve.tensor_tensor(h[:, a, :], h[:, a, :], gb[:, 0, :], ALU.mult).then_inc(g_done, 1)
                        dve.wait_ge(g_done, a + 1)
                        dve.tensor_tensor(h[:, a, :], h[:, a, :], gb[:, 1, :], ALU.add).then_inc(ln_done, 1)
                    if final:
                        return
                    for i in range(2 * TC):
                        a, q = divmod(i, 2)
                        dve.wait_ge(xh_done, i + 1)
                        dve.tensor_tensor(xTl[:, 4 * q:4 * q + 4, a * P:a * P + P], xT_full[:, 4 * q:4 * q + 4, a * P:a * P + P],
                                          xTh[:, 4 * q:4 * q + 4, a * P:a * P + P].bitcast(F32), ALU.subtract).then_inc(xl_done, 1)
                    if router is None:
                        return
                    count = [0]

                    def link(ins):
                        count[0] += 1
                        ins.then_inc(rc, 1)
                        dve.wait_ge(rc, count[0])

                    dve.wait_ge(r_in, 48)
                    for a in range(TC):
                        sc, ch, mk, gt = (rt[f"{n}{a}"] for n in ("sc", "ch", "mk", "gt"))
                        dve.wait_ge(re_done, a + 1)
                        link(dve.tensor_scalar(sc[:, :], sc[:, :], 1.0, None, ALU.add))
                        link(dve.reciprocal(sc[:, :], sc[:, :]))
                        link(dve.tensor_tensor(ch[:, :], sc[:, :], eb[:, :], ALU.add))
                        for g in range(N_GROUPS):
                            ins = dve.max(m8[:, a, g, :], ch[:, g * GROUP:(g + 1) * GROUP])
                            if g < N_GROUPS - 1:
                                count[0] += 1
                                ins.then_inc(rc, 1)
                        link(ins)
                        link(dve.tensor_tensor(gs[:, a, :], m8[:, a, :, 0], m8[:, a, :, 1], ALU.add))
                        mine = gs[:, a, :].unsqueeze(2).broadcast_to([P, N_GROUPS, N_GROUPS])
                        others = gs[:, a, :].unsqueeze(1).broadcast_to([P, N_GROUPS, N_GROUPS])
                        link(dve.tensor_tensor(gtm[:, a, :, :], others, mine, ALU.is_gt))
                        link(dve.tensor_tensor(eqm[:, a, :, :], others, mine, ALU.is_equal))
                        link(dve.tensor_tensor(eqm[:, a, :, :], eqm[:, a, :, :], tri[:, :, :], ALU.mult))
                        link(dve.tensor_tensor(gtm[:, a, :, :], gtm[:, a, :, :], eqm[:, a, :, :], ALU.add))
                        link(dve.tensor_reduce(rank[:, a, :], gtm[:, a, :, :], AX.X, ALU.add))
                        link(dve.tensor_scalar(rank[:, a, :], rank[:, a, :], float(TOPK_GROUPS), None, ALU.is_lt))
                        link(dve.tensor_scalar(pen[:, a, :], rank[:, a, :], -MASKED, MASKED, ALU.mult, ALU.add))
                        chv = ch[:, :].rearrange("p (g e) -> p g e", g=N_GROUPS)
                        link(dve.tensor_tensor(chv, chv, rank[:, a, :].unsqueeze(2).broadcast_to([P, N_GROUPS, GROUP]), ALU.mult))
                        link(dve.tensor_tensor(chv, chv, pen[:, a, :].unsqueeze(2).broadcast_to([P, N_GROUPS, GROUP]), ALU.add))
                        link(dve.max(top8[:, a, :], ch[:, :]))
                        link(dve.match_replace(mk[:, :], top8[:, a, :], ch[:, :], TAKEN))
                        link(dve.tensor_scalar(mk[:, :], mk[:, :], TAKEN, None, ALU.is_equal))
                        link(dve.tensor_tensor(gt[:, :], sc[:, :], mk[:, :], ALU.mult))
                        link(dve.tensor_reduce(gsum[:, a:a + 1], gt[:, :], AX.X, ALU.add))
                        link(dve.reciprocal(ginv[:, a:a + 1], gsum[:, a:a + 1]))
                        link(dve.tensor_scalar(rt[f"gts{a}"][:, :], gt[:, :], ginv[:, a:a + 1], ROUTED_SCALE, ALU.mult, ALU.mult))
                        dve.sem_inc(gt_done, 1)

                @block.scalar
                def _(act):
                    act.wait_ge(eps_done, 1)
                    act.activation(rstd[:, :], rstd[:, :], ACT.Sqrt).then_inc(sq_done, 1)
                    if final:
                        return
                    for i in range(2 * TC):
                        a, q = divmod(i, 2)
                        act.wait_ge(tr_done, i + 1)
                        v = psum[:, 4 + i, :].rearrange("p (k t) -> p k t", k=4)
                        act.activation(xT_full[:, 4 * q:4 * q + 4, a * P:a * P + P], v, ACT.Copy).then_inc(xf_done, 1)
                        act.activation(xTh[:, 4 * q:4 * q + 4, a * P:a * P + P], v, ACT.Copy).then_inc(xh_done, 1)
                    if router is None:
                        return
                    for a in range(TC):
                        act.wait_ge(lg_done, a + 1)
                        act.activation(rt[f"sc{a}"][:, :], psum[:, a, 0:N_EXPERTS], ACT.Exp, scale=-1.0).then_inc(re_done, 1)
                    act.wait_ge(gt_done, TC + 1)
                    act.activation(gT[:, :], psum[0:N_EXPERTS, 2, 0:SEQ], ACT.Copy).then_inc(ge_done, 1)

                @block.tensor
                def _(pe):
                    if final:
                        return
                    for i in range(2 * TC):
                        a, q = divmod(i, 2)
                        pe.wait_ge(ln_done, a + 1)
                        for k in range(4):
                            last = pe.transpose(psum[:, 4 + i, k * P:k * P + P], h[:, a, 4 * q + k::KC], ident[:, :])
                        last.then_inc(tr_done, 1)
                    if router is None:
                        return
                    pe.wait_ge(r_in, 48)
                    for a in range(TC):
                        pe.wait_ge(xf_done, 2 * a + 2)
                        for k in range(KC):
                            last = pe.matmul(psum[:, a, 0:N_EXPERTS], xT_full[:, k, a * P:a * P + P], wr[:, k, :],
                                             start=(k == 0), stop=(k == KC - 1))
                        last.then_inc(lg_done, 1)
                    for a in range(TC):
                        pe.wait_ge(gt_done, a + 1)
                        last = pe.transpose(psum[0:N_EXPERTS, 2, a * P:a * P + P], rt[f"gts{a}"][:, :], ident[:, :])
                    last.then_inc(gt_done, 1)

        def expert_loads(l, raw_in):
            def views(n):
                if isinstance(n, int) and n == 0:
                    w = (t["moe_ws_gate"][l], t["moe_ws_up"][l], t["moe_ws_down"][l])
                else:
                    w = tuple(t[x][l, n - 1] for x in ("moe_w_gate", "moe_w_up", "moe_w_down"))
                return [w[0].rearrange("(p k) f -> p (k f)", k=KC), w[1].rearrange("(p k) f -> p (k f)", k=KC),
                        w[2].rearrange("(p j) d -> p (j d)", j=2)]

            def load(eng, n, b, i):
                eng.dma_start(raw[:, 3 * b + i, :], views(n)[i]).then_inc(raw_in[3 * b + i], 16)
            return load

        def experts(*args):
            made = []
            with ExitStack() as scope:
                experts_phase(phase_sems(scope, made), tuple(spent), *args)
            spent[:] = made

        def experts_phase(sem, old, l, load, raw_in, gate_in, gates):
            tag = f"m{l}_"
            ar = Arena(tag)
            hi = ar("w_hi", [P, 6, UNIT], F32R)
            lo = ar("w_lo", [P, 6, UNIT], F32R)
            E = ar("sig", [P, 2, 512])
            S = ar("act", [P, 512])
            H = ar("hid", [P, 512])
            Hh = ar("hid_hi", [P, 2, 2, SEQ], F32R)
            Hl = ar("hid_lo", [P, 2, 2, SEQ], F32R)
            N = N_EXPERTS + 1
            hi_done = [sem(f"{tag}hi{i}") for i in range(3)]
            lo_done = [sem(f"{tag}lo{i}") for i in range(3)]
            mm_done = [sem(tag + "gate_done"), sem(tag + "up_done"), sem(tag + "down_done")]
            ex_done, one_done, sig_done = sem(tag + "exp"), sem(tag + "one"), sem(tag + "sigmoid")
            silu_done, act_done, hid_done = sem(tag + "silu"), sem(tag + "act"), sem(tag + "hidden")
            hh_done, hl_done = sem(tag + "hid_hi"), sem(tag + "hid_lo")

            def loop(eng, stage):
                stage(0, 0, 0)
                stage(1, 1, 0)
                with eng.Fori(0, N_EXPERTS // 2 - 1) as it:
                    stage(2 * it + 2, 0, it + 1)
                    stage(2 * it + 3, 1, it + 1)
                stage(N - 1, 0, (N - 1) // 2)

            with nc.Block() as block:
                @block.sync
                def _(sp):
                    def units(n, b):
                        for i in range(3):
                            sp.wait_ge(lo_done[i], n - 1)
                            load(sp, n, b, i)
                    with sp.Fori(0, N_EXPERTS // 2 - 1) as it:
                        units(2 * it + 2, 0)
                        units(2 * it + 3, 1)
                    units(N - 1, 0)

                @block.gpsimd
                def _(pool):
                    clear_spent(pool, old)

                    def row(n, b):
                        pool.dma_start(gate_rows[:, b, :], gates[n - 1, :].partition_broadcast(P)).then_inc(gate_in[b], 16)
                    row(1, 1)
                    row(2, 0)
                    with pool.Fori(0, N_EXPERTS // 2 - 1) as it:
                        pool.wait_ge(hid_done, 2 * it + 2)
                        row(2 * it + 3, 1)
                        pool.wait_ge(hid_done, 2 * it + 3)
                        row(2 * it + 4, 0)

                @block.scalar
                def _(act):
                    def upper(n, b, half, i):
                        act.wait_ge(raw_in[3 * b + i], 16 * half + 16)
                        wait(act, mm_done[i], n - 1)
                        act.activation(hi[:, 3 * b + i, :], raw[:, 3 * b + i, :], ACT.Copy).then_inc(hi_done[i], 1)

                    def stage(n, b, half):
                        more = not (isinstance(n, int) and n == N - 1)
                        nxt = (n + 1, 1 - b, half + b)
                        if more:
                            upper(*nxt, 0)
                            upper(*nxt, 1)
                        act.wait_ge(mm_done[0], n + 1)
                        wait(act, silu_done, n - 1)
                        act.activation(E[:, b, :], psum[:, 4 + 2 * b, :], ACT.Exp, scale=-1.0).then_inc(ex_done, 1)
                        if more:
                            upper(*nxt, 2)
                        act.wait_ge(hid_done, n + 1)
                        wait(act, mm_done[2], n - 1)
                        act.activation(Hh[:, b, :, :].rearrange("p j t -> p (j t)"), H[:, :], ACT.Copy).then_inc(hh_done, 1)

                    for i in range(3):
                        upper(0, 0, 0, i)
                    loop(act, stage)

                @block.vector
                def _(dve):
                    def lower(n, b, half, i):
                        dve.wait_ge(hi_done[i], n + 1)
                        wait(dve, mm_done[i], n - 1)
                        dve.tensor_tensor(lo[:, 3 * b + i, :], raw[:, 3 * b + i, :], hi[:, 3 * b + i, :].bitcast(F32),
                                          ALU.subtract).then_inc(lo_done[i], 1)

                    def stage(n, b, half):
                        more = not (isinstance(n, int) and n == N - 1)
                        nxt = (n + 1, 1 - b, half + b)
                        if more:
                            lower(*nxt, 0)
                            lower(*nxt, 1)
                        G, U = psum[:, 4 + 2 * b, :], psum[:, 5 + 2 * b, :]
                        dve.wait_ge(ex_done, n + 1)
                        dve.tensor_scalar(E[:, b, :], E[:, b, :], 1.0, None, ALU.add).then_inc(one_done, 1)
                        dve.wait_ge(one_done, n + 1)
                        dve.reciprocal(E[:, b, :], E[:, b, :]).then_inc(sig_done, 1)
                        dve.wait_ge(sig_done, n + 1)
                        wait(dve, hid_done, n)
                        dve.tensor_tensor(S[:, :], G, E[:, b, :], ALU.mult).then_inc(silu_done, 1)
                        dve.wait_ge(silu_done, n + 1)
                        dve.wait_ge(mm_done[1], n + 1)
                        dve.tensor_tensor(S[:, :], S[:, :], U, ALU.mult).then_inc(act_done, 1)
                        dve.wait_ge(act_done, n + 1)
                        wait(dve, hl_done, n)
                        if isinstance(n, int) and n == 0:
                            dve.tensor_copy(H[:, :], S[:, :]).then_inc(hid_done, 1)
                        else:
                            dve.wait_ge(gate_in[b], 16 * half + 16 * b)
                            dve.tensor_tensor(H[:, :].rearrange("p (j t) -> p j t", j=2), S[:, :].rearrange("p (j t) -> p j t", j=2),
                                              gate_rows[:, b, :].unsqueeze(1).broadcast_to([P, 2, SEQ]), ALU.mult)\
                               .then_inc(hid_done, 1)
                        if more:
                            lower(*nxt, 2)
                        dve.wait_ge(hh_done, n + 1)
                        wait(dve, mm_done[2], n - 1)
                        dve.tensor_tensor(Hl[:, b, :, :].rearrange("p j t -> p (j t)"), H[:, :],
                                          Hh[:, b, :, :].rearrange("p j t -> p (j t)").bitcast(F32), ALU.subtract).then_inc(hl_done, 1)

                    for i in range(3):
                        lower(0, 0, 0, i)
                    loop(dve, stage)

                @block.tensor
                def _(pe):
                    def gate_up(n, b):
                        wait(pe, act_done, n - 1)
                        for i in range(2):
                            pe.wait_ge(hi_done[i], n + 1)
                            pe.wait_ge(lo_done[i], n + 1)
                            for j in range(2):
                                for step, (w, x) in enumerate(((hi, xTh), (hi, xTl), (lo, xTh))):
                                    for k in range(KC):
                                        wk = w[:, 3 * b + i, k * D_EXPERT + j:(k + 1) * D_EXPERT:2]
                                        last = pe.matmul(psum[:, 4 + 2 * b + i, j * SEQ:(j + 1) * SEQ], wk, x[:, k, :],
                                                         start=(step == 0 and k == 0), stop=(step == 2 and k == KC - 1))
                            last.then_inc(mm_done[i], 1)

                    def down(n, b):
                        first = isinstance(n, int) and n == 0
                        final = isinstance(n, int) and n == N - 1
                        pe.wait_ge(hi_done[2], n + 1)
                        pe.wait_ge(lo_done[2], n + 1)
                        pe.wait_ge(hh_done, n + 1)
                        pe.wait_ge(hl_done, n + 1)
                        for step, (x, w) in enumerate(((Hh, hi), (Hh, lo), (Hl, hi))):
                            for j in range(2):
                                for a in range(TC):
                                    for m in range(2):
                                        last = pe.matmul(psum[:, 2 * a + m, :], x[:, b, j, a * P:a * P + P],
                                                         w[:, 3 * b + 2, j * D_MODEL + m * 512:j * D_MODEL + m * 512 + 512],
                                                         start=(first and step == 0 and j == 0),
                                                         stop=(final and step == 2 and j == 1), skip_group_check=True)
                        last.then_inc(mm_done[2], 1)

                    def stage(n, b, half):
                        if not (isinstance(n, int) and n == N - 1):
                            gate_up(n + 1, 1 - b)
                        down(n, b)

                    gate_up(0, 0)
                    loop(pe, stage)

        scale_a = A_HD ** -0.5
        ar = Arena("a")
        xT = ar("xT", [P, KC, SEQ])
        kT = ar("kT", [P, SEQ])
        v_a = ar("v", [P, TC, A_HD])
        sel = ar("sel", [P, LINE])
        bias_in_a = ar("bias", [P, 2, 2, LINE])
        bias_sel = ar("bias_sel", [P, 2, 2, LINE])
        q_a = ar("q", [P, 2, 2, SEQ])
        mark = ar.at - arena_at
        qiT = ar("qiT", [P, IDX_HEADS // 2, SEQ])
        kiT = ar("kiT", [P, SEQ])
        wi = ar("wi", [P, TC, IDX_HEADS])
        rel = ar("rel", [P, 2, SEQ])
        score = ar("score", [P, TC, SEQ])
        best = ar("best", [P, TC, 8])
        causal = ar("causal", [P, P])
        lines = ar("lines", [REL_HEADS, 1 + len(B_GROUPS), LINE])
        rel_tab = ar("rel_tab", [REL_BUCKETS + 1, REL_HEADS])
        hot = ar("hot", [REL_BUCKETS + 1, 1 + len(B_GROUPS), LINE])

        x_in, h_in, c_in, rel_in, neg_done = sem("x_in"), sem("h_in"), sem("const_in"), sem("rel_in"), sem("masked_row")
        wa_in = [sem(f"wa_in{i}") for i in range(4)]
        q_in = [sem(f"qa_in{i}") for i in range(2)]
        bias_in = [sem(f"bias_a_in{i}") for i in range(2)]
        line_mm, line_ev, line_dram = sem("line_mm"), sem("line_ev"), sem("line_dram")
        pre_mm, pre_ev, s_mm, s_relu, s_acc, tk, sel_done = (sem("pre_mm"), sem("pre_ev"), sem("score_mm"), sem("score_relu"),
                                                             sem("score_acc"), sem("topk_step"), sem("sel_done"))
        wa = t["a_w_in_parts"]

        def load_q(eng, j, b):
            eng.dma_start(raw[:, 4 + b, :], t["a_w_q"][j]).then_inc(q_in[b], 16)

        with nc.Block() as block:
            @block.sync
            def _(sp):
                sp.dma_start(rel_tab[0:REL_BUCKETS, :], t["rel_bias"]).then_inc(rel_in, 16)
                sp.dma_start(hot[:, :, :], t["hot"]).then_inc(rel_in, 16)
                sp.dma_start(xT[:, :, :], t["x_T"]).then_inc(x_in, 16)
                sp.dma_start(raw[:, 0, 0:KC * 136], t["a_w_ki"]).then_inc(wa_in[0], 16)
                for i in range(2):
                    sp.dma_start(raw[:, 1 + i, :], wa[i]).then_inc(wa_in[1 + i], 16)
                sp.dma_start(causal[:, :], t["causal"]).then_inc(c_in, 16)
                sp.dma_start(raw[:, 3, :], wa[2]).then_inc(wa_in[3], 16)
                sp.dma_start(ident[:, :], t["ident"]).then_inc(c_in, 16)
                load_q(sp, 0, 0)
                load_q(sp, 1, 1)
                sp.dma_start(h[:, :, :], t["x"][0].rearrange("(a p) d -> p a d", p=P)).then_inc(h_in, 16)
                sp.wait_ge(line_ev, 4)
                sp.dma_start(lines_d.rearrange("g h m -> h g m"), lines[:, :, :]).then_inc(line_dram, 16)
                sp.wait_ge(line_dram, 16)
                sp.wait_ge(h_in, 16)
                sp.wait_ge(c_in, 32)

            @block.gpsimd
            def _(pool):
                pool.memset(rel_tab[REL_BUCKETS:REL_BUCKETS + 1, :], MASKED).then_inc(neg_done, 1)

            @block.tensor
            def _(pe):
                pe.wait_ge(rel_in, 32)
                pe.wait_ge(neg_done, 1)
                for g in range(1 + len(B_GROUPS)):
                    pe.matmul(psum[0:REL_HEADS, 2 + g, 0:LINE], rel_tab[:, :], hot[:, g, :], start=True, stop=True)\
                      .then_inc(line_mm, 1)
                pe.wait_ge(x_in, 16)
                pe.wait_ge(wa_in[0], 16)
                wk = raw[:, 0, 0:KC * 136].rearrange("p (k c) -> p k c", k=KC)
                for k in range(KC):
                    last = pe.matmul(psum[:, 0, 0:SEQ], wk[:, k, 0:P], xT[:, k, :], start=(k == 0), stop=(k == KC - 1))
                last.then_inc(pre_mm, 1)
                for a in range(TC):
                    for k in range(KC):
                        last = pe.matmul(psum[:, 1, a * IDX_HEADS:(a + 1) * IDX_HEADS], xT[:, k, a * P:a * P + P],
                                         wk[:, k, P:P + IDX_HEADS], start=(k == 0), stop=(k == KC - 1))
                last.then_inc(pre_mm, 1)
                for c in range(4):
                    if c % 2 == 0:
                        pe.wait_ge(wa_in[1 + c // 2], 16)
                    wv = raw[:, 1 + c // 2, :].rearrange("p (k c) -> p k c", k=KC)
                    pe.wait_ge(line_ev, c + 1)
                    for k in range(KC):
                        last = pe.matmul(psum[:, 2 + c, 0:SEQ], wv[:, k, (c % 2) * P:(c % 2) * P + P], xT[:, k, :],
                                         start=(k == 0), stop=(k == KC - 1))
                    last.then_inc(pre_mm, 1)
                pe.wait_ge(pre_ev, 6)
                for n in range(TC * IDX_HEADS):
                    a, hd = TC - 1 - n // IDX_HEADS, n % IDX_HEADS
                    wait(pe, s_relu, n - 1)
                    r0 = IDX_HD * (hd % 2)
                    pe.matmul(psum[:, n % 2, 0:P * (a + 1)], qiT[r0:r0 + IDX_HD, hd // 2, a * P:a * P + P],
                              kiT[r0:r0 + IDX_HD, 0:P * (a + 1)], start=True, stop=True).then_inc(s_mm, 1)
                    if n == IDX_HEADS - 1:
                        pe.wait_ge(wa_in[3], 16)
                        wv = raw[:, 3, :].rearrange("p (k c) -> p k c", k=KC)
                        for k in range(KC):
                            last = pe.matmul(psum[:, 6, 0:SEQ], wv[:, k, 0:A_HD], xT[:, k, :], start=(k == 0), stop=(k == KC - 1))
                        last.then_inc(pre_mm, 1)
                        for aa in range(TC):
                            for k in range(KC):
                                last = pe.matmul(psum[:, 7, aa * A_HD:(aa + 1) * A_HD], xT[:, k, aa * P:aa * P + P],
                                                 wv[:, k, A_HD:2 * A_HD], start=(k == 0), stop=(k == KC - 1))
                        last.then_inc(pre_mm, 1)

            @block.scalar
            def _(act):
                for g in range(1 + len(B_GROUPS)):
                    act.wait_ge(line_mm, g + 1)
                    act.activation(lines[:, g, :], psum[0:REL_HEADS, 2 + g, 0:LINE], ACT.Copy).then_inc(line_ev, 1)
                act.wait_ge(pre_mm, 1)
                act.activation(kiT[:, :], psum[:, 0, 0:SEQ], ACT.Copy).then_inc(pre_ev, 1)
                act.wait_ge(pre_mm, 2)
                act.activation(wi[:, :, :], psum[:, 1, 0:TC * IDX_HEADS].rearrange("p (a h) -> p a h", a=TC), ACT.Copy,
                               scale=IDX_HEADS ** -0.5).then_inc(pre_ev, 1)
                for c in range(4):
                    act.wait_ge(pre_mm, 3 + c)
                    act.activation(qiT[:, c, :], psum[:, 2 + c, 0:SEQ], ACT.Copy).then_inc(pre_ev, 1)
                for n in range(TC * IDX_HEADS):
                    a = TC - 1 - n // IDX_HEADS
                    act.wait_ge(s_mm, n + 1)
                    wait(act, s_acc, n - 1)
                    act.activation(rel[:, n % 2, 0:P * (a + 1)], psum[:, n % 2, 0:P * (a + 1)], ACT.Relu,
                                   scale=IDX_HD ** -0.5).then_inc(s_relu, 1)
                act.wait_ge(pre_mm, 7)
                act.activation(kT[:, :], psum[:, 6, 0:SEQ], ACT.Copy).then_inc(pre_ev, 1)
                act.wait_ge(pre_mm, 8)
                act.activation(v_a[:, :, :], psum[:, 7, 0:TC * A_HD].rearrange("p (a e) -> p a e", a=TC), ACT.Copy).then_inc(pre_ev, 1)

            @block.vector
            def _(dve):
                steps = [0]

                def link(ins):
                    steps[0] += 1
                    ins.then_inc(tk, 1)
                    dve.wait_ge(tk, steps[0])

                dve.wait_ge(pre_ev, 2)
                dve.wait_ge(c_in, 32)
                for ai in range(TC):
                    a = TC - 1 - ai
                    n_keys = P * (a + 1)
                    sc = score[:, a, 0:n_keys]
                    for hd in range(IDX_HEADS):
                        n = ai * IDX_HEADS + hd
                        dve.wait_ge(s_relu, n + 1)
                        if hd == 0:
                            dve.tensor_scalar(sc, rel[:, n % 2, 0:n_keys], wi[:, a, hd:hd + 1], None, ALU.mult).then_inc(s_acc, 1)
                        else:
                            dve.wait_ge(s_acc, n)
                            dve.scalar_tensor_tensor(out=sc, in0=rel[:, n % 2, 0:n_keys], scalar=wi[:, a, hd:hd + 1], in1=sc,
                                                     op0=ALU.mult, op1=ALU.add).then_inc(s_acc, 1)
                    dve.wait_ge(s_acc, (ai + 1) * IDX_HEADS)
                    dg = score[:, a, a * P:a * P + P]
                    link(dve.tensor_tensor(dg, dg, causal[:, :], ALU.add))
                    for rnd in range(TOPK_KEYS // 8):
                        link(dve.max(best[:, a, :], sc))
                        link(dve.match_replace(sc, best[:, a, :], sc, TAKEN))
                    dst = sel[:, a * P:a * P + n_keys]
                    link(dve.tensor_scalar(sc, sc, TAKEN, -MASKED, ALU.is_equal, ALU.mult))
                    link(dve.tensor_scalar(dst, sc, MASKED, None, ALU.add))

        wo_a = t["a_w_o"][0].rearrange("(u c p) n -> u p c n", c=2, p=P)
        sel_used = sem("bias_sel_ready")

        def a_first(sp, pr_done):
            for j in range(2):
                sp.dma_start(bias_in_a[:, j, :, SEQ:LINE], bias_tile(0, 1, j, P)[:, 0]).then_inc(bias_in[j], 16)
                sp.dma_start(bias_in_a[:, j, :, 0:SEQ], bias_tile(0, 1, j, SEQ)[:, 0]).then_inc(bias_in[j], 16)

        def a_loop(sp, pr_done, stt_done):
            with sp.Fori(0, STEPS // 2 - 1) as it:
                for b in range(2):
                    j = 2 * it + 2 + b
                    sp.wait_ge(pr_done, 2 * j - 2)
                    load_q(sp, j, b)
                    sp.wait_ge(sel_used, 2 * j - 2)
                    sp.dma_start(bias_in_a[:, b, :, SEQ:LINE], bias_tile(0, 1, j, P)[:, 0]).then_inc(bias_in[b], 16)
                    sp.dma_start(bias_in_a[:, b, :, 0:SEQ], bias_tile(0, 1, j, SEQ)[:, 0]).then_inc(bias_in[b], 16)

        def a_pool(pool, stt_done):
            def combine(j, b, half, first):
                pool.wait_ge(bias_in[b], 32 * half + 32)
                if not first:
                    pool.wait_ge(stt_done, 2 * j - 2)
                for c in range(2):
                    pool.tensor_tensor(bias_sel[:, b, c, :], bias_in_a[:, b, c, ::-1], sel[:, :], ALU.add).then_inc(sel_used, 1)
            combine(0, 0, 0, True)
            combine(1, 1, 0, True)
            with pool.Fori(0, STEPS // 2 - 1) as it:
                combine(2 * it + 2, 0, it + 1, False)
                combine(2 * it + 3, 1, it + 1, False)

        def a_project(pe, j, b, half, i):
            if i == 0:
                pe.wait_ge(q_in[b], 16 * half + 16)
            wq = raw[:, 4 + b, :].rearrange("p (k c) -> p k c", k=KC)
            for k in range(KC):
                last = pe.matmul(psum[:, i % 2, 0:SEQ], wq[:, k, i * P:i * P + P], xT[:, k, :], start=(k == 0), stop=(k == KC - 1))
            return last

        raw_in = [[sem(f"raw{l}_in{i}") for i in range(6)] for l in range(DEPTH)]
        gate_in = [[sem(f"gate{l}_in{i}") for i in range(2)] for l in range(DEPTH)]
        load_e = [expert_loads(l, raw_in[l]) for l in range(DEPTH)]

        def prefetch(l):
            def f(sp):
                for n in range(2):
                    for i in range(3):
                        load_e[l](sp, n, n, i)
            return f

        attention(
            "a_", 1, scale_a, xT, 2, a_project, a_first, a_loop, prefetch(0),
            bias_ready=lambda dve, j, b, half: dve.wait_ge(sel_used, 2 * j + 2),
            bias_of=lambda b, c: bias_sel[:, b, c, :],
            q_of=lambda b, c, g, a: q_a[:, b, c, a * P:a * P + P],
            k_of=lambda b, c, g, a: kT[:, 0:P * (a + 1)],
            v_of=lambda b, c, g, s: v_a[:, s, :],
            evac_piece=lambda act, b, i: act.activation(q_a[:, b, i, :], psum[:, i % 2, 0:SEQ], ACT.Copy),
            o_step=lambda OT, c: OT[:, c * SEQ:(c + 1) * SEQ],
            o_chunks=A_HEADS, wo_view=lambda u: wo_a[u], wo_units=A_HEADS // 2,
            ar=Arena("a2", mark), extra_pool=a_pool)

        def router_of(l):
            return (t["moe_w_router"][l].rearrange("(p k) e -> p k e", k=KC), t["moe_bias"][l])

        def ln_rows(l, i):
            return (t["ln_g"][l, i], t["ln_b"][l, i])

        def norm_arena(tag):
            a = Arena(tag)
            return a("xT", [P, KC, SEQ]), a

        xF, ar = norm_arena("n0")
        norm("n0_", ln_rows(0, 0), xF, ar, router=router_of(0), gates=gates_d[0])
        experts(0, load_e[0], raw_in[0], gate_in[0], gates_d[0])

        G = len(B_GROUPS)
        WB = KC * G * P
        rawB = raw[:, :, :].rearrange("p u n -> p (u n)")[:, 0:3 * WB].rearrange("p (s k g c) -> p s k g c", s=3, k=KC, g=G)
        wb_in = [sem(f"wb_in{i}") for i in range(3)]
        bias_b_in = [sem(f"bias_b_in{i}") for i in range(2)]

        def load_b(eng, j, i):
            eng.dma_start(rawB[:, i, :, :, :].rearrange("p k g c -> p (k g c)"), t["b_w_in_parts"][j, i]).then_inc(wb_in[i], 16)

        def first_b(sp):
            for i in range(3):
                load_b(sp, 0, i)

        xF, ar = norm_arena("n1")
        norm("n1_", ln_rows(0, 1), xF, ar, early_loads=first_b)

        xTb = xF
        ar = Arena("b", start=4 * KC * SEQ)
        qk = ar("qk", [P, 2, 2, G, SEQ])
        vb = ar("v", [P, 2, TC, G * P])
        bias_b = ar("bias", [P, 2, 2, G, LINE])

        def load_bias(sp, j, b):
            for c in range(2):
                for lo_, n_ in ((0, SEQ), (SEQ, P)):
                    src = bias_tile(1, G, j, n_)[:, :, c]
                    sp.dma_start(bias_b[:, b, c, :, lo_:lo_ + n_], src).then_inc(bias_b_in[b], 16)

        def b_first(sp, pr_done):
            for j in range(2):
                load_bias(sp, j, j)

        def b_loop(sp, pr_done, stt_done):
            def weights(j):
                for i in range(3):
                    sp.wait_ge(pr_done, 8 * j - 8 + (3, 6, 8)[i])
                    load_b(sp, j, i)
            weights(1)
            with sp.Fori(0, STEPS // 2 - 1) as it:
                for b in range(2):
                    j = 2 * it + 2 + b
                    weights(j)
                    sp.wait_ge(stt_done, 2 * j - 2)
                    load_bias(sp, j, b)

        def b_project(pe, j, b, half, i):
            if i in (0, 3, 6):
                pe.wait_ge(wb_in[i // 3], 16 * j + 16)
            for k in range(KC):
                if i < 6:
                    last = pe.matmul(psum[:, i % 2, 0:SEQ], rawB[:, i // 3, k, i % 3, :], xTb[:, k, :], start=(k == 0), stop=(k == KC - 1))
                else:
                    last = pe.matmul(psum[:, i % 2, 0:G * P], xTb[:, k, (i - 6) * P:(i - 5) * P],
                                     rawB[:, 2, k, :, :], start=(k == 0), stop=(k == KC - 1))
            return last

        def b_evac(act, b, i):
            if i < 6:
                return act.activation(qk[:, b, i // 3, i % 3, :], psum[:, i % 2, 0:SEQ], ACT.Copy)
            return act.activation(vb[:, b, i - 6, :], psum[:, i % 2, 0:G * P], ACT.Copy)

        wo_b = t["b_w_o"][0].rearrange("(u c p) n -> u p c n", c=2, p=P)
        attention(
            "b_", G, B_HD ** -0.5, xTb, 8, b_project, b_first, b_loop, prefetch(1),
            bias_ready=lambda dve, j, b, half: dve.wait_ge(bias_b_in[b], 64 * half + 64),
            bias_of=lambda b, c: bias_b[:, b, c, :, ::-1],
            q_of=lambda b, c, g, a: qk[c * B_HD:(c + 1) * B_HD, b, 0, g, a * P:a * P + P],
            k_of=lambda b, c, g, a: qk[c * B_HD:(c + 1) * B_HD, b, 1, g, 0:P * (a + 1)],
            v_of=lambda b, c, g, s: vb[:, b, s, g * P + c * B_HD:g * P + (c + 1) * B_HD],
            evac_piece=b_evac,
            o_step=lambda OT, c: OT[c * B_HD:(c + 1) * B_HD, 0:SEQ],
            o_chunks=B_HEADS // 2, wo_view=lambda u: wo_b[u], wo_units=B_HEADS // 4, ar=ar)

        xF, ar = norm_arena("n2")
        norm("n2_", ln_rows(1, 0), xF, ar, router=router_of(1), gates=gates_d[1])
        experts(1, load_e[1], raw_in[1], gate_in[1], gates_d[1])
        xF, ar = norm_arena("n3")
        norm("n3_", ln_rows(1, 1), xF, ar, final=True)


def t5_bucket(dist):
    exact = REL_BUCKETS // 2
    if dist < exact:
        return dist
    large = exact + int(math.log(dist / exact) / math.log(REL_MAX_DIST / exact) * (REL_BUCKETS - exact))
    return min(large, REL_BUCKETS - 1)


def bucket_table():
    hot = np.zeros((REL_BUCKETS + 1, 1 + len(B_GROUPS), LINE), np.float32)
    for g, (window, dil) in enumerate(((SEQ, 1),) + B_GROUPS):
        for m in range(LINE):
            dist = m - (P - 1)
            reach = SEQ if g == 0 else window // dil
            ok = dist >= 0 and dist % dil == 0 and dist // dil <= reach
            hot[t5_bucket(dist) if ok else REL_BUCKETS, g, m] = 1.0
    return hot


def kernel(**inputs):
    import concourse.bacc as bacc
    from concourse.bass_utils import run_bass_kernel_spmd

    a = {n: np.ascontiguousarray(inputs[n]) for n in
         ("x", "rel_bias", "a_w_o", "b_w_o", "ln_g", "ln_b", "moe_w_router", "moe_bias", "moe_w_gate", "moe_w_up",
          "moe_w_down", "moe_ws_gate", "moe_ws_up", "moe_ws_down")}

    def chunked(w):
        return np.ascontiguousarray(w.reshape(P, KC * w.shape[1]))

    a["x_T"] = np.ascontiguousarray(np.asarray(inputs["x"])[0].T.reshape(P, KC, SEQ))
    w = np.asarray(inputs["a_w_in"])[0]
    nq, nk = A_HEADS * A_HD, A_HEADS * A_HD + 2 * A_HD
    a["a_w_q"] = np.stack([chunked(w[:, j * 256:(j + 1) * 256]) for j in range(STEPS)])
    ni = IDX_HEADS * IDX_HD
    a["a_w_in_parts"] = np.stack([chunked(w[:, nk:nk + 256]), chunked(w[:, nk + 256:nk + 512]), chunked(w[:, nq:nk])])
    ki = w[:, nk + ni:nk + ni + IDX_HD]
    a["a_w_ki"] = chunked(np.concatenate([ki, ki, w[:, nk + ni + IDX_HD:]], axis=1))
    wb = np.asarray(inputs["b_w_in"])[0].reshape(P, KC, len(B_GROUPS), 3, STEPS, P)
    a["b_w_in_parts"] = np.ascontiguousarray(wb.transpose(4, 3, 0, 1, 2, 5)).reshape(STEPS, 3, P, -1)
    a["hot"] = bucket_table()
    a["ident"] = np.eye(P, dtype=np.float32)
    a["causal"] = np.where(np.arange(P)[None, :] <= np.arange(P)[:, None], 0.0, MASKED).astype(np.float32)
    earlier = (np.arange(N_GROUPS)[None, :] < np.arange(N_GROUPS)[:, None]).astype(np.float32)
    a["tri"] = np.ascontiguousarray(np.broadcast_to(earlier, (P, N_GROUPS, N_GROUPS)))

    nc = bacc.Bacc("TRN2", target_bir_lowering=False, num_devices=1)
    t = {n: nc.dram_tensor(f"in_{n}", v.shape, mybir.dt.from_np(v.dtype), kind="ExternalInput").ap() for n, v in a.items()}
    out = nc.dram_tensor("out", (1, SEQ, D_MODEL), F32, kind="ExternalOutput").ap()
    build(nc, t, out)
    r = run_bass_kernel_spmd(nc, [{f"in_{n}": v for n, v in a.items()}], core_ids=[0])
    return r.results[0]["out"]
```

```python
import math
from contextlib import ExitStack

import numpy as np

import concourse.bass as bass
from concourse import mybir

F32 = mybir.dt.float32
F32R = mybir.dt.float32r
ALU = mybir.AluOpType
ACT = mybir.ActivationFunctionType
AX = mybir.AxisListType

D_MODEL, SEQ, DEPTH = 1024, 256, 2
P = 128
KC = D_MODEL // P
TC = SEQ // P
REL_BUCKETS, REL_MAX_DIST, REL_HEADS = 32, 2048, 16
A_HEADS, A_HD, IDX_HEADS, IDX_HD = 16, 128, 8, 64
TOPK_KEYS = min(256, SEQ // 4)
B_GROUPS = ((128, 1), (512, 4), (2048, 16))
B_HEADS, B_HD = 16, 64
N_EXPERTS, TOP_K, N_GROUPS, TOPK_GROUPS, D_EXPERT = 64, 8, 8, 4, 256
SLOTS = 64
GROUP = N_EXPERTS // N_GROUPS
ROUTED_SCALE = 2.5
NORM_EPS = 1e-5
DN_ALPHA = (2 * DEPTH) ** 0.25
MASKED = -1e30
TAKEN = -3e38
LINE = 3 * P
STEPS = A_HEADS // 2
UNIT = KC * D_EXPERT


def wait(eng, sem, value):
    if isinstance(value, int) and value <= 0:
        return
    eng.wait_ge(sem, value)


def build(nc, t, out):
    with ExitStack() as ctx:
        def sem(name):
            return ctx.enter_context(nc.semaphore(name))

        spent = []

        def phase_sems(scope, made):
            before = {s.num for s in spent}

            def f(name):
                s = scope.enter_context(nc.semaphore(name))
                assert s.num not in before
                made.append(s)
                return s
            return f

        def clear_spent(pool, old):
            for s in old:
                pool.sem_clear(s)

        def sb(name, shape, dt=F32):
            return ctx.enter_context(nc.sbuf_tensor(name, shape, dt))

        ident = sb("ident", [P, P])
        h = sb("h", [P, TC, D_MODEL])
        xT_at = nc.sbuf_base
        xTh = sb("xTh", [P, KC, SEQ], F32R)
        xTl = sb("xTl", [P, KC, SEQ], F32R)
        xh = sb("xh", [P, TC, D_MODEL], F32R)
        xl = sb("xl", [P, TC, D_MODEL], F32R)
        gate_of = sb("gate_of", [P, TC, N_EXPERTS])
        slot_of = sb("slot_of", [P, TC, N_EXPERTS])
        slot_no = sb("slot_no", [P, SLOTS])
        most_tokens = sb("most_tokens", [1, 1], mybir.dt.int32)
        raw = sb("raw", [P, 6, UNIT])
        arena_at = nc.sbuf_base
        top = nc.sbuf_usable_end

        class Arena:
            def __init__(self, tag, start=0):
                self.tag, self.at = tag, arena_at + start

            def __call__(self, name, shape, dt=F32):
                size = 4 * int(np.prod(shape[1:]))
                x = nc.alloc_sbuf_tensor_at(f"{self.tag}_{name}", shape, dt, offset=self.at)
                self.at += (size + 31) // 32 * 32
                assert self.at <= top, (self.tag, name, self.at, top)
                return x

        psum = ctx.enter_context(nc.psum_tensor("psum", [P, 8, 512], F32))

        lines_d = nc.dram_tensor("bias_lines", [1 + len(B_GROUPS), REL_HEADS, LINE], F32, kind="Internal").ap()
        gates_d = [nc.dram_tensor(f"gates{l}", [N_EXPERTS, SEQ], F32, kind="Internal").ap() for l in range(DEPTH)]

        def bias_tile(table, nt, j, n):
            base = lines_d[table:table + nt, bass.ds(2 * j, 2) if not isinstance(j, int) else slice(2 * j, 2 * j + 2), :]
            return bass.AP(base.tensor, base.offset,
                           [[1, P], [REL_HEADS * LINE, nt], [LINE, 2], [1, n]])

        def attention(*args, **kw):
            made = []
            with ExitStack() as scope:
                attention_phase(phase_sems(scope, made), tuple(spent), *args, **kw)
            spent[:] = made

        def attention_phase(sem, old, tag, G, scale, xT, pieces, project, load_first, load_loop, load_after, bias_ready, bias_of,
                      q_of, k_of, v_of, evac_piece, o_step, o_chunks, wo_view, wo_units, ar, extra_pool=None):
            PP = pieces
            S = ar("scores", [P, 2, G, LINE])
            pT = ar("pT", [P, 3, LINE])
            smax = ar("smax", [P, 2, TC])
            nmax = ar("nmax", [P, 2, TC])
            ssum = ar("ssum", [P, 2, TC])
            sinv = ar("sinv", [P, 2, TC])
            oT = ar("oT", [P, o_chunks, SEQ])
            wo = ar("wo", [P, 4, 2, D_MODEL])
            prob = ar("prob", [P, 2, G, LINE])

            pr_done, pr_free = sem(tag + "proj_done"), sem(tag + "proj_free")
            qk_done, stt_done = sem(tag + "qk_done"), sem(tag + "logits_done")
            red_done, max_done = sem(tag + "red_done"), sem(tag + "max_done")
            ex_done, rc_done, nrm = sem(tag + "exp_done"), sem(tag + "recip_done"), sem(tag + "norm_done")
            tr_done, pt_ev, pv_done = sem(tag + "tr_done"), sem(tag + "pT_ready"), sem(tag + "pv_done")
            ot_ev, y_done = sem(tag + "oT_ready"), sem(tag + "y_done")
            wo_in = [sem(f"{tag}wo_in{i}") for i in range(4)]
            wo_used = sem(tag + "wo_used")
            SL, ST, OT = psum[:, 2:5, :], psum[:, 5:7, :], psum[:, 7, :]

            def loop(eng, stage):
                stage(0, 0, 0)
                with eng.Fori(0, STEPS // 2 - 1) as it:
                    stage(2 * it + 1, 1, it)
                    stage(2 * it + 2, 0, it + 1)
                stage(STEPS - 1, 1, STEPS // 2 - 1)

            with nc.Block() as block:
                @block.sync
                def _(sp):
                    load_first(sp, pr_done)
                    for u in range(4):
                        sp.dma_start(wo[:, u, :, :], wo_view(u)).then_inc(wo_in[u], 16)
                    load_loop(sp, pr_done, stt_done)
                    sp.wait_ge(pr_done, PP * STEPS)
                    load_after(sp)
                    for u in range(4, wo_units):
                        sp.wait_ge(wo_used, u - 3)
                        sp.dma_start(wo[:, u % 4, :, :], wo_view(u)).then_inc(wo_in[u % 4], 16)

                @block.gpsimd
                def _(pool):
                    clear_spent(pool, old)
                    if extra_pool:
                        extra_pool(pool, stt_done)

                @block.tensor
                def _(pe):
                    def piece(j, b, half, i):
                        wait(pe, pr_free, PP * j + i - 1)
                        project(pe, j, b, half, i).then_inc(pr_done, 1)

                    def stage(j, b, half):
                        for c in range(2):
                            r = 2 * j + c
                            pe.wait_ge(pr_free, PP * j + PP)
                            wait(pe, stt_done, r)
                            for g in range(G):
                                bank = psum[:, 2 + (c if G == 1 else g), :]
                                for a in range(TC):
                                    last = pe.matmul(bank[:, a * P:a * P + P * (a + 1)], q_of(b, c, g, a), k_of(b, c, g, a),
                                                     start=True, stop=True)
                            last.then_inc(qk_done, 1)
                            if not (isinstance(j, int) and j == STEPS - 1):
                                for i in range(c * PP // 2, (c + 1) * PP // 2):
                                    nb, nhalf = 1 - b, (half if b == 0 else half + 1)
                                    piece(j + 1, nb, nhalf, i)
                            pe.wait_ge(nrm, 2 * r + 2)

                            def trans(g):
                                w = G * r + g
                                wait(pe, pt_ev, w - 1)
                                for s in range(3):
                                    last = pe.transpose(ST[:, (c * G + g) % 2, s * P:s * P + P], prob[:, c, g, s * P:s * P + P],
                                                        ident[:, :])
                                last.then_inc(tr_done, 1)

                            def pv(g):
                                w = G * r + g
                                pe.wait_ge(pt_ev, w + 1)
                                if c == 0 and g == 0:
                                    wait(pe, ot_ev, j)
                                o = o_step(OT, c)
                                slot = g if G > 1 else c
                                pe.matmul(o[:, 0:SEQ], v_of(b, c, g, 0), pT[:, slot, 0:2 * P], start=(g == 0), stop=False)
                                pe.matmul(o[:, P:SEQ], v_of(b, c, g, 1), pT[:, slot, 2 * P:3 * P], start=False,
                                          stop=(g == G - 1)).then_inc(pv_done, 1)

                            trans(0)
                            for g in range(1, G):
                                trans(g)
                                pv(g - 1)
                            pv(G - 1)

                    for i in range(PP):
                        piece(0, 0, 0, i)
                    loop(pe, stage)
                    pe.wait_ge(ot_ev, STEPS)
                    for u in range(wo_units):
                        pe.wait_ge(wo_in[u % 4], 16 * (u // 4 + 1))
                        for cc in range(2):
                            for a in range(TC):
                                for n in range(2):
                                    last = pe.matmul(psum[:, 2 * a + n, :], oT[:, 2 * u + cc, a * P:a * P + P],
                                                     wo[:, u % 4, cc, n * 512:n * 512 + 512],
                                                     start=(u == 0 and cc == 0), stop=(u == wo_units - 1 and cc == 1))
                        last.then_inc(wo_used, 1)

                @block.scalar
                def _(act):
                    def evac(j, b, i):
                        act.wait_ge(pr_done, PP * j + i + 1)
                        evac_piece(act, b, i).then_inc(pr_free, 1)

                    def stage(j, b, half):
                        for c in range(2):
                            r = 2 * j + c
                            act.wait_ge(max_done, r + 1)
                            wait(act, tr_done, G * (r - 1))
                            for a in range(TC):
                                act.activation(prob[:, c, :, a * P:a * P + P * (a + 1)], S[:, c, :, a * P:a * P + P * (a + 1)],
                                               ACT.Exp, bias=nmax[:, c, a:a + 1],
                                               accum_out=ssum[:, c, a:a + 1]).then_inc(ex_done, 1)
                            if not (isinstance(j, int) and j == STEPS - 1):
                                if c == 0:
                                    wait(act, pv_done, 2 * G * j)
                                for i in range(c * PP // 2, (c + 1) * PP // 2):
                                    evac(j + 1, 1 - b, i)
                            for g in range(G):
                                w = G * r + g
                                act.wait_ge(tr_done, w + 1)
                                wait(act, pv_done, w - (2 if G > 1 else 1))
                                act.activation(pT[:, g if G > 1 else c, :], ST[:, (c * G + g) % 2, 0:LINE], ACT.Copy).then_inc(pt_ev, 1)
                        act.wait_ge(pv_done, 2 * G * (j + 1))
                        o_evac(act, j)

                    def o_evac(act, j):
                        per = o_chunks // STEPS
                        act.activation(oT[:, bass.ds(per * j, per), :] if not isinstance(j, int) else oT[:, per * j:per * j + per, :],
                                       OT[:, 0:per * SEQ].rearrange("p (c t) -> p c t", c=per), ACT.Copy).then_inc(ot_ev, 1)

                    for i in range(PP):
                        evac(0, 0, i)
                    loop(act, stage)

                @block.vector
                def _(dve):
                    def stage(j, b, half):
                        for c in range(2):
                            r = 2 * j + c
                            if c == 0:
                                bias_ready(dve, j, b, half)
                            dve.wait_ge(qk_done, r + 1)
                            wait(dve, ex_done, 2 * (r - 1))
                            src = psum[:, 2 + c, 0:LINE] if G == 1 else SL[:, :, 0:LINE]
                            dst = S[:, c, 0, :] if G == 1 else S[:, c, :, :]
                            dve.scalar_tensor_tensor(out=dst, in0=src, scalar=scale, in1=bias_of(b, c), op0=ALU.mult,
                                                     op1=ALU.add).then_inc(stt_done, 1)
                            dve.wait_ge(stt_done, r + 1)
                            for a in range(TC):
                                dve.tensor_reduce(smax[:, c, a:a + 1], S[:, c, :, a * P:a * P + P * (a + 1)], AX.XY, ALU.max)\
                                   .then_inc(red_done, 1)
                            dve.wait_ge(red_done, 2 * r + 2)
                            dve.tensor_scalar(nmax[:, c, :], smax[:, c, :], -1.0, None, ALU.mult).then_inc(max_done, 1)
                            dve.wait_ge(ex_done, 2 * r + 2)
                            dve.reciprocal(sinv[:, c, :], ssum[:, c, :]).then_inc(rc_done, 1)
                            dve.wait_ge(rc_done, r + 1)
                            for a in range(TC):
                                dve.tensor_scalar(prob[:, c, :, a * P:a * P + P * (a + 1)], prob[:, c, :, a * P:a * P + P * (a + 1)],
                                                  sinv[:, c, a:a + 1], None, ALU.mult).then_inc(nrm, 1)
                    loop(dve, stage)

        def norm(*args, **kw):
            made = []
            with ExitStack() as scope:
                norm_phase(phase_sems(scope, made), tuple(spent), *args, **kw)
            spent[:] = made

        def norm_phase(sem, old, tag, which, xT_full, ar, early_loads=None, router=None, gates=None, final=False):
            gb = ar("ln_gb", [P, 2, D_MODEL])
            stats = ar("stats", [P, TC, 2, 6])
            mv = ar("mv", [P, TC, 2])
            rstd = ar("rstd", [P, TC])
            ln_in = sem(tag + "ln_in")
            res_done, st_done, ag_done = sem(tag + "res"), sem(tag + "stats"), sem(tag + "mean_var")
            eps_done, sq_done, rs_done = sem(tag + "eps"), sem(tag + "sqrt"), sem(tag + "rstd")
            cn_done, g_done, ln_done = sem(tag + "centered"), sem(tag + "gained"), sem(tag + "ln_done")
            tr_done, xf_done, xh_done, xl_done = sem(tag + "tr"), sem(tag + "xf"), sem(tag + "xh"), sem(tag + "xl")
            out_done = sem(tag + "out")
            if router is not None:
                wr = ar("wr", [P, KC, N_EXPERTS])
                eb = ar("eb", [P, N_EXPERTS])
                tri = ar("tri", [P, N_GROUPS, N_GROUPS])
                rt = {n: ar(n, [P, N_EXPERTS]) for n in
                      ("sc0", "sc1", "ch0", "ch1", "mk0", "mk1", "gt0", "gt1")}
                before = ar("before", [P, 2, P])
                most = ar("most", [1, 1])
                m8 = ar("m8", [P, TC, N_GROUPS, 8])
                gs = ar("gs", [P, TC, N_GROUPS])
                gtm = ar("gtm", [P, TC, N_GROUPS, N_GROUPS])
                eqm = ar("eqm", [P, TC, N_GROUPS, N_GROUPS])
                rank = ar("rank", [P, TC, N_GROUPS])
                pen = ar("pen", [P, TC, N_GROUPS])
                top8 = ar("top8", [P, TC, 8])
                gsum = ar("gsum", [P, TC])
                ginv = ar("ginv", [P, TC])
                gT = ar("gT", [N_EXPERTS, SEQ])
                r_in, lg_done, re_done, rc = sem(tag + "router_in"), sem(tag + "router"), sem(tag + "router_exp"), sem(tag + "route")
                gt_done, ge_done, gd_done = sem(tag + "gates_T"), sem(tag + "gates_ev"), sem(tag + "gates_dram")
                xrh, xrl, sl_mm = sem(tag + "rows_hi"), sem(tag + "rows_lo"), sem(tag + "slots_mm")
                w_router, bias_row = router

            with nc.Block() as block:
                @block.sync
                def _(sp):
                    g_row, b_row = which
                    sp.dma_start(gb[:, 0, :], g_row.partition_broadcast(P)).then_inc(ln_in, 16)
                    sp.dma_start(gb[:, 1, :], b_row.partition_broadcast(P)).then_inc(ln_in, 16)
                    if router is not None:
                        sp.dma_start(wr[:, :, :], w_router).then_inc(r_in, 16)
                        sp.dma_start(eb[:, :], bias_row.partition_broadcast(P)).then_inc(r_in, 16)
                        sp.dma_start(tri[:, :, :], t["tri"]).then_inc(r_in, 16)
                        sp.dma_start(before[:, :, :], t["before"]).then_inc(r_in, 16)
                        sp.dma_start(slot_no[:, :], t["slot_no"]).then_inc(r_in, 16)
                    if early_loads:
                        early_loads(sp)
                    if router is not None:
                        sp.wait_ge(ge_done, 1)
                        sp.dma_start(gates, gT[:, :]).then_inc(gd_done, 16)
                        sp.wait_ge(gd_done, 16)
                    if final:
                        for a in range(TC):
                            sp.wait_ge(ln_done, a + 1)
                            sp.dma_start(out[0, a * P:(a + 1) * P, :], h[:, a, :]).then_inc(out_done, 16)
                        sp.wait_ge(out_done, 16 * TC)

                @block.gpsimd
                def _(pool):
                    clear_spent(pool, old)

                @block.vector
                def _(dve):
                    for a in range(TC):
                        for n in range(2):
                            dve.scalar_tensor_tensor(out=h[:, a, n * 512:n * 512 + 512], in0=h[:, a, n * 512:n * 512 + 512],
                                                     scalar=DN_ALPHA, in1=psum[:, 2 * a + n, :], op0=ALU.mult,
                                                     op1=ALU.add).then_inc(res_done, 1)
                    for a in range(TC):
                        for n in range(2):
                            dve.wait_ge(res_done, 2 * a + n + 1)
                            dve.bn_stats(stats[:, a, n, :], h[:, a, n * 512:n * 512 + 512]).then_inc(st_done, 1)
                    for a in range(TC):
                        dve.wait_ge(st_done, 2 * a + 2)
                        dve.bn_aggr(mv[:, a, :], stats[:, a, :, :]).then_inc(ag_done, 1)
                    dve.wait_ge(ag_done, TC)
                    dve.tensor_scalar(rstd[:, :], mv[:, :, 1], NORM_EPS, None, ALU.add).then_inc(eps_done, 1)
                    dve.wait_ge(sq_done, 1)
                    dve.reciprocal(rstd[:, :], rstd[:, :]).then_inc(rs_done, 1)
                    dve.wait_ge(rs_done, 1)
                    for a in range(TC):
                        dve.tensor_scalar(h[:, a, :], h[:, a, :], mv[:, a, 0:1], rstd[:, a:a + 1], ALU.subtract, ALU.mult)\
                           .then_inc(cn_done, 1)
                    dve.wait_ge(ln_in, 32)
                    for a in range(TC):
                        dve.wait_ge(cn_done, a + 1)
                        dve.tensor_tensor(h[:, a, :], h[:, a, :], gb[:, 0, :], ALU.mult).then_inc(g_done, 1)
                        dve.wait_ge(g_done, a + 1)
                        dve.tensor_tensor(h[:, a, :], h[:, a, :], gb[:, 1, :], ALU.add).then_inc(ln_done, 1)
                    if final:
                        return
                    for i in range(2 * TC):
                        a, q = divmod(i, 2)
                        dve.wait_ge(xh_done, i + 1)
                        dve.tensor_tensor(xTl[:, 4 * q:4 * q + 4, a * P:a * P + P], xT_full[:, 4 * q:4 * q + 4, a * P:a * P + P],
                                          xTh[:, 4 * q:4 * q + 4, a * P:a * P + P].bitcast(F32), ALU.subtract).then_inc(xl_done, 1)
                    if router is None:
                        return
                    count = [0]

                    def link(ins):
                        count[0] += 1
                        ins.then_inc(rc, 1)
                        dve.wait_ge(rc, count[0])

                    dve.wait_ge(r_in, 80)
                    for a in range(TC):
                        sc, ch, mk, gt = (rt[f"{n}{a}"] for n in ("sc", "ch", "mk", "gt"))
                        dve.wait_ge(re_done, a + 1)
                        link(dve.tensor_scalar(sc[:, :], sc[:, :], 1.0, None, ALU.add))
                        link(dve.reciprocal(sc[:, :], sc[:, :]))
                        link(dve.tensor_tensor(ch[:, :], sc[:, :], eb[:, :], ALU.add))
                        for g in range(N_GROUPS):
                            ins = dve.max(m8[:, a, g, :], ch[:, g * GROUP:(g + 1) * GROUP])
                            if g < N_GROUPS - 1:
                                count[0] += 1
                                ins.then_inc(rc, 1)
                        link(ins)
                        link(dve.tensor_tensor(gs[:, a, :], m8[:, a, :, 0], m8[:, a, :, 1], ALU.add))
                        mine = gs[:, a, :].unsqueeze(2).broadcast_to([P, N_GROUPS, N_GROUPS])
                        others = gs[:, a, :].unsqueeze(1).broadcast_to([P, N_GROUPS, N_GROUPS])
                        link(dve.tensor_tensor(gtm[:, a, :, :], others, mine, ALU.is_gt))
                        link(dve.tensor_tensor(eqm[:, a, :, :], others, mine, ALU.is_equal))
                        link(dve.tensor_tensor(eqm[:, a, :, :], eqm[:, a, :, :], tri[:, :, :], ALU.mult))
                        link(dve.tensor_tensor(gtm[:, a, :, :], gtm[:, a, :, :], eqm[:, a, :, :], ALU.add))
                        link(dve.tensor_reduce(rank[:, a, :], gtm[:, a, :, :], AX.X, ALU.add))
                        link(dve.tensor_scalar(rank[:, a, :], rank[:, a, :], float(TOPK_GROUPS), None, ALU.is_lt))
                        link(dve.tensor_scalar(pen[:, a, :], rank[:, a, :], -MASKED, MASKED, ALU.mult, ALU.add))
                        chv = ch[:, :].rearrange("p (g e) -> p g e", g=N_GROUPS)
                        link(dve.tensor_tensor(chv, chv, rank[:, a, :].unsqueeze(2).broadcast_to([P, N_GROUPS, GROUP]), ALU.mult))
                        link(dve.tensor_tensor(chv, chv, pen[:, a, :].unsqueeze(2).broadcast_to([P, N_GROUPS, GROUP]), ALU.add))
                        link(dve.max(top8[:, a, :], ch[:, :]))
                        link(dve.match_replace(mk[:, :], top8[:, a, :], ch[:, :], TAKEN))
                        link(dve.tensor_scalar(mk[:, :], mk[:, :], TAKEN, None, ALU.is_equal))
                        link(dve.tensor_tensor(gt[:, :], sc[:, :], mk[:, :], ALU.mult))
                        link(dve.tensor_reduce(gsum[:, a:a + 1], gt[:, :], AX.X, ALU.add))
                        link(dve.reciprocal(ginv[:, a:a + 1], gsum[:, a:a + 1]))
                        link(dve.tensor_scalar(gate_of[:, a, :], gt[:, :], ginv[:, a:a + 1], ROUTED_SCALE, ALU.mult, ALU.mult))
                        dve.sem_inc(gt_done, 1)
                    dve.wait_ge(sl_mm, 3)
                    for a in range(TC):
                        mk = rt[f"mk{a}"]
                        link(dve.scalar_tensor_tensor(out=slot_of[:, a, :], in0=psum[:, 4 + a, 0:N_EXPERTS], scalar=1.0,
                                                      in1=mk[:, :], op0=ALU.add, op1=ALU.mult))
                        link(dve.tensor_scalar(slot_of[:, a, :], slot_of[:, a, :], -1.0, None, ALU.add))
                    link(dve.tensor_reduce(most[:, :], psum[0:1, 6, 0:N_EXPERTS], AX.X, ALU.max))
                    dve.tensor_copy(most_tokens[:, :], most[:, :])
                    for a in range(TC):
                        dve.wait_ge(xrh, a + 1)
                        dve.tensor_tensor(xl[:, a, :], h[:, a, :], xh[:, a, :].bitcast(F32), ALU.subtract).then_inc(xrl, 1)

                @block.scalar
                def _(act):
                    act.wait_ge(eps_done, 1)
                    act.activation(rstd[:, :], rstd[:, :], ACT.Sqrt).then_inc(sq_done, 1)
                    if final:
                        return
                    for i in range(2 * TC):
                        a, q = divmod(i, 2)
                        act.wait_ge(tr_done, i + 1)
                        v = psum[:, 4 + i, :].rearrange("p (k t) -> p k t", k=4)
                        act.activation(xT_full[:, 4 * q:4 * q + 4, a * P:a * P + P], v, ACT.Copy).then_inc(xf_done, 1)
                        act.activation(xTh[:, 4 * q:4 * q + 4, a * P:a * P + P], v, ACT.Copy).then_inc(xh_done, 1)
                    if router is None:
                        return
                    for a in range(TC):
                        act.activation(xh[:, a, :], h[:, a, :], ACT.Copy).then_inc(xrh, 1)
                    for a in range(TC):
                        act.wait_ge(lg_done, a + 1)
                        act.activation(rt[f"sc{a}"][:, :], psum[:, a, 0:N_EXPERTS], ACT.Exp, scale=-1.0).then_inc(re_done, 1)
                    act.wait_ge(gt_done, TC + 1)
                    act.activation(gT[:, :], psum[0:N_EXPERTS, 2, 0:SEQ], ACT.Copy).then_inc(ge_done, 1)

                @block.tensor
                def _(pe):
                    if final:
                        return
                    for i in range(2 * TC):
                        a, q = divmod(i, 2)
                        pe.wait_ge(ln_done, a + 1)
                        for k in range(4):
                            last = pe.transpose(psum[:, 4 + i, k * P:k * P + P], h[:, a, 4 * q + k::KC], ident[:, :])
                        last.then_inc(tr_done, 1)
                    if router is None:
                        return
                    pe.wait_ge(r_in, 80)
                    for a in range(TC):
                        pe.wait_ge(xf_done, 2 * a + 2)
                        for k in range(KC):
                            last = pe.matmul(psum[:, a, 0:N_EXPERTS], xT_full[:, k, a * P:a * P + P], wr[:, k, :],
                                             start=(k == 0), stop=(k == KC - 1))
                        last.then_inc(lg_done, 1)
                    for a in range(TC):
                        pe.wait_ge(gt_done, a + 1)
                        last = pe.transpose(psum[0:N_EXPERTS, 2, a * P:a * P + P], gate_of[:, a, :], ident[:, :])
                    last.then_inc(gt_done, 1)
                    pe.wait_ge(xl_done, 2 * TC)
                    pe.matmul(psum[:, 4, 0:N_EXPERTS], before[:, 0, :], rt["mk0"][:, :], start=True, stop=True).then_inc(sl_mm, 1)
                    pe.matmul(psum[:, 5, 0:N_EXPERTS], before[:, 1, :], rt["mk0"][:, :], start=True, stop=False)
                    pe.matmul(psum[:, 5, 0:N_EXPERTS], before[:, 0, :], rt["mk1"][:, :], start=False, stop=True).then_inc(sl_mm, 1)
                    for a in range(TC):
                        last = pe.matmul(psum[0:1, 6, 0:N_EXPERTS], before[:, 1, 0:1], rt[f"mk{a}"][:, :], start=(a == 0),
                                         stop=(a == TC - 1))
                    last.then_inc(sl_mm, 1)

        def expert_loads(l, raw_in):
            def views(n):
                if isinstance(n, int) and n == 0:
                    w = (t["moe_ws_gate"][l], t["moe_ws_up"][l], t["moe_ws_down"][l])
                else:
                    w = tuple(t[x][l, n - 1] for x in ("moe_w_gate", "moe_w_up", "moe_w_down"))
                return [w[0].rearrange("(p k) f -> p (k f)", k=KC), w[1].rearrange("(p k) f -> p (k f)", k=KC),
                        w[2].rearrange("(p j) d -> p (j d)", j=2)]

            def load(eng, n, b, u):
                eng.dma_start(raw[:, u, :], views(n)[u % 3]).then_inc(raw_in[u], 16)
            return load

        def experts(*args):
            made = []
            with ExitStack() as scope:
                experts_phase(phase_sems(scope, made), tuple(spent), *args)
            spent[:] = made

        def experts_phase(sem, old, l, load, raw_in, gate_in, gates):
            tag = f"m{l}_"
            ar = Arena(tag)
            hi = ar("w_hi", [P, 6, UNIT], F32R)
            lo = ar("w_lo", [P, 6, UNIT], F32R)
            rest = ar.at - arena_at
            E = ar("sig", [P, 2, 512])
            S = ar("act", [P, 512])
            H = ar("hid", [P, 512])
            gate_rows = ar("gate_rows", [P, 2, SEQ])
            Hh = ar("hid_hi", [P, 2, 2, SEQ], F32R)
            Hl = ar("hid_lo", [P, 2, 2, SEQ], F32R)
            N = N_EXPERTS + 1
            hi_done = [sem(f"{tag}hi{i}") for i in range(3)]
            lo_done = [sem(f"{tag}lo{i}") for i in range(3)]
            mm_done = [sem(tag + "gate_done"), sem(tag + "up_done"), sem(tag + "down_done")]
            silu_done, act_done, hid_done = sem(tag + "silu"), sem(tag + "act"), sem(tag + "hidden")
            hh_done, hl_done = sem(tag + "hid_hi"), sem(tag + "hid_lo")

            class Dense:

                @staticmethod
                def upper(act, n, b, half, i):
                    act.wait_ge(raw_in[3 * (1 - b) + i], 16 * half + 16)
                    wait(act, mm_done[i], n - 1)
                    act.activation(hi[:, 3 * (1 - b) + i, :], raw[:, 3 * (1 - b) + i, :], ACT.Copy).then_inc(hi_done[i], 1)

                @staticmethod
                def lower(dve, n, b, half, i):
                    dve.wait_ge(hi_done[i], n + 1)
                    wait(dve, mm_done[i], n - 1)
                    u = 3 * (1 - b) + i
                    dve.tensor_tensor(lo[:, u, :], raw[:, u, :], hi[:, u, :].bitcast(F32), ALU.subtract).then_inc(lo_done[i], 1)

                @staticmethod
                def act_stage(act, n, b, half, more):
                    nxt = (n + 1, 1 - b, half + b)
                    if more:
                        Dense.upper(act, *nxt, 0)
                        Dense.upper(act, *nxt, 1)
                    act.wait_ge(mm_done[0], n + 1)
                    wait(act, act_done, n - 1)
                    act.activation(E[:, b, :], psum[:, 4 + 2 * b, :], ACT.Silu).then_inc(silu_done, 1)
                    if more:
                        Dense.upper(act, *nxt, 2)
                    act.wait_ge(hid_done, n + 1)
                    wait(act, mm_done[2], n - 1)
                    act.activation(Hh[:, b, :, :].rearrange("p j t -> p (j t)"), H[:, :], ACT.Copy).then_inc(hh_done, 1)

                @staticmethod
                def dve_stage(dve, n, b, half, more):
                    nxt = (n + 1, 1 - b, half + b)
                    if more:
                        Dense.lower(dve, *nxt, 0)
                        Dense.lower(dve, *nxt, 1)
                    dve.wait_ge(silu_done, n + 1)
                    dve.wait_ge(mm_done[1], n + 1)
                    wait(dve, hid_done, n)
                    dve.tensor_tensor(S[:, :], E[:, b, :], psum[:, 5 + 2 * b, :], ALU.mult).then_inc(act_done, 1)
                    dve.wait_ge(act_done, n + 1)
                    wait(dve, hl_done, n)
                    if isinstance(n, int) and n == 0:
                        dve.tensor_copy(H[:, :], S[:, :]).then_inc(hid_done, 1)
                    else:
                        dve.wait_ge(gate_in[b], 16 * half + 16 * b)
                        dve.tensor_tensor(H[:, :].rearrange("p (j t) -> p j t", j=2), S[:, :].rearrange("p (j t) -> p j t", j=2),
                                          gate_rows[:, b, :].unsqueeze(1).broadcast_to([P, 2, SEQ]), ALU.mult)\
                           .then_inc(hid_done, 1)
                    if more:
                        Dense.lower(dve, *nxt, 2)
                    dve.wait_ge(hh_done, n + 1)
                    wait(dve, mm_done[2], n - 1)
                    dve.tensor_tensor(Hl[:, b, :, :].rearrange("p j t -> p (j t)"), H[:, :],
                                      Hh[:, b, :, :].rearrange("p j t -> p (j t)").bitcast(F32), ALU.subtract).then_inc(hl_done, 1)

                @staticmethod
                def gate_up(pe, n, b):
                    wait(pe, act_done, n - 1)
                    for i in range(2):
                        pe.wait_ge(hi_done[i], n + 1)
                        pe.wait_ge(lo_done[i], n + 1)
                        for j in range(2):
                            for step, (w, x) in enumerate(((hi, xTh), (hi, xTl), (lo, xTh))):
                                for k in range(KC):
                                    wk = w[:, 3 * (1 - b) + i, k * D_EXPERT + j:(k + 1) * D_EXPERT:2]
                                    last = pe.matmul(psum[:, 4 + 2 * b + i, j * SEQ:(j + 1) * SEQ], wk, x[:, k, :],
                                                     start=(step == 0 and k == 0), stop=(step == 2 and k == KC - 1))
                        last.then_inc(mm_done[i], 1)

                @staticmethod
                def down(pe, n, b):
                    first = isinstance(n, int) and n == 0
                    final = isinstance(n, int) and n == N - 1
                    for ready in (hi_done[2], lo_done[2], hh_done, hl_done):
                        pe.wait_ge(ready, n + 1)
                    for step, (x, w) in enumerate(((Hh, hi), (Hh, lo), (Hl, hi))):
                        for j in range(2):
                            for a in range(TC):
                                for m in range(2):
                                    last = pe.matmul(psum[:, 2 * a + m, :], x[:, b, j, a * P:a * P + P],
                                                     w[:, 3 * (1 - b) + 2, j * D_MODEL + m * 512:j * D_MODEL + m * 512 + 512],
                                                     start=(first and step == 0 and j == 0),
                                                     stop=(final and step == 2 and j == 1), skip_group_check=True)
                    last.then_inc(mm_done[2], 1)

                @staticmethod
                def loop(eng, stage):
                    stage(1, 1, 0, True)
                    with eng.Fori(0, N_EXPERTS // 2 - 1) as it:
                        stage(2 * it + 2, 0, it + 1, True)
                        stage(2 * it + 3, 1, it + 1, True)
                    stage(N - 1, 0, (N - 1) // 2, False)

            ov = Arena(tag + "x", start=xT_at - arena_at)
            X = ov("X", [P, 4, KC, P], F32R)
            ar = Arena(tag + "s", start=rest)
            yh = ar("y_hi", [P, 2, 512], F32R)
            yl = ar("y_lo", [P, 2, 512], F32R)
            pick = ar("pick", [P, TC, 2 * P], F32R)
            pickT = ar("pickT", [P, 2, SEQ], F32R)
            hidh = ar("s_hid_hi", [P, 2, 2, P], F32R)
            hidl = ar("s_hid_lo", [P, 2, 2, P], F32R)
            part = ar("part", [P, 512])
            gu = ar("gate_up", [P, 512])
            av = ar("s_act", [P, D_EXPERT])
            gsl = ar("slot_gate", [P, 2])
            gq = ar("pair_gates", [P, TC, 4])
            gu_hi = [sem(f"{tag}gu_hi{x}") for x in "AB"]
            whi = [sem(f"{tag}whi{u}") for u in range(6)]
            wlo = [sem(f"{tag}wlo{u}") for u in range(6)]
            gu_mm = [sem(f"{tag}gu_mm{x}") for x in "AB"]
            part_done = [sem(f"{tag}part{x}") for x in "AB"]
            sum_done = [sem(f"{tag}sum{x}") for x in "AB"]
            names = ("zeroed pick gather xhi xlo ptmm pt gsl gates silu sact htmm hhi hlo ymm yhi ylo comb").split()
            sm = {n: sem(f"{tag}s_{n}") for n in names}
            NP = N_EXPERTS // 2
            R0, R1 = psum[:, 6, :], psum[:, 7, :]
            CAB = [psum[:, 4, :], psum[:, 5, :]]

            def X_upper(r):
                return X[:, :, 2 * r:2 * r + 2, 0:SLOTS].rearrange("p c k s -> p k c s")

            def X_lower(r):
                return X[:, :, 2 * r:2 * r + 2, SLOTS:P].rearrange("p c k s -> p k c s")

            def gathered(r):
                return psum[:, 6 + r % 2, :].rearrange("p (k c s) -> p k c s", k=2, c=4)

            def hid_slots(tensor):
                v = tensor[:, :, :, :]
                return bass.AP(v.tensor, v.offset, [list(v.ap[0]), [P, 2], [2 * P + SLOTS, 2], [1, SLOTS]])

            def run_pairs(eng, stage):
                stage(0, 0, 0, True)
                stage(1, 1, 0, True)
                with eng.Fori(1, NP // 2 - 1) as it:
                    stage(2 * it, 0, it, True)
                    stage(2 * it + 1, 1, it, True)
                stage(NP - 2, 0, NP // 2 - 1, True)
                stage(NP - 1, 1, NP // 2 - 1, False)

            def by_load(eng, sparse, dense):
                most = eng.value_load(most_tokens[0:1, 0:1], min_val=0, max_val=SEQ)
                with eng.If(most <= SLOTS):
                    sparse()
                with eng.Else():
                    dense()

            with nc.Block() as block:
                @block.sync
                def _(sp):
                    def sparse():
                        def slot(p, u):
                            sp.wait_ge(wlo[u], p)
                            load(sp, 2 * p + 1 + u // 3, 0, u)
                        for i in range(3):
                            sp.wait_ge(lo_done[i], 1)
                            load(sp, 2, 0, 3 + i)
                        for p, u in ((1, 0), (1, 1), (1, 3), (1, 4), (2, 0), (2, 1)):
                            slot(p, u)
                        order = ((2, 3), (1, 5), (2, 4), (1, 2), (3, 0), (3, 1))
                        with sp.Fori(0, NP - 3) as p:
                            for ahead, u in order:
                                slot(p + ahead, u)
                        for p in (NP - 3, NP - 2):
                            for ahead, u in order:
                                if p + ahead < NP:
                                    slot(p + ahead, u)

                    def dense():
                        def units(n, b):
                            for i in range(3):
                                sp.wait_ge(lo_done[i], n - 1)
                                load(sp, n, b, 3 * (1 - b) + i)
                        with sp.Fori(0, N_EXPERTS // 2 - 1) as it:
                            units(2 * it + 2, 0)
                            units(2 * it + 3, 1)
                        units(N - 1, 0)
                    by_load(sp, sparse, dense)

                @block.gpsimd
                def _(pool):
                    clear_spent(pool, old)

                    def sparse():
                        pool.wait_ge(mm_done[2], 1)
                        pool.memset(hidh[:, :, :, :].rearrange("p a j s -> p (a j s)").bitcast(F32), 0.0).then_inc(sm["zeroed"], 1)
                        pool.memset(hidl[:, :, :, :].rearrange("p a j s -> p (a j s)").bitcast(F32), 0.0).then_inc(sm["zeroed"], 1)

                        with pool.Fori(0, NP) as p:
                            pool.wait_ge(whi[5], p + 1)
                            pool.tensor_tensor(lo[:, 5, :], raw[:, 5, :], hi[:, 5, :].bitcast(F32), ALU.subtract).then_inc(wlo[5], 1)

                    def dense():
                        def row(n, b):
                            pool.dma_start(gate_rows[:, b, :], gates[n - 1, :].partition_broadcast(P)).then_inc(gate_in[b], 16)
                        row(1, 1)
                        row(2, 0)
                        with pool.Fori(0, N_EXPERTS // 2 - 1) as it:
                            pool.wait_ge(hid_done, 2 * it + 2)
                            row(2 * it + 3, 1)
                            pool.wait_ge(hid_done, 2 * it + 3)
                            row(2 * it + 4, 0)
                    by_load(pool, sparse, dense)

                @block.scalar
                def _(act):
                    for i in range(3):
                        Dense.upper(act, 0, 0, 0, i)
                    Dense.act_stage(act, 0, 0, 0, False)

                    def sparse():
                        def upper(p, u):
                            act.wait_ge(raw_in[u], 16 * p + (16 if u < 3 else 32))
                            if isinstance(p, int) and p == 0:
                                if u >= 3:
                                    act.wait_ge(mm_done[u - 3], 1)
                            else:
                                act.wait_ge(gu_hi[u // 3] if u % 3 < 2 else sm["ymm"], p if u % 3 < 2 else 2 * p)
                            act.activation(hi[:, u, :], raw[:, u, :], ACT.Copy).then_inc(whi[u], 1)

                        def slots_in(q):
                            wait(act, gu_mm[1], 2 * q)
                            for r in range(4):
                                act.wait_ge(sm["gather"], 4 * q + r + 1)
                                act.activation(X_upper(r), gathered(r), ACT.Copy).then_inc(sm["xhi"], 1)

                        def picks(p, b):
                            act.wait_ge(sm["ptmm"], p + 1)
                            wait(act, sm["comb"], p - 1)
                            act.activation(pickT[:, b, :], R0[:, 0:SEQ], ACT.Copy).then_inc(sm["pt"], 1)
                            for x in range(2):
                                q = slice(x * SLOTS, (x + 1) * SLOTS)
                                act.activation(gsl[q, b:b + 1], psum[q, 6, SEQ + x:SEQ + x + 1], ACT.Copy).then_inc(sm["gsl"], 1)

                        def partial(p, x):
                            act.wait_ge(gu_mm[x], p + 1)
                            wait(act, sum_done[x], p)
                            dst, src = slice(x * SLOTS, (x + 1) * SLOTS), slice((1 - x) * SLOTS, (2 - x) * SLOTS)
                            act.activation(part[dst, :], psum[src, 4 + x, :], ACT.Copy).then_inc(part_done[x], 1)

                        act.wait_ge(mm_done[2], 1)
                        slots_in(0)
                        upper(0, 0)
                        upper(0, 1)
                        picks(0, 0)
                        upper(0, 3)
                        upper(0, 4)
                        partial(0, 0)
                        upper(1, 0)
                        upper(1, 1)
                        upper(1, 3)

                        def stage(p, b, half, more):
                            two_more = more and not (isinstance(p, int) and p == NP - 2)
                            partial(p, 1)
                            upper(p, 5)
                            act.wait_ge(sum_done[1], p + 1)
                            wait(act, sm["htmm"], p)
                            act.activation(av[:, :], gu[:, 0:D_EXPERT], ACT.Silu).then_inc(sm["silu"], 1)
                            if more:
                                picks(p + 1, 1 - b)
                                upper(p + 1, 4)
                            upper(p, 2)
                            act.wait_ge(sm["htmm"], p + 1)
                            if isinstance(p, int) and p == 0:
                                act.wait_ge(sm["zeroed"], 2)
                            wait(act, sm["ymm"], 2 * p)
                            act.activation(hid_slots(hidh), R1[:, 0:SEQ].rearrange("p (j x s) -> p j x s", j=2, x=2),
                                           ACT.Copy).then_inc(sm["hhi"], 1)
                            if more:
                                partial(p + 1, 0)
                            if two_more:
                                upper(p + 2, 0)
                                upper(p + 2, 1)
                            for m in range(2):
                                act.wait_ge(sm["ymm"], 2 * p + m + 1)
                                wait(act, sm["comb"], p)
                                act.activation(yh[:, m, :], psum[:, 6 + m, :], ACT.Copy, scale=gsl[:, b:b + 1]).then_inc(sm["yhi"], 1)
                                if two_more and m == 0:
                                    upper(p + 2, 3)
                            if two_more and b == 0:
                                slots_in(half + 1)

                        run_pairs(act, stage)

                    def dense():
                        for i in range(3):
                            Dense.upper(act, 1, 1, 0, i)
                        Dense.loop(act, lambda *s: Dense.act_stage(act, *s))
                    by_load(act, sparse, dense)

                @block.vector
                def _(dve):
                    for i in range(3):
                        Dense.lower(dve, 0, 0, 0, i)
                    Dense.dve_stage(dve, 0, 0, 0, False)

                    def sparse():
                        def lower(p, u):
                            dve.wait_ge(whi[u], p + 1)
                            if u % 3 < 2:
                                wait(dve, gu_mm[u // 3], p)
                            dve.tensor_tensor(lo[:, u, :], raw[:, u, :], hi[:, u, :].bitcast(F32), ALU.subtract).then_inc(wlo[u], 1)

                        def slots_in(q):
                            for r in range(4):
                                dve.wait_ge(sm["xhi"], 4 * q + r + 1)
                                dve.tensor_tensor(X_lower(r), gathered(r), X_upper(r).bitcast(F32), ALU.subtract)\
                                   .then_inc(sm["xlo"], 1)

                        def total(p, x):
                            dve.wait_ge(part_done[x], p + 1)
                            wait(dve, sm["sact"], p)
                            q = slice(x * SLOTS, (x + 1) * SLOTS)
                            dve.tensor_tensor(gu[q, :], part[q, :], psum[q, 4 + x, :], ALU.add).then_inc(sum_done[x], 1)

                        def build(q):
                            wait(dve, sm["ptmm"], 2 * q)
                            where = (slice(4 * q, 4 * q + 4) if isinstance(q, int) else bass.ds(4 * q, 4))
                            dve.tensor_tensor(pick[:, :, :].rearrange("p a (x s) -> p a x s", x=4),
                                              slot_no[:, :].unsqueeze(1).unsqueeze(1).broadcast_to([P, TC, 4, SLOTS]),
                                              slot_of[:, :, where].unsqueeze(3).broadcast_to([P, TC, 4, SLOTS]),
                                              ALU.is_equal).then_inc(sm["pick"], 1)
                            dve.tensor_copy(gq[:, :, :], gate_of[:, :, where]).then_inc(sm["gates"], 1)

                        dve.wait_ge(mm_done[2], 1)
                        build(0)
                        slots_in(0)
                        for u in (0, 1, 3, 4):
                            lower(0, u)
                        total(0, 0)
                        lower(1, 0)
                        lower(1, 1)

                        def stage(p, b, half, more):
                            two_more = more and not (isinstance(p, int) and p == NP - 2)
                            total(p, 1)
                            if more:
                                lower(p + 1, 3)
                            dve.wait_ge(sm["silu"], p + 1)
                            dve.wait_ge(sum_done[1], p + 1)
                            dve.tensor_tensor(av[:, :], av[:, :], gu[:, D_EXPERT:], ALU.mult).then_inc(sm["sact"], 1)
                            if more:
                                lower(p + 1, 4)
                            dve.wait_ge(sm["hhi"], p + 1)
                            dve.tensor_tensor(hid_slots(hidl), R1[:, 0:SEQ].rearrange("p (j x s) -> p j x s", j=2, x=2),
                                              hid_slots(hidh).bitcast(F32), ALU.subtract).then_inc(sm["hlo"], 1)
                            lower(p, 2)
                            if more:
                                total(p + 1, 0)
                            if two_more:
                                if b == 0:
                                    build(half + 1)
                                lower(p + 2, 0)
                            for m in range(2):
                                dve.wait_ge(sm["yhi"], 2 * p + m + 1)
                                dve.scalar_tensor_tensor(out=yl[:, m, :], in0=psum[:, 6 + m, :], scalar=gsl[:, b:b + 1],
                                                         in1=yh[:, m, :].bitcast(F32), op0=ALU.mult, op1=ALU.subtract)\
                                   .then_inc(sm["ylo"], 1)
                                if two_more and m == 0:
                                    lower(p + 2, 1)
                            if two_more and b == 0:
                                slots_in(half + 1)
                        run_pairs(dve, stage)

                    def dense():
                        for i in range(3):
                            Dense.lower(dve, 1, 1, 0, i)
                        Dense.loop(dve, lambda *s: Dense.dve_stage(dve, *s))
                    by_load(dve, sparse, dense)

                @block.tensor
                def _(pe):
                    Dense.gate_up(pe, 0, 0)
                    Dense.down(pe, 0, 0)

                    def sparse():
                        def gather(q, r):
                            if r >= 2:
                                pe.wait_ge(sm["xlo"], 4 * q + r - 1)
                            for kk in range(2):
                                for s, x in enumerate((xh, xl)):
                                    for a in range(TC):
                                        last = pe.matmul(psum[:, 6 + r % 2, kk * 2 * P:(kk + 1) * 2 * P],
                                                         x[:, a, 2 * r + kk::KC], pick[:, a, :],
                                                         start=(s == 0 and a == 0), stop=(s == 1 and a == TC - 1))
                            last.then_inc(sm["gather"], 1)

                        def picks(p, b, half):
                            if b == 0:
                                pe.wait_ge(sm["xlo"], 4 * half + 3)
                            elif isinstance(p, int) and p == 1:
                                pe.wait_ge(sm["gsl"], 2)
                            wait(pe, sm["ylo"], 2 * (p - 1))
                            for a in range(TC):
                                pe.transpose(R0[:, a * P:a * P + P], pick[:, a, b * P:b * P + P].bitcast(F32), ident[:, :])
                            pe.wait_ge(sm["gates"], half + 1)
                            for a in range(TC):
                                last = pe.matmul(R0[:, SEQ:SEQ + 2], pick[:, a, b * P:b * P + P].bitcast(F32), gq[:, a, 2 * b:2 * b + 2],
                                                 start=(a == 0), stop=(a == TC - 1))
                            last.then_inc(sm["ptmm"], 1)

                        def gate_up(p, b, half, x, s):
                            if s == 0:
                                pe.wait_ge(sm["xlo"], 4 * half + 4)
                                wait(pe, sum_done[x], p)
                            w, ready = ((hi, whi), (lo, wlo))[s]
                            for i in range(2):
                                pe.wait_ge(ready[3 * x + i], p + 1)
                            for k in range(KC):
                                last = pe.matmul(CAB[x].rearrange("p (i f) -> p i f", i=2), X[:, 2 * b + x, k, :],
                                                 w[:, 3 * x:3 * x + 2, k * D_EXPERT:(k + 1) * D_EXPERT],
                                                 start=(s == 0 and k == 0), stop=(s == 1 and k == KC - 1))
                            last.then_inc((gu_hi, gu_mm)[s][x], 1)

                        def hidden(p, half, final):
                            pe.wait_ge(sm["sact"], p + 1)
                            for j in range(2):
                                last = pe.transpose(R1[:, j * P:j * P + P], av[:, j::2], ident[:, :])
                            last.then_inc(sm["htmm"], 1)

                        def down(p, final):
                            pe.wait_ge(sm["hlo"], p + 1)
                            pe.wait_ge(sm["gsl"], (2 * p + 4) if not final else 2 * NP)
                            for m in range(2):
                                for s, (hd, w) in enumerate(((hidh, hi), (hidl, hi), (hidh, lo))):
                                    for x in range(2):
                                        if m == 0 and s != 1:
                                            pe.wait_ge((whi if s == 0 else wlo)[3 * x + 2], p + 1)
                                        for j in range(2):
                                            last = pe.matmul(psum[:, 6 + m, :], hd[:, x, j, :],
                                                             w[:, 3 * x + 2, j * D_MODEL + m * 512:j * D_MODEL + m * 512 + 512],
                                                             start=(x == 0 and s == 0 and j == 0),
                                                             stop=(x == 1 and s == 2 and j == 1))
                                last.then_inc(sm["ymm"], 1)

                        def combine(p, b, m, final):
                            pe.wait_ge(sm["ylo"], 2 * p + m + 1)
                            for a in range(TC):
                                for s, y in enumerate((yh, yl)):
                                    last = pe.matmul(psum[:, 2 * a + m, :], pickT[:, b, a * P:a * P + P], y[:, m, :],
                                                     start=False, stop=(final and s == 1), skip_group_check=True)
                            if m == 1:
                                last.then_inc(sm["comb"], 1)

                        def stage(p, b, half, more):
                            nxt = (p + 1, 1 - b, half + b)
                            next_quad = more and b == 0 and not (isinstance(p, int) and p == NP - 2)
                            if more:
                                picks(*nxt)
                                gate_up(*nxt, 0, 0)
                                gate_up(*nxt, 0, 1)
                            hidden(p, half, not more)
                            if more:
                                gate_up(*nxt, 1, 0)
                            down(p, not more)
                            if more:
                                gate_up(*nxt, 1, 1)
                            if next_quad:
                                pe.wait_ge(sm["pick"], half + 2)
                            for m in range(2):
                                combine(p, b, m, not more)
                                if next_quad:
                                    gather(half + 1, m)
                            if next_quad:
                                gather(half + 1, 2)
                                gather(half + 1, 3)

                        pe.wait_ge(sm["pick"], 1)
                        for r in range(4):
                            gather(0, r)
                        picks(0, 0, 0)
                        for x in range(2):
                            for s in range(2):
                                gate_up(0, 0, 0, x, s)
                        run_pairs(pe, stage)

                    def dense():
                        Dense.gate_up(pe, 1, 1)

                        def stage(n, b, half, more):
                            if more:
                                Dense.gate_up(pe, n + 1, 1 - b)
                            Dense.down(pe, n, b)
                        Dense.loop(pe, stage)
                    by_load(pe, sparse, dense)

        scale_a = A_HD ** -0.5
        ar = Arena("a")
        xT = ar("xT", [P, KC, SEQ])
        kT = ar("kT", [P, SEQ])
        v_a = ar("v", [P, TC, A_HD])
        sel = ar("sel", [P, LINE])
        bias_in_a = ar("bias", [P, 2, 2, LINE])
        bias_sel = ar("bias_sel", [P, 2, 2, LINE])
        q_a = ar("q", [P, 2, 2, SEQ])
        mark = ar.at - arena_at
        qiT = ar("qiT", [P, IDX_HEADS // 2, SEQ])
        kiT = ar("kiT", [P, SEQ])
        wi = ar("wi", [P, TC, IDX_HEADS])
        rel = ar("rel", [P, 2, SEQ])
        score = ar("score", [P, TC, SEQ])
        best = ar("best", [P, TC, 8])
        causal = ar("causal", [P, P])
        lines = ar("lines", [REL_HEADS, 1 + len(B_GROUPS), LINE])
        rel_tab = ar("rel_tab", [REL_BUCKETS + 1, REL_HEADS])
        hot = ar("hot", [REL_BUCKETS + 1, 1 + len(B_GROUPS), LINE])

        made = []
        prelude_scope = ExitStack()
        q_in = [sem(f"qa_in{i}") for i in range(2)]
        all_sem, sem = sem, phase_sems(prelude_scope, made)
        x_in, h_in, c_in, rel_in, neg_done = sem("x_in"), sem("h_in"), sem("const_in"), sem("rel_in"), sem("masked_row")
        wa_in = [sem(f"wa_in{i}") for i in range(4)]
        line_mm, line_ev, line_dram = sem("line_mm"), sem("line_ev"), sem("line_dram")
        pre_mm, pre_ev, s_mm, s_relu, s_acc, tk, sel_done = (sem("pre_mm"), sem("pre_ev"), sem("score_mm"), sem("score_relu"),
                                                             sem("score_acc"), sem("topk_step"), sem("sel_done"))
        wa = t["a_w_in_parts"]

        def load_q(eng, j, b):
            eng.dma_start(raw[:, 4 + b, :], t["a_w_q"][j]).then_inc(q_in[b], 16)

        with nc.Block() as block:
            @block.sync
            def _(sp):
                sp.dma_start(rel_tab[0:REL_BUCKETS, :], t["rel_bias"]).then_inc(rel_in, 16)
                sp.dma_start(hot[:, :, :], t["hot"]).then_inc(rel_in, 16)
                sp.dma_start(xT[:, :, :], t["x_T"]).then_inc(x_in, 16)
                sp.dma_start(raw[:, 0, 0:KC * 136], t["a_w_ki"]).then_inc(wa_in[0], 16)
                for i in range(2):
                    sp.dma_start(raw[:, 1 + i, :], wa[i]).then_inc(wa_in[1 + i], 16)
                sp.dma_start(causal[:, :], t["causal"]).then_inc(c_in, 16)
                sp.dma_start(raw[:, 3, :], wa[2]).then_inc(wa_in[3], 16)
                sp.dma_start(ident[:, :], t["ident"]).then_inc(c_in, 16)
                load_q(sp, 0, 0)
                load_q(sp, 1, 1)
                sp.dma_start(h[:, :, :], t["x"][0].rearrange("(a p) d -> p a d", p=P)).then_inc(h_in, 16)
                sp.wait_ge(line_ev, 4)
                sp.dma_start(lines_d.rearrange("g h m -> h g m"), lines[:, :, :]).then_inc(line_dram, 16)
                sp.wait_ge(line_dram, 16)
                sp.wait_ge(h_in, 16)
                sp.wait_ge(c_in, 32)

            @block.gpsimd
            def _(pool):
                pool.memset(rel_tab[REL_BUCKETS:REL_BUCKETS + 1, :], MASKED).then_inc(neg_done, 1)

            @block.tensor
            def _(pe):
                pe.wait_ge(rel_in, 32)
                pe.wait_ge(neg_done, 1)
                for g in range(1 + len(B_GROUPS)):
                    pe.matmul(psum[0:REL_HEADS, 2 + g, 0:LINE], rel_tab[:, :], hot[:, g, :], start=True, stop=True)\
                      .then_inc(line_mm, 1)
                pe.wait_ge(x_in, 16)
                pe.wait_ge(wa_in[0], 16)
                wk = raw[:, 0, 0:KC * 136].rearrange("p (k c) -> p k c", k=KC)
                for k in range(KC):
                    last = pe.matmul(psum[:, 0, 0:SEQ], wk[:, k, 0:P], xT[:, k, :], start=(k == 0), stop=(k == KC - 1))
                last.then_inc(pre_mm, 1)
                for a in range(TC):
                    for k in range(KC):
                        last = pe.matmul(psum[:, 1, a * IDX_HEADS:(a + 1) * IDX_HEADS], xT[:, k, a * P:a * P + P],
                                         wk[:, k, P:P + IDX_HEADS], start=(k == 0), stop=(k == KC - 1))
                last.then_inc(pre_mm, 1)
                for c in range(4):
                    if c % 2 == 0:
                        pe.wait_ge(wa_in[1 + c // 2], 16)
                    wv = raw[:, 1 + c // 2, :].rearrange("p (k c) -> p k c", k=KC)
                    pe.wait_ge(line_ev, c + 1)
                    for k in range(KC):
                        last = pe.matmul(psum[:, 2 + c, 0:SEQ], wv[:, k, (c % 2) * P:(c % 2) * P + P], xT[:, k, :],
                                         start=(k == 0), stop=(k == KC - 1))
                    last.then_inc(pre_mm, 1)
                pe.wait_ge(pre_ev, 6)
                for n in range(TC * IDX_HEADS):
                    a, hd = TC - 1 - n // IDX_HEADS, n % IDX_HEADS
                    wait(pe, s_relu, n - 1)
                    r0 = IDX_HD * (hd % 2)
                    pe.matmul(psum[:, n % 2, 0:P * (a + 1)], qiT[r0:r0 + IDX_HD, hd // 2, a * P:a * P + P],
                              kiT[r0:r0 + IDX_HD, 0:P * (a + 1)], start=True, stop=True).then_inc(s_mm, 1)
                    if n == IDX_HEADS - 1:
                        pe.wait_ge(wa_in[3], 16)
                        wv = raw[:, 3, :].rearrange("p (k c) -> p k c", k=KC)
                        for k in range(KC):
                            last = pe.matmul(psum[:, 6, 0:SEQ], wv[:, k, 0:A_HD], xT[:, k, :], start=(k == 0), stop=(k == KC - 1))
                        last.then_inc(pre_mm, 1)
                        for aa in range(TC):
                            for k in range(KC):
                                last = pe.matmul(psum[:, 7, aa * A_HD:(aa + 1) * A_HD], xT[:, k, aa * P:aa * P + P],
                                                 wv[:, k, A_HD:2 * A_HD], start=(k == 0), stop=(k == KC - 1))
                        last.then_inc(pre_mm, 1)

            @block.scalar
            def _(act):
                for g in range(1 + len(B_GROUPS)):
                    act.wait_ge(line_mm, g + 1)
                    act.activation(lines[:, g, :], psum[0:REL_HEADS, 2 + g, 0:LINE], ACT.Copy).then_inc(line_ev, 1)
                act.wait_ge(pre_mm, 1)
                act.activation(kiT[:, :], psum[:, 0, 0:SEQ], ACT.Copy).then_inc(pre_ev, 1)
                act.wait_ge(pre_mm, 2)
                act.activation(wi[:, :, :], psum[:, 1, 0:TC * IDX_HEADS].rearrange("p (a h) -> p a h", a=TC), ACT.Copy,
                               scale=IDX_HEADS ** -0.5).then_inc(pre_ev, 1)
                for c in range(4):
                    act.wait_ge(pre_mm, 3 + c)
                    act.activation(qiT[:, c, :], psum[:, 2 + c, 0:SEQ], ACT.Copy).then_inc(pre_ev, 1)
                for n in range(TC * IDX_HEADS):
                    a = TC - 1 - n // IDX_HEADS
                    act.wait_ge(s_mm, n + 1)
                    wait(act, s_acc, n - 1)
                    act.activation(rel[:, n % 2, 0:P * (a + 1)], psum[:, n % 2, 0:P * (a + 1)], ACT.Relu,
                                   scale=IDX_HD ** -0.5).then_inc(s_relu, 1)
                act.wait_ge(pre_mm, 7)
                act.activation(kT[:, :], psum[:, 6, 0:SEQ], ACT.Copy).then_inc(pre_ev, 1)
                act.wait_ge(pre_mm, 8)
                act.activation(v_a[:, :, :], psum[:, 7, 0:TC * A_HD].rearrange("p (a e) -> p a e", a=TC), ACT.Copy).then_inc(pre_ev, 1)

            @block.vector
            def _(dve):
                steps = [0]

                def link(ins):
                    steps[0] += 1
                    ins.then_inc(tk, 1)
                    dve.wait_ge(tk, steps[0])

                dve.wait_ge(pre_ev, 2)
                dve.wait_ge(c_in, 32)
                for ai in range(TC):
                    a = TC - 1 - ai
                    n_keys = P * (a + 1)
                    sc = score[:, a, 0:n_keys]
                    for hd in range(IDX_HEADS):
                        n = ai * IDX_HEADS + hd
                        dve.wait_ge(s_relu, n + 1)
                        if hd == 0:
                            dve.tensor_scalar(sc, rel[:, n % 2, 0:n_keys], wi[:, a, hd:hd + 1], None, ALU.mult).then_inc(s_acc, 1)
                        else:
                            dve.wait_ge(s_acc, n)
                            dve.scalar_tensor_tensor(out=sc, in0=rel[:, n % 2, 0:n_keys], scalar=wi[:, a, hd:hd + 1], in1=sc,
                                                     op0=ALU.mult, op1=ALU.add).then_inc(s_acc, 1)
                    dve.wait_ge(s_acc, (ai + 1) * IDX_HEADS)
                    dg = score[:, a, a * P:a * P + P]
                    link(dve.tensor_tensor(dg, dg, causal[:, :], ALU.add))
                    for rnd in range(TOPK_KEYS // 8):
                        link(dve.max(best[:, a, :], sc))
                        link(dve.match_replace(sc, best[:, a, :], sc, TAKEN))
                    dst = sel[:, a * P:a * P + n_keys]
                    link(dve.tensor_scalar(sc, sc, TAKEN, -MASKED, ALU.is_equal, ALU.mult))
                    link(dve.tensor_scalar(dst, sc, MASKED, None, ALU.add))

        prelude_scope.close()
        spent[:] = made
        sem = all_sem
        bias_in = [sem(f"bias_a_in{i}") for i in range(2)]
        wo_a = t["a_w_o"][0].rearrange("(u c p) n -> u p c n", c=2, p=P)
        sel_used = sem("bias_sel_ready")

        def a_first(sp, pr_done):
            for j in range(2):
                sp.dma_start(bias_in_a[:, j, :, SEQ:LINE], bias_tile(0, 1, j, P)[:, 0]).then_inc(bias_in[j], 16)
                sp.dma_start(bias_in_a[:, j, :, 0:SEQ], bias_tile(0, 1, j, SEQ)[:, 0]).then_inc(bias_in[j], 16)

        def a_loop(sp, pr_done, stt_done):
            with sp.Fori(0, STEPS // 2 - 1) as it:
                for b in range(2):
                    j = 2 * it + 2 + b
                    sp.wait_ge(pr_done, 2 * j - 2)
                    load_q(sp, j, b)
                    sp.wait_ge(sel_used, 2 * j - 2)
                    sp.dma_start(bias_in_a[:, b, :, SEQ:LINE], bias_tile(0, 1, j, P)[:, 0]).then_inc(bias_in[b], 16)
                    sp.dma_start(bias_in_a[:, b, :, 0:SEQ], bias_tile(0, 1, j, SEQ)[:, 0]).then_inc(bias_in[b], 16)

        def a_pool(pool, stt_done):
            def combine(j, b, half, first):
                pool.wait_ge(bias_in[b], 32 * half + 32)
                if not first:
                    pool.wait_ge(stt_done, 2 * j - 2)
                for c in range(2):
                    pool.tensor_tensor(bias_sel[:, b, c, :], bias_in_a[:, b, c, ::-1], sel[:, :], ALU.add).then_inc(sel_used, 1)
            combine(0, 0, 0, True)
            combine(1, 1, 0, True)
            with pool.Fori(0, STEPS // 2 - 1) as it:
                combine(2 * it + 2, 0, it + 1, False)
                combine(2 * it + 3, 1, it + 1, False)

        def a_project(pe, j, b, half, i):
            if i == 0:
                pe.wait_ge(q_in[b], 16 * half + 16)
            wq = raw[:, 4 + b, :].rearrange("p (k c) -> p k c", k=KC)
            for k in range(KC):
                last = pe.matmul(psum[:, i % 2, 0:SEQ], wq[:, k, i * P:i * P + P], xT[:, k, :], start=(k == 0), stop=(k == KC - 1))
            return last

        raw_in = [[sem(f"raw{l}_in{i}") for i in range(6)] for l in range(DEPTH)]
        gate_in = [[sem(f"gate{l}_in{i}") for i in range(2)] for l in range(DEPTH)]
        load_e = [expert_loads(l, raw_in[l]) for l in range(DEPTH)]

        def prefetch(l):
            def f(sp):
                for n, ring_set in ((0, 1), (1, 0)):
                    for i in range(3):
                        load_e[l](sp, n, n, 3 * ring_set + i)
            return f

        attention(
            "a_", 1, scale_a, xT, 2, a_project, a_first, a_loop, prefetch(0),
            bias_ready=lambda dve, j, b, half: dve.wait_ge(sel_used, 2 * j + 2),
            bias_of=lambda b, c: bias_sel[:, b, c, :],
            q_of=lambda b, c, g, a: q_a[:, b, c, a * P:a * P + P],
            k_of=lambda b, c, g, a: kT[:, 0:P * (a + 1)],
            v_of=lambda b, c, g, s: v_a[:, s, :],
            evac_piece=lambda act, b, i: act.activation(q_a[:, b, i, :], psum[:, i % 2, 0:SEQ], ACT.Copy),
            o_step=lambda OT, c: OT[:, c * SEQ:(c + 1) * SEQ],
            o_chunks=A_HEADS, wo_view=lambda u: wo_a[u], wo_units=A_HEADS // 2,
            ar=Arena("a2", mark), extra_pool=a_pool)

        def router_of(l):
            return (t["moe_w_router"][l].rearrange("(p k) e -> p k e", k=KC), t["moe_bias"][l])

        def ln_rows(l, i):
            return (t["ln_g"][l, i], t["ln_b"][l, i])

        def norm_arena(tag):
            a = Arena(tag)
            return a("xT", [P, KC, SEQ]), a

        xF, ar = norm_arena("n0")
        norm("n0_", ln_rows(0, 0), xF, ar, router=router_of(0), gates=gates_d[0])
        experts(0, load_e[0], raw_in[0], gate_in[0], gates_d[0])

        G = len(B_GROUPS)
        WB = KC * G * P
        rawB = raw[:, :, :].rearrange("p u n -> p (u n)")[:, 0:3 * WB].rearrange("p (s k g c) -> p s k g c", s=3, k=KC, g=G)
        wb_in = [sem(f"wb_in{i}") for i in range(3)]
        bias_b_in = [sem(f"bias_b_in{i}") for i in range(2)]

        def load_b(eng, j, i):
            eng.dma_start(rawB[:, i, :, :, :].rearrange("p k g c -> p (k g c)"), t["b_w_in_parts"][j, i]).then_inc(wb_in[i], 16)

        def first_b(sp):
            for i in range(3):
                load_b(sp, 0, i)

        xF, ar = norm_arena("n1")
        norm("n1_", ln_rows(0, 1), xF, ar, early_loads=first_b)

        xTb = xF
        ar = Arena("b", start=4 * KC * SEQ)
        qk = ar("qk", [P, 2, 2, G, SEQ])
        vb = ar("v", [P, 2, TC, G * P])
        bias_b = ar("bias", [P, 2, 2, G, LINE])

        def load_bias(sp, j, b):
            for c in range(2):
                for lo_, n_ in ((0, SEQ), (SEQ, P)):
                    src = bias_tile(1, G, j, n_)[:, :, c]
                    sp.dma_start(bias_b[:, b, c, :, lo_:lo_ + n_], src).then_inc(bias_b_in[b], 16)

        def b_first(sp, pr_done):
            for j in range(2):
                load_bias(sp, j, j)

        def b_loop(sp, pr_done, stt_done):
            def weights(j):
                for i in range(3):
                    sp.wait_ge(pr_done, 8 * j - 8 + (3, 6, 8)[i])
                    load_b(sp, j, i)
            weights(1)
            with sp.Fori(0, STEPS // 2 - 1) as it:
                for b in range(2):
                    j = 2 * it + 2 + b
                    weights(j)
                    sp.wait_ge(stt_done, 2 * j - 2)
                    load_bias(sp, j, b)

        def b_project(pe, j, b, half, i):
            if i in (0, 3, 6):
                pe.wait_ge(wb_in[i // 3], 16 * j + 16)
            for k in range(KC):
                if i < 6:
                    last = pe.matmul(psum[:, i % 2, 0:SEQ], rawB[:, i // 3, k, i % 3, :], xTb[:, k, :], start=(k == 0), stop=(k == KC - 1))
                else:
                    last = pe.matmul(psum[:, i % 2, 0:G * P], xTb[:, k, (i - 6) * P:(i - 5) * P],
                                     rawB[:, 2, k, :, :], start=(k == 0), stop=(k == KC - 1))
            return last

        def b_evac(act, b, i):
            if i < 6:
                return act.activation(qk[:, b, i // 3, i % 3, :], psum[:, i % 2, 0:SEQ], ACT.Copy)
            return act.activation(vb[:, b, i - 6, :], psum[:, i % 2, 0:G * P], ACT.Copy)

        wo_b = t["b_w_o"][0].rearrange("(u c p) n -> u p c n", c=2, p=P)
        attention(
            "b_", G, B_HD ** -0.5, xTb, 8, b_project, b_first, b_loop, prefetch(1),
            bias_ready=lambda dve, j, b, half: dve.wait_ge(bias_b_in[b], 64 * half + 64),
            bias_of=lambda b, c: bias_b[:, b, c, :, ::-1],
            q_of=lambda b, c, g, a: qk[c * B_HD:(c + 1) * B_HD, b, 0, g, a * P:a * P + P],
            k_of=lambda b, c, g, a: qk[c * B_HD:(c + 1) * B_HD, b, 1, g, 0:P * (a + 1)],
            v_of=lambda b, c, g, s: vb[:, b, s, g * P + c * B_HD:g * P + (c + 1) * B_HD],
            evac_piece=b_evac,
            o_step=lambda OT, c: OT[c * B_HD:(c + 1) * B_HD, 0:SEQ],
            o_chunks=B_HEADS // 2, wo_view=lambda u: wo_b[u], wo_units=B_HEADS // 4, ar=ar)

        xF, ar = norm_arena("n2")
        norm("n2_", ln_rows(1, 0), xF, ar, router=router_of(1), gates=gates_d[1])
        experts(1, load_e[1], raw_in[1], gate_in[1], gates_d[1])
        xF, ar = norm_arena("n3")
        norm("n3_", ln_rows(1, 1), xF, ar, final=True)


def t5_bucket(dist):
    exact = REL_BUCKETS // 2
    if dist < exact:
        return dist
    large = exact + int(math.log(dist / exact) / math.log(REL_MAX_DIST / exact) * (REL_BUCKETS - exact))
    return min(large, REL_BUCKETS - 1)


def bucket_table():
    hot = np.zeros((REL_BUCKETS + 1, 1 + len(B_GROUPS), LINE), np.float32)
    for g, (window, dil) in enumerate(((SEQ, 1),) + B_GROUPS):
        for m in range(LINE):
            dist = m - (P - 1)
            reach = SEQ if g == 0 else window // dil
            ok = dist >= 0 and dist % dil == 0 and dist // dil <= reach
            hot[t5_bucket(dist) if ok else REL_BUCKETS, g, m] = 1.0
    return hot


def kernel(**inputs):
    import concourse.bacc as bacc
    from concourse.bass_utils import run_bass_kernel_spmd

    a = {n: np.ascontiguousarray(inputs[n]) for n in
         ("x", "rel_bias", "a_w_o", "b_w_o", "ln_g", "ln_b", "moe_w_router", "moe_bias", "moe_w_gate", "moe_w_up",
          "moe_w_down", "moe_ws_gate", "moe_ws_up", "moe_ws_down")}

    def chunked(w):
        return np.ascontiguousarray(w.reshape(P, KC * w.shape[1]))

    a["x_T"] = np.ascontiguousarray(np.asarray(inputs["x"])[0].T.reshape(P, KC, SEQ))
    w = np.asarray(inputs["a_w_in"])[0]
    nq, nk = A_HEADS * A_HD, A_HEADS * A_HD + 2 * A_HD
    a["a_w_q"] = np.stack([chunked(w[:, j * 256:(j + 1) * 256]) for j in range(STEPS)])
    ni = IDX_HEADS * IDX_HD
    a["a_w_in_parts"] = np.stack([chunked(w[:, nk:nk + 256]), chunked(w[:, nk + 256:nk + 512]), chunked(w[:, nq:nk])])
    ki = w[:, nk + ni:nk + ni + IDX_HD]
    a["a_w_ki"] = chunked(np.concatenate([ki, ki, w[:, nk + ni + IDX_HD:]], axis=1))
    wb = np.asarray(inputs["b_w_in"])[0].reshape(P, KC, len(B_GROUPS), 3, STEPS, P)
    a["b_w_in_parts"] = np.ascontiguousarray(wb.transpose(4, 3, 0, 1, 2, 5)).reshape(STEPS, 3, P, -1)
    a["hot"] = bucket_table()
    a["ident"] = np.eye(P, dtype=np.float32)
    a["causal"] = np.where(np.arange(P)[None, :] <= np.arange(P)[:, None], 0.0, MASKED).astype(np.float32)
    earlier = (np.arange(N_GROUPS)[None, :] < np.arange(N_GROUPS)[:, None]).astype(np.float32)
    a["tri"] = np.ascontiguousarray(np.broadcast_to(earlier, (P, N_GROUPS, N_GROUPS)))

    upto = np.arange(P)
    a["before"] = np.stack([(upto[:, None] < upto[None, :]), np.ones((P, P), bool)], axis=1).astype(np.float32)
    a["slot_no"] = np.ascontiguousarray(np.broadcast_to(np.arange(SLOTS, dtype=np.float32), (P, SLOTS)))

    nc = bacc.Bacc("TRN2", target_bir_lowering=False, num_devices=1)
    t = {n: nc.dram_tensor(f"in_{n}", v.shape, mybir.dt.from_np(v.dtype), kind="ExternalInput").ap() for n, v in a.items()}
    out = nc.dram_tensor("out", (1, SEQ, D_MODEL), F32, kind="ExternalOutput").ap()
    build(nc, t, out)
    r = run_bass_kernel_spmd(nc, [{f"in_{n}": v for n, v in a.items()}], core_ids=[0])
    return r.results[0]["out"]
```

```python
import math
from contextlib import ExitStack

import numpy as np

import concourse.bass as bass
from concourse import mybir

F32 = mybir.dt.float32
F32R = mybir.dt.float32r
ALU = mybir.AluOpType
ACT = mybir.ActivationFunctionType
AX = mybir.AxisListType

D_MODEL, SEQ, DEPTH = 1024, 256, 2
P = 128
KC = D_MODEL // P
TC = SEQ // P
REL_BUCKETS, REL_MAX_DIST, REL_HEADS = 32, 2048, 16
A_HEADS, A_HD, IDX_HEADS, IDX_HD = 16, 128, 8, 64
TOPK_KEYS = min(256, SEQ // 4)
B_GROUPS = ((128, 1), (512, 4), (2048, 16))
B_HEADS, B_HD = 16, 64
N_EXPERTS, TOP_K, N_GROUPS, TOPK_GROUPS, D_EXPERT = 64, 8, 8, 4, 256
SLOTS = 64
GROUP = N_EXPERTS // N_GROUPS
ROUTED_SCALE = 2.5
NORM_EPS = 1e-5
DN_ALPHA = (2 * DEPTH) ** 0.25
MASKED = -1e30
TAKEN = -3e38
LINE = 3 * P
STEPS = A_HEADS // 2
UNIT = KC * D_EXPERT


def wait(eng, sem, value):
    if isinstance(value, int) and value <= 0:
        return
    eng.wait_ge(sem, value)


def build(nc, t, out):
    with ExitStack() as ctx:
        def sem(name):
            return ctx.enter_context(nc.semaphore(name))

        spent = []

        def phase_sems(scope, made):
            before = {s.num for s in spent}

            def f(name):
                s = scope.enter_context(nc.semaphore(name))
                assert s.num not in before
                made.append(s)
                return s
            return f

        def clear_spent(pool, old):
            for s in old:
                pool.sem_clear(s)

        def sb(name, shape, dt=F32):
            return ctx.enter_context(nc.sbuf_tensor(name, shape, dt))

        ident = sb("ident", [P, P])
        h = sb("h", [P, TC, D_MODEL])
        xT_at = nc.sbuf_base
        xTh = sb("xTh", [P, KC, SEQ], F32R)
        xTl = sb("xTl", [P, KC, SEQ], F32R)
        xh_at = nc.sbuf_base
        xh = sb("xh", [P, TC, D_MODEL], F32R)
        xl = sb("xl", [P, TC, D_MODEL], F32R)
        gate_of = sb("gate_of", [P, TC, N_EXPERTS])
        slot_of = sb("slot_of", [P, TC, N_EXPERTS])
        slot_no = sb("slot_no", [P, SLOTS])
        most_tokens = sb("most_tokens", [1, 1], mybir.dt.int32)
        raw_at = (nc.sbuf_base + 31) // 32 * 32
        raw = sb("raw", [P, 6, UNIT])
        raw_low = nc.alloc_sbuf_tensor_at("raw_low", [P, 6, UNIT], F32R, offset=raw_at)
        arena_at = nc.sbuf_base
        top = nc.sbuf_usable_end

        class Arena:
            def __init__(self, tag, start=0):
                self.tag, self.at = tag, arena_at + start

            def __call__(self, name, shape, dt=F32):
                size = 4 * int(np.prod(shape[1:]))
                x = nc.alloc_sbuf_tensor_at(f"{self.tag}_{name}", shape, dt, offset=self.at)
                self.at += (size + 31) // 32 * 32
                assert self.at <= top, (self.tag, name, self.at, top)
                return x

        psum = ctx.enter_context(nc.psum_tensor("psum", [P, 8, 512], F32))

        lines_d = nc.dram_tensor("bias_lines", [1 + len(B_GROUPS), REL_HEADS, LINE], F32, kind="Internal").ap()
        gates_d = [nc.dram_tensor(f"gates{l}", [N_EXPERTS, SEQ], F32, kind="Internal").ap() for l in range(DEPTH)]

        def bias_tile(table, nt, j, n):
            base = lines_d[table:table + nt, bass.ds(2 * j, 2) if not isinstance(j, int) else slice(2 * j, 2 * j + 2), :]
            return bass.AP(base.tensor, base.offset,
                           [[1, P], [REL_HEADS * LINE, nt], [LINE, 2], [1, n]])

        def attention(*args, **kw):
            made = []
            with ExitStack() as scope:
                attention_phase(phase_sems(scope, made), tuple(spent), *args, **kw)
            spent[:] = made

        def attention_phase(sem, old, tag, G, scale, pieces, project, load_first, load_loop, load_after, bias_ready, bias_of,
                      q_of, k_of, v_of, evac_piece, o_step, o_chunks, wo_view, wo_units, ar, far,
                      upper, lower, upper_at, lower_at, first_lowers, second_logits, w_hi_at, w_hi_size,
                      extra_pool=None, first_done=False):
            PP = pieces
            S = ar("scores", [P, 2, G, LINE])
            pT = ar("pT", [P, 3, LINE])
            smax = ar("smax", [P, 2, TC])
            nmax = ar("nmax", [P, 2, TC])
            ssum = ar("ssum", [P, 2, TC])
            sinv = ar("sinv", [P, 2, TC])
            oT_at = far.at
            oT = far("oT", [P, o_chunks, SEQ])
            wo_at = ar.at
            wo = ar("wo", [P, 4, 2, D_MODEL])
            prob = far("prob", [P, 2, G, LINE])
            oT_low = nc.alloc_sbuf_tensor_at(tag + "oT_low", [P, o_chunks, SEQ], F32R, offset=oT_at)
            oT_up = nc.alloc_sbuf_tensor_at(tag + "oT_up", [P, o_chunks, SEQ], F32R, offset=xT_at)
            wo_low = nc.alloc_sbuf_tensor_at(tag + "wo_low", [P, 4, 2, D_MODEL], F32R, offset=wo_at)
            wo_ring = min(4, w_hi_size // (8 * D_MODEL))
            wo_up = nc.alloc_sbuf_tensor_at(tag + "wo_up", [P, wo_ring, 2, D_MODEL], F32R, offset=w_hi_at)

            pr_done, pr_free = sem(tag + "proj_done"), sem(tag + "proj_free")
            qk_done, stt_done = sem(tag + "qk_done"), sem(tag + "logits_done")
            red_done, max_done = sem(tag + "red_done"), sem(tag + "max_done")
            ex_done, rc_done, nrm = sem(tag + "exp_done"), sem(tag + "recip_done"), sem(tag + "norm_done")
            tr_done, pt_ev, pv_done = sem(tag + "tr_done"), sem(tag + "pT_ready"), sem(tag + "pv_done")
            ot_ev, y_done = sem(tag + "oT_ready"), sem(tag + "y_done")
            wo_in = [sem(f"{tag}wo_in{i}") for i in range(4)]
            wo_used = sem(tag + "wo_used")
            wo_upper, wo_lower = sem(tag + "wo_upper"), sem(tag + "wo_lower")
            oT_upper, oT_lower = sem(tag + "oT_upper"), sem(tag + "oT_lower")
            pairs_per_unit = 2 * STEPS // o_chunks
            SL, ST, OT = psum[:, 2:5, :], psum[:, 5:7, :], psum[:, 7, :]

            def loop(eng, stage):
                stage(0, 0, 0)
                with eng.Fori(0, STEPS // 2 - 2) as it:
                    stage(2 * it + 1, 1, it)
                    stage(2 * it + 2, 0, it + 1)
                for j in range(STEPS - 3, STEPS):
                    stage(j, j % 2, j // 2)

            def split(eng, part, table, at, j, b, half):
                for ahead, i in table.get(at, ()):
                    if not (isinstance(j, int) and j + ahead >= STEPS):
                        part(eng, j + ahead, (b + ahead) % 2, half + (b + ahead) // 2, i)

            with nc.Block() as block:
                @block.sync
                def _(sp):
                    load_first(sp, pr_done)
                    for u in range(4):
                        sp.dma_start(wo[:, u, :, :], wo_view(u)).then_inc(wo_in[u], 16)
                    load_loop(sp, pr_done, stt_done)
                    sp.wait_ge(pr_done, PP * STEPS)
                    load_after(sp)
                    for u in range(4, wo_units):
                        sp.wait_ge(wo_used, u - 3)
                        sp.dma_start(wo[:, u % 4, :, :], wo_view(u)).then_inc(wo_in[u % 4], 16)

                @block.gpsimd
                def _(pool):
                    if extra_pool:
                        extra_pool(pool, stt_done)
                    clear_spent(pool, old)

                @block.tensor
                def _(pe):
                    def piece(j, b, half, i):
                        wait(pe, pr_free, PP * j + i - 1)
                        project(pe, j, b, half, i).then_inc(pr_done, 1)

                    def logits(j, b, c):
                        r = 2 * j + c
                        pe.wait_ge(pr_free, PP * j + PP)
                        wait(pe, stt_done, r - 1 if G == 1 else r)
                        for g in range(G):
                            bank = psum[:, 2 + (c if G == 1 else g), :]
                            for a in range(TC):
                                last = pe.matmul(bank[:, a * P:a * P + P * (a + 1)], q_of(b, c, g, a), k_of(b, c, g, a),
                                                 start=True, stop=True)
                        last.then_inc(qk_done, 1)

                    def trans(r, c, g):
                        w = G * r + g
                        if g == 0:
                            pe.wait_ge(nrm, 2 * r + 2)
                        wait(pe, pt_ev, w - 1)
                        for s in range(3):
                            last = pe.transpose(ST[:, (c * G + g) % 2, s * P:s * P + P], prob[:, c, g, s * P:s * P + P],
                                                ident[:, :])
                        last.then_inc(tr_done, 1)

                    def pv(r, j, b, c, g):
                        pe.wait_ge(pt_ev, G * r + g + 1)
                        if c == 0 and g == 0:
                            wait(pe, ot_ev, j)
                        o = o_step(OT, c)
                        slot = g if G > 1 else c
                        pe.matmul(o[:, 0:SEQ], v_of(b, c, g, 0), pT[:, slot, 0:2 * P], start=(g == 0), stop=False)
                        pe.matmul(o[:, P:SEQ], v_of(b, c, g, 1), pT[:, slot, 2 * P:3 * P], start=False,
                                  stop=(g == G - 1)).then_inc(pv_done, 1)

                    def stage(j, b, half):
                        more = not (isinstance(j, int) and j == STEPS - 1)
                        for c in range(2):
                            r = 2 * j + c
                            for i in range(c * PP // 2, (c + 1) * PP // 2):
                                if i == second_logits:
                                    logits(j, b, 1)
                                if more:
                                    piece(j + 1, 1 - b, half if b == 0 else half + 1, i)
                            trans(r, c, 0)
                            if c == 1 and more:
                                logits(j + 1, 1 - b, 0)
                            for g in range(1, G):
                                trans(r, c, g)
                                pv(r, j, b, c, g - 1)
                            pv(r, j, b, c, G - 1)

                    if first_done:
                        pe.sem_inc(pr_done, PP)
                    else:
                        for i in range(PP):
                            piece(0, 0, 0, i)
                    logits(0, 0, 0)
                    loop(pe, stage)
                    pe.wait_ge(ot_ev, STEPS)
                    for u in range(wo_units):
                        pe.wait_ge(oT_lower, u + 1)
                        pe.wait_ge(wo_lower, u + 1)
                        passes = ((oT_up, wo_up, u % wo_ring), (oT_low, wo_up, u % wo_ring), (oT_up, wo_low, u % 4))
                        for step, (x, w, slot) in enumerate(passes):
                            for cc in range(2):
                                for a in range(TC):
                                    for n in range(2):
                                        last = pe.matmul(psum[:, 2 * a + n, :], x[:, 2 * u + cc, a * P:a * P + P],
                                                         w[:, slot, cc, n * 512:n * 512 + 512],
                                                         start=(u == 0 and step == 0 and cc == 0),
                                                         stop=(u == wo_units - 1 and step == 2 and cc == 1))
                        last.then_inc(wo_used, 1)

                @block.scalar
                def _(act):
                    def evac(j, b, i):
                        act.wait_ge(pr_done, PP * j + i + 1)
                        evac_piece(act, b, i).then_inc(pr_free, 1)

                    def stage(j, b, half):
                        for c in range(2):
                            r = 2 * j + c
                            act.wait_ge(max_done, r + 1)
                            wait(act, tr_done, G * (r - 1))
                            for a in range(TC):
                                act.activation(prob[:, c, :, a * P:a * P + P * (a + 1)], S[:, c, :, a * P:a * P + P * (a + 1)],
                                               ACT.Exp, bias=nmax[:, c, a:a + 1],
                                               accum_out=ssum[:, c, a:a + 1]).then_inc(ex_done, 1)
                            if not (isinstance(j, int) and j == STEPS - 1):
                                if c == 0:
                                    wait(act, pv_done, 2 * G * j)
                                for i in range(c * PP // 2, (c + 1) * PP // 2):
                                    evac(j + 1, 1 - b, i)
                                    split(act, upper, upper_at, i, j, b, half)
                            for g in range(G):
                                w = G * r + g
                                act.wait_ge(tr_done, w + 1)
                                wait(act, pv_done, w - (2 if G > 1 else 1))
                                act.activation(pT[:, g if G > 1 else c, :], ST[:, (c * G + g) % 2, 0:LINE], ACT.Copy).then_inc(pt_ev, 1)
                            split(act, upper, upper_at, ("head", c), j, b, half)
                            if isinstance(j, int) and j == STEPS - 1 and c == 0:
                                out_upper(0)
                        act.wait_ge(pv_done, 2 * G * (j + 1))
                        o_evac(act, j)

                    def o_evac(act, j):
                        per = o_chunks // STEPS
                        act.activation(oT[:, bass.ds(per * j, per), :] if not isinstance(j, int) else oT[:, per * j:per * j + per, :],
                                       OT[:, 0:per * SEQ].rearrange("p (c t) -> p c t", c=per), ACT.Copy).then_inc(ot_ev, 1)

                    def out_upper(u):
                        act.wait_ge(wo_in[u % 4], 16 * (u // 4 + 1))
                        act.wait_ge(pr_done, PP * STEPS)
                        wait(act, wo_used, u - wo_ring + 1)
                        act.activation(wo_up[:, u % wo_ring, :, :], wo[:, u % 4, :, :], ACT.Copy).then_inc(wo_upper, 1)
                        act.wait_ge(ot_ev, pairs_per_unit * (u + 1))
                        act.activation(oT_up[:, 2 * u:2 * u + 2, :], oT[:, 2 * u:2 * u + 2, :], ACT.Copy).then_inc(oT_upper, 1)

                    if first_done:
                        act.sem_inc(pr_free, PP)
                    else:
                        for i in range(PP):
                            evac(0, 0, i)
                            if i == PP - 3:
                                upper(act, 1, 1, 0, 0)
                    loop(act, stage)
                    for u in range(1, wo_units):
                        out_upper(u)

                @block.vector
                def _(dve):
                    def stage(j, b, half):
                        for c in range(2):
                            r = 2 * j + c
                            if c == 0:
                                bias_ready(dve, j, b, half)
                            dve.wait_ge(qk_done, r + 1)
                            wait(dve, ex_done, 2 * (r - 1))
                            src = psum[:, 2 + c, 0:LINE] if G == 1 else SL[:, :, 0:LINE]
                            dst = S[:, c, 0, :] if G == 1 else S[:, c, :, :]
                            dve.scalar_tensor_tensor(out=dst, in0=src, scalar=scale, in1=bias_of(b, c), op0=ALU.mult,
                                                     op1=ALU.add).then_inc(stt_done, 1)
                            dve.wait_ge(stt_done, r + 1)
                            for a in range(TC):
                                dve.tensor_reduce(smax[:, c, a:a + 1], S[:, c, :, a * P:a * P + P * (a + 1)], AX.XY, ALU.max)\
                                   .then_inc(red_done, 1)
                            dve.wait_ge(red_done, 2 * r + 2)
                            dve.tensor_scalar(nmax[:, c, :], smax[:, c, :], -1.0, None, ALU.mult).then_inc(max_done, 1)
                            dve.wait_ge(ex_done, 2 * r + 2)
                            dve.reciprocal(sinv[:, c, :], ssum[:, c, :]).then_inc(rc_done, 1)
                            dve.wait_ge(rc_done, r + 1)
                            for a in range(TC):
                                dve.tensor_scalar(prob[:, c, :, a * P:a * P + P * (a + 1)], prob[:, c, :, a * P:a * P + P * (a + 1)],
                                                  sinv[:, c, a:a + 1], None, ALU.mult).then_inc(nrm, 1)
                            split(dve, lower, lower_at, c, j, b, half)
                    for part in first_lowers:
                        lower(dve, *part)
                    loop(dve, stage)
                    for u in range(wo_units):
                        dve.wait_ge(wo_upper, u + 1)
                        dve.tensor_tensor(wo_low[:, u % 4, :, :], wo[:, u % 4, :, :], wo_up[:, u % wo_ring, :, :].bitcast(F32),
                                          ALU.subtract).then_inc(wo_lower, 1)
                        dve.wait_ge(oT_upper, u + 1)
                        dve.tensor_tensor(oT_low[:, 2 * u:2 * u + 2, :], oT[:, 2 * u:2 * u + 2, :],
                                          oT_up[:, 2 * u:2 * u + 2, :].bitcast(F32), ALU.subtract).then_inc(oT_lower, 1)

        def norm(*args, **kw):
            made = []
            with ExitStack() as scope:
                norm_phase(phase_sems(scope, made), tuple(spent), *args, **kw)
            spent[:] = made

        def norm_phase(sem, old, tag, which, xT_full, ar, early_loads=None, router=None, gates=None, final=False,
                       act_first=None, act_second=None, pool_work=None, pe_work=None):
            gb = ar("ln_gb", [P, 2, D_MODEL])
            stats = ar("stats", [P, TC, 2, 6])
            mv = ar("mv", [P, TC, 2])
            rstd = ar("rstd", [P, TC])
            ln_in = sem(tag + "ln_in")
            res_done, st_done, ag_done = sem(tag + "res"), sem(tag + "stats"), sem(tag + "mean_var")
            eps_done, sq_done, rs_done = sem(tag + "eps"), sem(tag + "sqrt"), sem(tag + "rstd")
            cn_done, g_done, ln_done = sem(tag + "centered"), sem(tag + "gained"), sem(tag + "ln_done")
            tr_done, xf_done, xh_done, xl_done = sem(tag + "tr"), sem(tag + "xf"), sem(tag + "xh"), sem(tag + "xl")
            out_done = sem(tag + "out")
            if router is not None:
                wr = ar("wr", [P, KC, N_EXPERTS])
                eb = ar("eb", [P, N_EXPERTS])
                tri = ar("tri", [P, N_GROUPS, N_GROUPS])
                sc, ch, mk, gt = (ar(n, [P, TC, N_EXPERTS]) for n in ("score", "choice", "chosen", "gate"))
                before = ar("before", [P, 2, P])
                most = ar("most", [1, 1])
                m8 = ar("m8", [P, TC, N_GROUPS, 8])
                gs = ar("gs", [P, TC, N_GROUPS])
                gtm = ar("gtm", [P, TC, N_GROUPS, N_GROUPS])
                eqm = ar("eqm", [P, TC, N_GROUPS, N_GROUPS])
                rank = ar("rank", [P, TC, N_GROUPS])
                pen = ar("pen", [P, TC, N_GROUPS])
                top8 = ar("top8", [P, TC, 8])
                gsum = ar("gsum", [P, TC])
                ginv = ar("ginv", [P, TC])
                gT = ar("gT", [N_EXPERTS, SEQ])
                r_in, lg_done, re_done, rc = sem(tag + "router_in"), sem(tag + "router"), sem(tag + "router_exp"), sem(tag + "route")
                gt_done, ge_done, gd_done = sem(tag + "gates_T"), sem(tag + "gates_ev"), sem(tag + "gates_dram")
                xrh, xrl, sl_mm = sem(tag + "rows_hi"), sem(tag + "rows_lo"), sem(tag + "slots_mm")
                w_router, bias_row = router
                slot_banks = (3, 7)

            with nc.Block() as block:
                @block.sync
                def _(sp):
                    g_row, b_row = which
                    sp.dma_start(gb[:, 0, :], g_row.partition_broadcast(P)).then_inc(ln_in, 16)
                    sp.dma_start(gb[:, 1, :], b_row.partition_broadcast(P)).then_inc(ln_in, 16)
                    if router is not None:
                        sp.dma_start(wr[:, :, :], w_router).then_inc(r_in, 16)
                        sp.dma_start(eb[:, :], bias_row.partition_broadcast(P)).then_inc(r_in, 16)
                        sp.dma_start(tri[:, :, :], t["tri"]).then_inc(r_in, 16)
                        sp.dma_start(before[:, :, :], t["before"]).then_inc(r_in, 16)
                        sp.dma_start(slot_no[:, :], t["slot_no"]).then_inc(r_in, 16)
                    if early_loads:
                        early_loads(sp)
                    if router is not None:
                        sp.wait_ge(ge_done, 1)
                        sp.dma_start(gates, gT[:, :]).then_inc(gd_done, 16)
                        sp.wait_ge(gd_done, 16)
                    if final:
                        for a in range(TC):
                            sp.wait_ge(ln_done, a + 1)
                            sp.dma_start(out[0, a * P:(a + 1) * P, :], h[:, a, :]).then_inc(out_done, 16)
                        sp.wait_ge(out_done, 16 * TC)

                @block.gpsimd
                def _(pool):
                    if pool_work:
                        pool_work(pool)
                    clear_spent(pool, old)

                @block.vector
                def _(dve):
                    for a in range(TC):
                        for n in range(2):
                            dve.scalar_tensor_tensor(out=h[:, a, n * 512:n * 512 + 512], in0=h[:, a, n * 512:n * 512 + 512],
                                                     scalar=DN_ALPHA, in1=psum[:, 2 * a + n, :], op0=ALU.mult,
                                                     op1=ALU.add).then_inc(res_done, 1)
                    for a in range(TC):
                        for n in range(2):
                            dve.wait_ge(res_done, 2 * a + n + 1)
                            dve.bn_stats(stats[:, a, n, :], h[:, a, n * 512:n * 512 + 512]).then_inc(st_done, 1)
                    for a in range(TC):
                        dve.wait_ge(st_done, 2 * a + 2)
                        dve.bn_aggr(mv[:, a, :], stats[:, a, :, :]).then_inc(ag_done, 1)
                    dve.wait_ge(ag_done, TC)
                    dve.tensor_scalar(rstd[:, :], mv[:, :, 1], NORM_EPS, None, ALU.add).then_inc(eps_done, 1)
                    dve.wait_ge(sq_done, 1)
                    dve.reciprocal(rstd[:, :], rstd[:, :]).then_inc(rs_done, 1)
                    dve.wait_ge(rs_done, 1)
                    for a in range(TC):
                        dve.tensor_scalar(h[:, a, :], h[:, a, :], mv[:, a, 0:1], rstd[:, a:a + 1], ALU.subtract, ALU.mult)\
                           .then_inc(cn_done, 1)
                    dve.wait_ge(ln_in, 32)
                    for a in range(TC):
                        dve.wait_ge(cn_done, a + 1)
                        dve.tensor_tensor(h[:, a, :], h[:, a, :], gb[:, 0, :], ALU.mult).then_inc(g_done, 1)
                        dve.wait_ge(g_done, a + 1)
                        dve.tensor_tensor(h[:, a, :], h[:, a, :], gb[:, 1, :], ALU.add).then_inc(ln_done, 1)
                    if final:
                        return
                    for i in range(2 * TC):
                        a, q = divmod(i, 2)
                        dve.wait_ge(xh_done, i + 1)
                        dve.tensor_tensor(xTl[:, 4 * q:4 * q + 4, a * P:a * P + P], xT_full[:, 4 * q:4 * q + 4, a * P:a * P + P],
                                          xTh[:, 4 * q:4 * q + 4, a * P:a * P + P].bitcast(F32), ALU.subtract).then_inc(xl_done, 1)
                    if router is None:
                        return
                    count = [0]

                    def link(ins):
                        count[0] += 1
                        ins.then_inc(rc, 1)
                        dve.wait_ge(rc, count[0])

                    for a in range(TC):
                        dve.wait_ge(xrh, a + 1)
                        dve.tensor_tensor(xl[:, a, :], h[:, a, :], xh[:, a, :].bitcast(F32), ALU.subtract).then_inc(xrl, 1)
                    dve.wait_ge(r_in, 80)
                    dve.wait_ge(re_done, TC)
                    link(dve.tensor_scalar(sc[:, :, :], sc[:, :, :], 1.0, None, ALU.add))
                    link(dve.reciprocal(sc[:, :, :], sc[:, :, :]))
                    link(dve.tensor_tensor(ch[:, :, :], sc[:, :, :], eb[:, :].unsqueeze(1).broadcast_to([P, TC, N_EXPERTS]), ALU.add))
                    for a in range(TC):
                        for g in range(N_GROUPS):
                            ins = dve.max(m8[:, a, g, :], ch[:, a, g * GROUP:(g + 1) * GROUP])
                            if (a, g) != (TC - 1, N_GROUPS - 1):
                                count[0] += 1
                                ins.then_inc(rc, 1)
                    link(ins)
                    link(dve.tensor_tensor(gs[:, :, :], m8[:, :, :, 0], m8[:, :, :, 1], ALU.add))
                    every = [P, TC, N_GROUPS, N_GROUPS]
                    mine = gs[:, :, :].unsqueeze(3).broadcast_to(every)
                    others = gs[:, :, :].unsqueeze(2).broadcast_to(every)
                    link(dve.tensor_tensor(gtm[:, :, :, :], others, mine, ALU.is_gt))
                    link(dve.tensor_tensor(eqm[:, :, :, :], others, mine, ALU.is_equal))
                    link(dve.tensor_tensor(eqm[:, :, :, :], eqm[:, :, :, :], tri[:, :, :].unsqueeze(1).broadcast_to(every), ALU.mult))
                    link(dve.tensor_tensor(gtm[:, :, :, :], gtm[:, :, :, :], eqm[:, :, :, :], ALU.add))
                    link(dve.tensor_reduce(rank[:, :, :], gtm[:, :, :, :], AX.X, ALU.add))
                    link(dve.tensor_scalar(rank[:, :, :], rank[:, :, :], float(TOPK_GROUPS), None, ALU.is_lt))
                    link(dve.tensor_scalar(pen[:, :, :], rank[:, :, :], -MASKED, MASKED, ALU.mult, ALU.add))
                    chv = ch[:, :, :].rearrange("p a (g e) -> p (a g) e", g=N_GROUPS)
                    for per_group, op in ((rank, ALU.mult), (pen, ALU.add)):
                        link(dve.tensor_tensor(chv, chv, per_group[:, :, :].rearrange("p a g -> p (a g)").unsqueeze(2)
                                               .broadcast_to([P, TC * N_GROUPS, GROUP]), op))
                    for a in range(TC):
                        link(dve.max(top8[:, a, :], ch[:, a, :]))
                        link(dve.match_replace(mk[:, a, :], top8[:, a, :], ch[:, a, :], TAKEN))
                    link(dve.tensor_scalar(mk[:, :, :], mk[:, :, :], TAKEN, None, ALU.is_equal))
                    link(dve.tensor_tensor(gt[:, :, :], sc[:, :, :], mk[:, :, :], ALU.mult))
                    link(dve.tensor_reduce(gsum[:, :], gt[:, :, :], AX.X, ALU.add))
                    link(dve.reciprocal(ginv[:, :], gsum[:, :]))
                    for a in range(TC):
                        dve.tensor_scalar(gate_of[:, a, :], gt[:, a, :], ginv[:, a:a + 1], ROUTED_SCALE, ALU.mult, ALU.mult)\
                           .then_inc(gt_done, 1)
                    dve.wait_ge(sl_mm, 3)
                    for a in range(TC):
                        link(dve.scalar_tensor_tensor(out=slot_of[:, a, :], in0=psum[:, slot_banks[a], 0:N_EXPERTS], scalar=1.0,
                                                      in1=mk[:, a, :], op0=ALU.add, op1=ALU.mult))
                        link(dve.tensor_scalar(slot_of[:, a, :], slot_of[:, a, :], -1.0, None, ALU.add))
                    link(dve.tensor_reduce(most[:, :], psum[0:1, 6, 0:N_EXPERTS], AX.X, ALU.max))
                    dve.tensor_copy(most_tokens[:, :], most[:, :])

                @block.scalar
                def _(act):
                    if act_first:
                        act_first(act)
                    act.wait_ge(eps_done, 1)
                    act.activation(rstd[:, :], rstd[:, :], ACT.Sqrt).then_inc(sq_done, 1)
                    if act_second:
                        act_second(act)
                    if final:
                        return
                    for i in range(2 * TC):
                        a, q = divmod(i, 2)
                        act.wait_ge(tr_done, i + 1)
                        v = psum[:, 4 + i, :].rearrange("p (k t) -> p k t", k=4)
                        act.activation(xT_full[:, 4 * q:4 * q + 4, a * P:a * P + P], v, ACT.Copy).then_inc(xf_done, 1)
                        act.activation(xTh[:, 4 * q:4 * q + 4, a * P:a * P + P], v, ACT.Copy).then_inc(xh_done, 1)
                    if router is None:
                        return
                    for a in range(TC):
                        act.activation(xh[:, a, :], h[:, a, :], ACT.Copy).then_inc(xrh, 1)
                    for a in range(TC):
                        act.wait_ge(lg_done, a + 1)
                        act.activation(sc[:, a, :], psum[:, a, 0:N_EXPERTS], ACT.Exp, scale=-1.0).then_inc(re_done, 1)
                    act.wait_ge(gt_done, TC + 1)
                    act.activation(gT[:, :], psum[0:N_EXPERTS, 2, 0:SEQ], ACT.Copy).then_inc(ge_done, 1)

                @block.tensor
                def _(pe):
                    if final:
                        return
                    for i in range(2 * TC):
                        a, q = divmod(i, 2)
                        pe.wait_ge(ln_done, a + 1)
                        for k in range(4):
                            last = pe.transpose(psum[:, 4 + i, k * P:k * P + P], h[:, a, 4 * q + k::KC], ident[:, :])
                        last.then_inc(tr_done, 1)
                    if router is None:
                        return
                    pe.wait_ge(r_in, 80)
                    for a in range(TC):
                        pe.wait_ge(xf_done, 2 * a + 2)
                        for k in range(KC):
                            last = pe.matmul(psum[:, a, 0:N_EXPERTS], xT_full[:, k, a * P:a * P + P], wr[:, k, :],
                                             start=(k == 0), stop=(k == KC - 1))
                        last.then_inc(lg_done, 1)
                    pe.wait_ge(xl_done, 2 * TC)
                    if pe_work:
                        pe_work(pe)
                    for a in range(TC):
                        pe.wait_ge(gt_done, a + 1)
                        last = pe.transpose(psum[0:N_EXPERTS, 2, a * P:a * P + P], gate_of[:, a, :], ident[:, :])
                    last.then_inc(gt_done, 1)
                    first, second = (psum[:, bank, 0:N_EXPERTS] for bank in slot_banks)
                    pe.matmul(first, before[:, 0, :], mk[:, 0, :], start=True, stop=True).then_inc(sl_mm, 1)
                    pe.matmul(second, before[:, 1, :], mk[:, 0, :], start=True, stop=False)
                    pe.matmul(second, before[:, 0, :], mk[:, 1, :], start=False, stop=True).then_inc(sl_mm, 1)
                    for a in range(TC):
                        last = pe.matmul(psum[0:1, 6, 0:N_EXPERTS], before[:, 1, 0:1], mk[:, a, :], start=(a == 0),
                                         stop=(a == TC - 1))
                    last.then_inc(sl_mm, 1)

        def expert_loads(l, raw_in):
            def views(n):
                if isinstance(n, int) and n == 0:
                    w = (t["moe_ws_gate"][l], t["moe_ws_up"][l], t["moe_ws_down"][l])
                else:
                    w = tuple(t[x][l, n - 1] for x in ("moe_w_gate", "moe_w_up", "moe_w_down"))
                return [w[0].rearrange("(p k) f -> p (k f)", k=KC), w[1].rearrange("(p k) f -> p (k f)", k=KC),
                        w[2].rearrange("(p j) d -> p (j d)", j=2)]

            def load(eng, n, b, u):
                eng.dma_start(raw[:, u, :], views(n)[u % 3]).then_inc(raw_in[u], 16)
            return load

        w_ar = Arena("w")
        hi = w_ar("hi", [P, 6, UNIT], F32R)
        lo = w_ar("lo", [P, 6, UNIT], F32R)
        behind_weights = w_ar.at - arena_at

        class SharedSplit:
            def __init__(self, l, load, raw_in):
                self.l, self.load, self.raw_in = l, load, raw_in
                self.up, self.low = sem(f"shared{l}_up"), sem(f"shared{l}_low")

            def upper(self, act, units):
                for i in units:
                    act.wait_ge(self.raw_in[3 + i], 16)
                    act.activation(hi[:, 3 + i, :], raw[:, 3 + i, :], ACT.Copy).then_inc(self.up, 1)

            def lower(self, pool):
                for i in range(3):
                    pool.wait_ge(self.up, i + 1)
                    pool.tensor_tensor(lo[:, 3 + i, :], raw[:, 3 + i, :], hi[:, 3 + i, :].bitcast(F32), ALU.subtract)\
                        .then_inc(self.low, 1)

            def next_loads(self, sp):
                for i in range(3):
                    sp.wait_ge(self.low, i + 1)
                    self.load(sp, 2, 0, 3 + i)

            def gate_up(self, pe):
                for i in range(2):
                    pe.wait_ge(self.low, i + 1)
                    for j in range(2):
                        for step, (w, x) in enumerate(((hi, xTh), (hi, xTl), (lo, xTh))):
                            for k in range(KC):
                                pe.matmul(psum[:, 4 + i, j * SEQ:(j + 1) * SEQ], w[:, 3 + i, k * D_EXPERT + j:(k + 1) * D_EXPERT:2],
                                          x[:, k, :], start=(step == 0 and k == 0), stop=(step == 2 and k == KC - 1))

            def hooks(self):
                return dict(pe_work=self.gate_up, act_first=lambda act: self.upper(act, range(2)), act_second=lambda act: self.upper(act, (2,)),
                            pool_work=self.lower, early_loads=self.next_loads)

        def experts(*args, **kw):
            made = []
            with ExitStack() as scope:
                experts_phase(phase_sems(scope, made), tuple(spent), *args, **kw)
            spent[:] = made

        def experts_phase(sem, old, l, load, raw_in, gate_in, gates, load_after=None):
            tag = f"m{l}_"
            rest = behind_weights
            ar = Arena(tag, start=rest)
            E = ar("sig", [P, 2, 512])
            S = ar("act", [P, 512])
            H = ar("hid", [P, 512])
            gate_rows = ar("gate_rows", [P, 2, SEQ])
            Hh = ar("hid_hi", [P, 2, 2, SEQ], F32R)
            Hl = ar("hid_lo", [P, 2, 2, SEQ], F32R)
            N = N_EXPERTS + 1
            hi_done = [sem(f"{tag}hi{i}") for i in range(3)]
            lo_done = [sem(f"{tag}lo{i}") for i in range(3)]
            mm_done = [sem(tag + "gate_done"), sem(tag + "up_done"), sem(tag + "down_done")]
            silu_done, act_done, hid_done = sem(tag + "silu"), sem(tag + "act"), sem(tag + "hidden")
            hh_done, hl_done = sem(tag + "hid_hi"), sem(tag + "hid_lo")

            class Dense:

                @staticmethod
                def upper(act, n, b, half, i):
                    act.wait_ge(raw_in[3 * (1 - b) + i], 16 * half + 16)
                    wait(act, mm_done[i], n - 1)
                    act.activation(hi[:, 3 * (1 - b) + i, :], raw[:, 3 * (1 - b) + i, :], ACT.Copy).then_inc(hi_done[i], 1)

                @staticmethod
                def lower(dve, n, b, half, i):
                    dve.wait_ge(hi_done[i], n + 1)
                    wait(dve, mm_done[i], n - 1)
                    u = 3 * (1 - b) + i
                    dve.tensor_tensor(lo[:, u, :], raw[:, u, :], hi[:, u, :].bitcast(F32), ALU.subtract).then_inc(lo_done[i], 1)

                @staticmethod
                def act_stage(act, n, b, half, more):
                    nxt = (n + 1, 1 - b, half + b)
                    if more:
                        Dense.upper(act, *nxt, 0)
                        Dense.upper(act, *nxt, 1)
                    act.wait_ge(mm_done[0], n + 1)
                    wait(act, act_done, n - 1)
                    act.activation(E[:, b, :], psum[:, 4 + 2 * b, :], ACT.Silu).then_inc(silu_done, 1)
                    if more:
                        Dense.upper(act, *nxt, 2)
                    act.wait_ge(hid_done, n + 1)
                    wait(act, mm_done[2], n - 1)
                    act.activation(Hh[:, b, :, :].rearrange("p j t -> p (j t)"), H[:, :], ACT.Copy).then_inc(hh_done, 1)

                @staticmethod
                def dve_stage(dve, n, b, half, more):
                    nxt = (n + 1, 1 - b, half + b)
                    if more:
                        Dense.lower(dve, *nxt, 0)
                        Dense.lower(dve, *nxt, 1)
                    dve.wait_ge(silu_done, n + 1)
                    dve.wait_ge(mm_done[1], n + 1)
                    wait(dve, hid_done, n)
                    dve.tensor_tensor(S[:, :], E[:, b, :], psum[:, 5 + 2 * b, :], ALU.mult).then_inc(act_done, 1)
                    dve.wait_ge(act_done, n + 1)
                    wait(dve, hl_done, n)
                    if isinstance(n, int) and n == 0:
                        dve.tensor_copy(H[:, :], S[:, :]).then_inc(hid_done, 1)
                    else:
                        dve.wait_ge(gate_in[b], 16 * half + 16 * b)
                        dve.tensor_tensor(H[:, :].rearrange("p (j t) -> p j t", j=2), S[:, :].rearrange("p (j t) -> p j t", j=2),
                                          gate_rows[:, b, :].unsqueeze(1).broadcast_to([P, 2, SEQ]), ALU.mult)\
                           .then_inc(hid_done, 1)
                    if more:
                        Dense.lower(dve, *nxt, 2)
                    dve.wait_ge(hh_done, n + 1)
                    wait(dve, mm_done[2], n - 1)
                    dve.tensor_tensor(Hl[:, b, :, :].rearrange("p j t -> p (j t)"), H[:, :],
                                      Hh[:, b, :, :].rearrange("p j t -> p (j t)").bitcast(F32), ALU.subtract).then_inc(hl_done, 1)

                @staticmethod
                def gate_up(pe, n, b):
                    wait(pe, act_done, n - 1)
                    for i in range(2):
                        pe.wait_ge(hi_done[i], n + 1)
                        for j in range(2):
                            for step, (w, x) in enumerate(((hi, xTh), (hi, xTl), (lo, xTh))):
                                if j == 0 and step == 2:
                                    pe.wait_ge(lo_done[i], n + 1)
                                for k in range(KC):
                                    wk = w[:, 3 * (1 - b) + i, k * D_EXPERT + j:(k + 1) * D_EXPERT:2]
                                    last = pe.matmul(psum[:, 4 + 2 * b + i, j * SEQ:(j + 1) * SEQ], wk, x[:, k, :],
                                                     start=(step == 0 and k == 0), stop=(step == 2 and k == KC - 1))
                        last.then_inc(mm_done[i], 1)

                @staticmethod
                def down(pe, n, b):
                    first = isinstance(n, int) and n == 0
                    final = isinstance(n, int) and n == N - 1
                    for ready in (hi_done[2], lo_done[2], hh_done, hl_done):
                        pe.wait_ge(ready, n + 1)
                    for step, (x, w) in enumerate(((Hh, hi), (Hh, lo), (Hl, hi))):
                        for j in range(2):
                            for a in range(TC):
                                for m in range(2):
                                    last = pe.matmul(psum[:, 2 * a + m, :], x[:, b, j, a * P:a * P + P],
                                                     w[:, 3 * (1 - b) + 2, j * D_MODEL + m * 512:j * D_MODEL + m * 512 + 512],
                                                     start=(first and step == 0 and j == 0),
                                                     stop=(final and step == 2 and j == 1), skip_group_check=True)
                    last.then_inc(mm_done[2], 1)

                @staticmethod
                def loop(eng, stage):
                    stage(1, 1, 0, True)
                    with eng.Fori(0, N_EXPERTS // 2 - 1) as it:
                        stage(2 * it + 2, 0, it + 1, True)
                        stage(2 * it + 3, 1, it + 1, True)
                    stage(N - 1, 0, (N - 1) // 2, False)

            ov = Arena(tag + "x", start=xT_at - arena_at)
            X = ov("X", [P, 4, KC, P], F32R)
            ar = Arena(tag + "s", start=rest)
            yh = ar("y_hi", [P, 2, 512], F32R)
            yl = ar("y_lo", [P, 2, 512], F32R)
            pickT = ar("pickT", [P, 2, SEQ], F32R)
            hidh = ar("s_hid_hi", [P, 2, 2, P], F32R)
            hidl = ar("s_hid_lo", [P, 2, 2, P], F32R)
            part = ar("part", [P, 512])
            gu = ar("gate_up", [P, 512])
            pick = ar("pick", [P, TC, 2 * P], F32R)
            av = ar("s_act", [P, D_EXPERT])
            gsl = ar("slot_gate", [P, 2])
            gq = ar("pair_gates", [P, TC, 4])
            gu_hi = [sem(f"{tag}gu_hi{x}") for x in "AB"]
            whi = [sem(f"{tag}whi{u}") for u in range(6)]
            wlo = [sem(f"{tag}wlo{u}") for u in range(6)]
            gu_mm = [sem(f"{tag}gu_mm{x}") for x in "AB"]
            part_done = [sem(f"{tag}part{x}") for x in "AB"]
            sum_done = [sem(f"{tag}sum{x}") for x in "AB"]
            names = ("zeroed pick gather xhi xlo ptmm pt gsl gates silu sact htmm hhi hlo ymm yhi ylo comb").split()
            sm = {n: sem(f"{tag}s_{n}") for n in names}
            NP = N_EXPERTS // 2
            R0, R1 = psum[:, 6, :], psum[:, 7, :]
            CAB = [psum[:, 4, :], psum[:, 5, :]]

            def X_upper(r):
                return X[:, :, 2 * r:2 * r + 2, 0:SLOTS].rearrange("p c k s -> p k c s")

            def X_lower(r):
                return X[:, :, 2 * r:2 * r + 2, SLOTS:P].rearrange("p c k s -> p k c s")

            def gathered(r):
                return psum[:, 6 + r % 2, :].rearrange("p (k c s) -> p k c s", k=2, c=4)

            def hid_slots(tensor):
                v = tensor[:, :, :, :]
                return bass.AP(v.tensor, v.offset, [list(v.ap[0]), [P, 2], [2 * P + SLOTS, 2], [1, SLOTS]])

            def run_pairs(eng, stage):
                stage(0, 0, 0, True)
                stage(1, 1, 0, True)
                with eng.Fori(1, NP // 2 - 1) as it:
                    stage(2 * it, 0, it, True)
                    stage(2 * it + 1, 1, it, True)
                stage(NP - 2, 0, NP // 2 - 1, True)
                stage(NP - 1, 1, NP // 2 - 1, False)

            def by_load(eng, sparse, dense):
                most = eng.value_load(most_tokens[0:1, 0:1], min_val=0, max_val=SEQ)
                with eng.If(most <= SLOTS):
                    sparse()
                with eng.Else():
                    dense()

            with nc.Block() as block:
                @block.sync
                def _(sp):
                    def sparse():
                        def slot(p, u):
                            sp.wait_ge(wlo[u], p)
                            load(sp, 2 * p + 1 + u // 3, 0, u)
                        for p, u in ((1, 0), (1, 1), (1, 2), (1, 3), (1, 4), (2, 0), (2, 1), (2, 3), (1, 5), (2, 4), (3, 0), (3, 1)):
                            slot(p, u)
                        order = ((2, 3), (1, 5), (2, 4), (1, 2), (3, 0), (3, 1))
                        with sp.Fori(1, NP - 3) as p:
                            for ahead, u in order:
                                slot(p + ahead, u)
                        for p in (NP - 3, NP - 2):
                            for ahead, u in order:
                                if p + ahead < NP:
                                    slot(p + ahead, u)
                        if load_after:
                            load_after(sp, [(wlo[u], NP) for u in range(6)])

                    def dense():
                        def units(n, b):
                            for i in range(3):
                                sp.wait_ge(lo_done[i], n - 1)
                                load(sp, n, b, 3 * (1 - b) + i)
                        with sp.Fori(0, N_EXPERTS // 2 - 1) as it:
                            units(2 * it + 3, 1)
                            units(2 * it + 4, 0)
                        if load_after:
                            load_after(sp, [(lo_done[i % 3], N) for i in range(6)])
                    by_load(sp, sparse, dense)

                @block.gpsimd
                def _(pool):
                    clear_spent(pool, old)

                    def sparse():
                        pool.wait_ge(mm_done[2], 1)
                        pool.memset(hidh[:, :, :, :].rearrange("p a j s -> p (a j s)").bitcast(F32), 0.0).then_inc(sm["zeroed"], 1)
                        pool.memset(hidl[:, :, :, :].rearrange("p a j s -> p (a j s)").bitcast(F32), 0.0).then_inc(sm["zeroed"], 1)

                        with pool.Fori(0, NP) as p:
                            pool.wait_ge(whi[5], p + 1)
                            pool.tensor_tensor(lo[:, 5, :], raw[:, 5, :], hi[:, 5, :].bitcast(F32), ALU.subtract).then_inc(wlo[5], 1)

                    def dense():
                        def row(n, b):
                            pool.dma_start(gate_rows[:, b, :], gates[n - 1, :].partition_broadcast(P)).then_inc(gate_in[b], 16)
                        row(1, 1)
                        row(2, 0)
                        with pool.Fori(0, N_EXPERTS // 2 - 1) as it:
                            pool.wait_ge(hid_done, 2 * it + 2)
                            row(2 * it + 3, 1)
                            pool.wait_ge(hid_done, 2 * it + 3)
                            row(2 * it + 4, 0)
                    by_load(pool, sparse, dense)

                @block.scalar
                def _(act):
                    for i in range(3):
                        act.sem_inc(hi_done[i], 1)

                    def sparse():
                        def upper(p, u):
                            act.wait_ge(raw_in[u], 16 * p + (16 if u < 3 else 32))
                            if isinstance(p, int) and p == 0:
                                if u >= 3:
                                    act.wait_ge(mm_done[u - 3], 1)
                            else:
                                act.wait_ge(gu_hi[u // 3] if u % 3 < 2 else sm["ymm"], p if u % 3 < 2 else 2 * p)
                            act.activation(hi[:, u, :], raw[:, u, :], ACT.Copy).then_inc(whi[u], 1)

                        def slots_in(q, rounds=range(4)):
                            wait(act, gu_mm[1], 2 * q)
                            for r in rounds:
                                act.wait_ge(sm["gather"], 4 * q + r + 1)
                                act.activation(X_upper(r), gathered(r), ACT.Copy).then_inc(sm["xhi"], 1)

                        def picks(p, b):
                            act.wait_ge(sm["ptmm"], p + 1)
                            wait(act, sm["comb"], p - 1)
                            act.activation(pickT[:, b, :], R0[:, 0:SEQ], ACT.Copy).then_inc(sm["pt"], 1)
                            for x in range(2):
                                q = slice(x * SLOTS, (x + 1) * SLOTS)
                                act.activation(gsl[q, b:b + 1], psum[q, 6, SEQ + x:SEQ + x + 1], ACT.Copy).then_inc(sm["gsl"], 1)

                        def partial(p, x):
                            act.wait_ge(gu_mm[x], p + 1)
                            wait(act, sum_done[x], p)
                            dst, src = slice(x * SLOTS, (x + 1) * SLOTS), slice((1 - x) * SLOTS, (2 - x) * SLOTS)
                            act.activation(part[dst, :], psum[src, 4 + x, :], ACT.Copy).then_inc(part_done[x], 1)

                        Dense.act_stage(act, 0, 0, 0, False)
                        act.wait_ge(mm_done[1], 1)
                        slots_in(0, range(2))
                        for u in range(3):
                            upper(0, u)
                        slots_in(0, range(2, 4))
                        upper(0, 3)
                        upper(0, 4)
                        act.wait_ge(mm_done[2], 1)
                        picks(0, 0)
                        partial(0, 0)
                        upper(1, 0)
                        upper(1, 1)
                        upper(1, 3)

                        def stage(p, b, half, more):
                            two_more = more and not (isinstance(p, int) and p == NP - 2)
                            partial(p, 1)
                            if b == 0 or (isinstance(p, int) and p == NP - 1):
                                upper(p, 5)
                            act.wait_ge(sum_done[1], p + 1)
                            wait(act, sm["htmm"], p)
                            act.activation(av[:, :], gu[:, 0:D_EXPERT], ACT.Silu).then_inc(sm["silu"], 1)
                            if more:
                                picks(p + 1, 1 - b)
                                upper(p + 1, 4)
                            if not (isinstance(p, int) and p == 0):
                                upper(p, 2)
                            act.wait_ge(sm["htmm"], p + 1)
                            if isinstance(p, int) and p == 0:
                                act.wait_ge(sm["zeroed"], 2)
                            wait(act, sm["ymm"], 2 * p)
                            act.activation(hid_slots(hidh), R1[:, 0:SEQ].rearrange("p (j x s) -> p j x s", j=2, x=2),
                                           ACT.Copy).then_inc(sm["hhi"], 1)
                            if more:
                                partial(p + 1, 0)
                            if two_more:
                                upper(p + 2, 0)
                                upper(p + 2, 1)
                            for m in range(2):
                                act.wait_ge(sm["ymm"], 2 * p + m + 1)
                                wait(act, sm["comb"], p)
                                act.activation(yh[:, m, :], psum[:, 6 + m, :], ACT.Copy, scale=gsl[:, b:b + 1]).then_inc(sm["yhi"], 1)
                                if two_more and m == 0:
                                    upper(p + 2, 3)
                            if two_more and b == 0:
                                upper(p + 1, 5)
                                slots_in(half + 1)

                        run_pairs(act, stage)

                    def dense():
                        Dense.act_stage(act, 0, 0, 0, False)
                        for i in range(3):
                            Dense.upper(act, 1, 1, 0, i)
                        Dense.loop(act, lambda *s: Dense.act_stage(act, *s))
                    by_load(act, sparse, dense)

                @block.vector
                def _(dve):
                    for i in range(3):
                        dve.sem_inc(lo_done[i], 1)

                    def sparse():
                        def lower(p, u):
                            dve.wait_ge(whi[u], p + 1)
                            if u % 3 < 2:
                                wait(dve, gu_mm[u // 3], p)
                            dve.tensor_tensor(lo[:, u, :], raw[:, u, :], hi[:, u, :].bitcast(F32), ALU.subtract).then_inc(wlo[u], 1)

                        def slots_in(q, rounds=range(4)):
                            for r in rounds:
                                dve.wait_ge(sm["xhi"], 4 * q + r + 1)
                                dve.tensor_tensor(X_lower(r), gathered(r), X_upper(r).bitcast(F32), ALU.subtract)\
                                   .then_inc(sm["xlo"], 1)

                        def total(p, x):
                            dve.wait_ge(part_done[x], p + 1)
                            wait(dve, sm["sact"], p)
                            q = slice(x * SLOTS, (x + 1) * SLOTS)
                            dve.tensor_tensor(gu[q, :], part[q, :], psum[q, 4 + x, :], ALU.add).then_inc(sum_done[x], 1)

                        def build(q):
                            wait(dve, sm["ptmm"], 2 * q)
                            where = (slice(4 * q, 4 * q + 4) if isinstance(q, int) else bass.ds(4 * q, 4))
                            dve.tensor_tensor(pick[:, :, :].rearrange("p a (x s) -> p a x s", x=4),
                                              slot_no[:, :].unsqueeze(1).unsqueeze(1).broadcast_to([P, TC, 4, SLOTS]),
                                              slot_of[:, :, where].unsqueeze(3).broadcast_to([P, TC, 4, SLOTS]),
                                              ALU.is_equal).then_inc(sm["pick"], 1)
                            dve.tensor_copy(gq[:, :, :], gate_of[:, :, where]).then_inc(sm["gates"], 1)

                        build(0)
                        Dense.dve_stage(dve, 0, 0, 0, False)
                        slots_in(0, range(2))
                        lower(0, 0)
                        lower(0, 1)
                        slots_in(0, range(2, 4))
                        for u in (2, 3, 4):
                            lower(0, u)
                        dve.wait_ge(mm_done[2], 1)
                        total(0, 0)
                        lower(1, 0)
                        lower(1, 1)

                        def stage(p, b, half, more):
                            two_more = more and not (isinstance(p, int) and p == NP - 2)
                            total(p, 1)
                            if more:
                                lower(p + 1, 3)
                            dve.wait_ge(sm["silu"], p + 1)
                            dve.wait_ge(sum_done[1], p + 1)
                            dve.tensor_tensor(av[:, :], av[:, :], gu[:, D_EXPERT:], ALU.mult).then_inc(sm["sact"], 1)
                            if more:
                                lower(p + 1, 4)
                            dve.wait_ge(sm["hhi"], p + 1)
                            dve.tensor_tensor(hid_slots(hidl), R1[:, 0:SEQ].rearrange("p (j x s) -> p j x s", j=2, x=2),
                                              hid_slots(hidh).bitcast(F32), ALU.subtract).then_inc(sm["hlo"], 1)
                            if not (isinstance(p, int) and p == 0):
                                lower(p, 2)
                            if more:
                                total(p + 1, 0)
                            if two_more:
                                if b == 0:
                                    build(half + 1)
                                lower(p + 2, 0)
                            for m in range(2):
                                dve.wait_ge(sm["yhi"], 2 * p + m + 1)
                                dve.scalar_tensor_tensor(out=yl[:, m, :], in0=psum[:, 6 + m, :], scalar=gsl[:, b:b + 1],
                                                         in1=yh[:, m, :].bitcast(F32), op0=ALU.mult, op1=ALU.subtract)\
                                   .then_inc(sm["ylo"], 1)
                                if two_more and m == 0:
                                    lower(p + 2, 1)
                            if two_more and b == 0:
                                slots_in(half + 1)
                        run_pairs(dve, stage)

                    def dense():
                        Dense.dve_stage(dve, 0, 0, 0, False)
                        for i in range(3):
                            Dense.lower(dve, 1, 1, 0, i)
                        Dense.loop(dve, lambda *s: Dense.dve_stage(dve, *s))
                    by_load(dve, sparse, dense)

                @block.tensor
                def _(pe):
                    for i in range(2):
                        pe.sem_inc(mm_done[i], 1)

                    def sparse():
                        def gather(q, r):
                            if r >= 2:
                                pe.wait_ge(sm["xlo"], 4 * q + r - 1)
                            for kk in range(2):
                                for s, x in enumerate((xh, xl)):
                                    for a in range(TC):
                                        last = pe.matmul(psum[:, 6 + r % 2, kk * 2 * P:(kk + 1) * 2 * P],
                                                         x[:, a, 2 * r + kk::KC], pick[:, a, :],
                                                         start=(s == 0 and a == 0), stop=(s == 1 and a == TC - 1))
                            last.then_inc(sm["gather"], 1)

                        def picks(p, b, half):
                            if b == 0:
                                pe.wait_ge(sm["xlo"], 4 * half + 3)
                            elif isinstance(p, int) and p == 1:
                                pe.wait_ge(sm["gsl"], 2)
                            wait(pe, sm["ylo"], 2 * (p - 1))
                            for a in range(TC):
                                pe.transpose(R0[:, a * P:a * P + P], pick[:, a, b * P:b * P + P].bitcast(F32), ident[:, :])
                            pe.wait_ge(sm["gates"], half + 1)
                            for a in range(TC):
                                last = pe.matmul(R0[:, SEQ:SEQ + 2], pick[:, a, b * P:b * P + P].bitcast(F32), gq[:, a, 2 * b:2 * b + 2],
                                                 start=(a == 0), stop=(a == TC - 1))
                            last.then_inc(sm["ptmm"], 1)

                        def gate_up(p, b, half, x, s):
                            if s == 0:
                                pe.wait_ge(sm["xlo"], 4 * half + 4)
                                wait(pe, sum_done[x], p)
                            w, ready = ((hi, whi), (lo, wlo))[s]
                            for i in range(2):
                                pe.wait_ge(ready[3 * x + i], p + 1)
                            for k in range(KC):
                                last = pe.matmul(CAB[x].rearrange("p (i f) -> p i f", i=2), X[:, 2 * b + x, k, :],
                                                 w[:, 3 * x:3 * x + 2, k * D_EXPERT:(k + 1) * D_EXPERT],
                                                 start=(s == 0 and k == 0), stop=(s == 1 and k == KC - 1))
                            last.then_inc((gu_hi, gu_mm)[s][x], 1)

                        def hidden(p, half, final):
                            pe.wait_ge(sm["sact"], p + 1)
                            for j in range(2):
                                last = pe.transpose(R1[:, j * P:j * P + P], av[:, j::2], ident[:, :])
                            last.then_inc(sm["htmm"], 1)

                        def down(p, final):
                            pe.wait_ge(sm["hlo"], p + 1)
                            pe.wait_ge(sm["gsl"], (2 * p + 4) if not final else 2 * NP)
                            for m in range(2):
                                for s, (hd, w) in enumerate(((hidh, hi), (hidl, hi), (hidh, lo))):
                                    for x in range(2):
                                        if m == 0 and s != 1:
                                            pe.wait_ge((whi if s == 0 else wlo)[3 * x + 2], p + 1)
                                        for j in range(2):
                                            last = pe.matmul(psum[:, 6 + m, :], hd[:, x, j, :],
                                                             w[:, 3 * x + 2, j * D_MODEL + m * 512:j * D_MODEL + m * 512 + 512],
                                                             start=(x == 0 and s == 0 and j == 0),
                                                             stop=(x == 1 and s == 2 and j == 1))
                                last.then_inc(sm["ymm"], 1)

                        def combine(p, b, m, final):
                            pe.wait_ge(sm["ylo"], 2 * p + m + 1)
                            for a in range(TC):
                                for s, y in enumerate((yh, yl)):
                                    last = pe.matmul(psum[:, 2 * a + m, :], pickT[:, b, a * P:a * P + P], y[:, m, :],
                                                     start=False, stop=(final and s == 1), skip_group_check=True)
                            if m == 1:
                                last.then_inc(sm["comb"], 1)

                        def stage(p, b, half, more):
                            nxt = (p + 1, 1 - b, half + b)
                            next_quad = more and b == 0 and not (isinstance(p, int) and p == NP - 2)
                            if more:
                                picks(*nxt)
                                gate_up(*nxt, 0, 0)
                                gate_up(*nxt, 0, 1)
                            hidden(p, half, not more)
                            if more:
                                gate_up(*nxt, 1, 0)
                            down(p, not more)
                            if more:
                                gate_up(*nxt, 1, 1)
                            if next_quad:
                                pe.wait_ge(sm["pick"], half + 2)
                            for m in range(2):
                                combine(p, b, m, not more)
                                if next_quad:
                                    gather(half + 1, m)
                            if next_quad:
                                gather(half + 1, 2)
                                gather(half + 1, 3)

                        pe.wait_ge(sm["pick"], 1)
                        gather(0, 0)
                        gather(0, 1)
                        Dense.down(pe, 0, 0)
                        gather(0, 2)
                        gather(0, 3)
                        picks(0, 0, 0)
                        for x in range(2):
                            for s in range(2):
                                gate_up(0, 0, 0, x, s)
                        run_pairs(pe, stage)

                    def dense():
                        Dense.down(pe, 0, 0)
                        Dense.gate_up(pe, 1, 1)

                        def stage(n, b, half, more):
                            if more:
                                Dense.gate_up(pe, n + 1, 1 - b)
                            Dense.down(pe, n, b)
                        Dense.loop(pe, stage)
                    by_load(pe, sparse, dense)

        scale_a = A_HD ** -0.5
        ar = Arena("a")
        xT = ar("xT", [P, KC, SEQ])
        kT = ar("kT", [P, SEQ])
        v_a = ar("v", [P, TC, A_HD])
        sel = ar("sel", [P, LINE])
        bias_in_a = ar("bias", [P, 2, 2, LINE])
        bias_sel = ar("bias_sel", [P, 2, 2, LINE])
        q_a = ar("q", [P, 2, 2, SEQ])
        wq_hi_at = ar.at
        wq_hi = ar("wq_hi", [P, 2, UNIT], F32R)
        mark = ar.at - arena_at
        qiT = ar("qiT", [P, IDX_HEADS // 2, SEQ])
        kiT = ar("kiT", [P, SEQ])
        wi = ar("wi", [P, TC, IDX_HEADS])
        rel = ar("rel", [P, 2, SEQ])
        score = ar("score", [P, TC, SEQ])
        best = ar("best", [P, TC, 8])
        causal = ar("causal", [P, P])
        lines = ar("lines", [REL_HEADS, 1 + len(B_GROUPS), LINE])
        rel_tab = ar("rel_tab", [REL_BUCKETS + 1, REL_HEADS])
        hot = ar("hot", [REL_BUCKETS + 1, 1 + len(B_GROUPS), LINE])

        made = []
        prelude_scope = ExitStack()
        q_in = [sem(f"qa_in{i}") for i in range(2)]
        wq_upper, wq_lower = sem("wq_upper"), sem("wq_lower")
        bias_in = [sem(f"bias_a_in{i}") for i in range(2)]
        all_sem, sem = sem, phase_sems(prelude_scope, made)
        x_in, h_in, c_in, rel_in, neg_done = sem("x_in"), sem("h_in"), sem("const_in"), sem("rel_in"), sem("masked_row")
        wa_in = [sem(f"wa_in{i}") for i in range(4)]
        x_upper = sem("x_upper")
        line_mm, line_ev, line_dram = sem("line_mm"), sem("line_ev"), sem("line_dram")
        pre_mm, pre_ev, s_mm, s_relu, s_acc, tk, sel_done = (sem("pre_mm"), sem("pre_ev"), sem("score_mm"), sem("score_relu"),
                                                             sem("score_acc"), sem("topk_step"), sem("sel_done"))
        wa = t["a_w_in_parts"]

        def load_q(eng, j, b):
            eng.dma_start(raw[:, 4 + b, :], t["a_w_q"][j]).then_inc(q_in[b], 16)


        def a_upper(act, j, b, half, i):
            act.wait_ge(q_in[b], 16 * half + 16)
            act.activation(wq_hi[:, b, :], raw[:, 4 + b, :], ACT.Copy).then_inc(wq_upper, 1)

        def a_lower(dve, j, b, half, i):
            dve.wait_ge(wq_upper, j + 1)
            dve.tensor_tensor(raw_low[:, 4 + b, :], raw[:, 4 + b, :], wq_hi[:, b, :].bitcast(F32), ALU.subtract).then_inc(wq_lower, 1)

        def a_project(pe, j, b, half, i, bank=0):
            if i == 0:
                pe.wait_ge(wq_lower, j + 1)
            for step, (w, x) in enumerate(((wq_hi[:, b, :], xTh), (wq_hi[:, b, :], xTl), (raw_low[:, 4 + b, :], xTh))):
                wq = w.rearrange("p (k c) -> p k c", k=KC)
                for k in range(KC):
                    last = pe.matmul(psum[:, bank + i % 2, 0:SEQ], wq[:, k, i * P:i * P + P], x[:, k, :],
                                     start=(step == 0 and k == 0), stop=(step == 2 and k == KC - 1))
            return last

        with nc.Block() as block:
            @block.sync
            def _(sp):
                sp.dma_start(rel_tab[0:REL_BUCKETS, :], t["rel_bias"]).then_inc(rel_in, 16)
                sp.dma_start(hot[:, :, :], t["hot"]).then_inc(rel_in, 16)
                sp.dma_start(xT[:, :, :], t["x_T"]).then_inc(x_in, 16)
                sp.dma_start(raw[:, 0, 0:KC * 136], t["a_w_ki"]).then_inc(wa_in[0], 16)
                for i in range(2):
                    sp.dma_start(raw[:, 1 + i, :], wa[i]).then_inc(wa_in[1 + i], 16)
                sp.dma_start(causal[:, :], t["causal"]).then_inc(c_in, 16)
                sp.dma_start(raw[:, 3, :], wa[2]).then_inc(wa_in[3], 16)
                sp.dma_start(ident[:, :], t["ident"]).then_inc(c_in, 16)
                load_q(sp, 0, 0)
                load_q(sp, 1, 1)
                sp.dma_start(h[:, :, :], t["x"][0].rearrange("(a p) d -> p a d", p=P)).then_inc(h_in, 16)
                sp.wait_ge(line_ev, 4)
                sp.dma_start(lines_d.rearrange("g h m -> h g m"), lines[:, :, :]).then_inc(line_dram, 16)
                sp.wait_ge(line_dram, 16)
                for j in range(2):
                    sp.dma_start(bias_in_a[:, j, :, SEQ:LINE], bias_tile(0, 1, j, P)[:, 0]).then_inc(bias_in[j], 16)
                    sp.dma_start(bias_in_a[:, j, :, 0:SEQ], bias_tile(0, 1, j, SEQ)[:, 0]).then_inc(bias_in[j], 16)
                sp.wait_ge(h_in, 16)
                sp.wait_ge(c_in, 32)

            @block.gpsimd
            def _(pool):
                pool.memset(rel_tab[REL_BUCKETS:REL_BUCKETS + 1, :], MASKED).then_inc(neg_done, 1)

            @block.tensor
            def _(pe):
                pe.wait_ge(rel_in, 32)
                pe.wait_ge(neg_done, 1)
                for g in range(1 + len(B_GROUPS)):
                    pe.matmul(psum[0:REL_HEADS, 2 + g, 0:LINE], rel_tab[:, :], hot[:, g, :], start=True, stop=True)\
                      .then_inc(line_mm, 1)
                pe.wait_ge(x_in, 16)
                pe.wait_ge(wa_in[0], 16)
                wk = raw[:, 0, 0:KC * 136].rearrange("p (k c) -> p k c", k=KC)
                for k in range(KC):
                    last = pe.matmul(psum[:, 0, 0:SEQ], wk[:, k, 0:P], xT[:, k, :], start=(k == 0), stop=(k == KC - 1))
                last.then_inc(pre_mm, 1)
                for c in range(4):
                    if c % 2 == 0:
                        pe.wait_ge(wa_in[1 + c // 2], 16)
                    wv = raw[:, 1 + c // 2, :].rearrange("p (k c) -> p k c", k=KC)
                    pe.wait_ge(line_ev, c + 1)
                    for k in range(KC):
                        last = pe.matmul(psum[:, 2 + c, 0:SEQ], wv[:, k, (c % 2) * P:(c % 2) * P + P], xT[:, k, :],
                                         start=(k == 0), stop=(k == KC - 1))
                    last.then_inc(pre_mm, 1)
                for a in range(TC):
                    for k in range(KC):
                        last = pe.matmul(psum[:, 1, a * IDX_HEADS:(a + 1) * IDX_HEADS], xT[:, k, a * P:a * P + P],
                                         wk[:, k, P:P + IDX_HEADS], start=(k == 0), stop=(k == KC - 1))
                last.then_inc(pre_mm, 1)
                pe.wait_ge(pre_ev, 6)
                for n in range(TC * IDX_HEADS):
                    a, hd = TC - 1 - n // IDX_HEADS, n % IDX_HEADS
                    wait(pe, s_relu, n - 1)
                    r0 = IDX_HD * (hd % 2)
                    pe.matmul(psum[:, n % 2, 0:P * (a + 1)], qiT[r0:r0 + IDX_HD, hd // 2, a * P:a * P + P],
                              kiT[r0:r0 + IDX_HD, 0:P * (a + 1)], start=True, stop=True).then_inc(s_mm, 1)
                    if n == IDX_HEADS - 1:
                        pe.wait_ge(wa_in[3], 16)
                        wv = raw[:, 3, :].rearrange("p (k c) -> p k c", k=KC)
                        for k in range(KC):
                            last = pe.matmul(psum[:, 6, 0:SEQ], wv[:, k, 0:A_HD], xT[:, k, :], start=(k == 0), stop=(k == KC - 1))
                        last.then_inc(pre_mm, 1)
                        for aa in range(TC):
                            for k in range(KC):
                                last = pe.matmul(psum[:, 7, aa * A_HD:(aa + 1) * A_HD], xT[:, k, aa * P:aa * P + P],
                                                 wv[:, k, A_HD:2 * A_HD], start=(k == 0), stop=(k == KC - 1))
                        last.then_inc(pre_mm, 1)
                for i in range(2):
                    a_project(pe, 0, 0, 0, i, 4).then_inc(pre_mm, 1)

            @block.scalar
            def _(act):
                act.wait_ge(x_in, 16)
                act.activation(xTh[:, :, :], xT[:, :, :], ACT.Copy).then_inc(x_upper, 1)
                for g in range(1 + len(B_GROUPS)):
                    act.wait_ge(line_mm, g + 1)
                    act.activation(lines[:, g, :], psum[0:REL_HEADS, 2 + g, 0:LINE], ACT.Copy).then_inc(line_ev, 1)
                act.wait_ge(pre_mm, 1)
                act.activation(kiT[:, :], psum[:, 0, 0:SEQ], ACT.Copy).then_inc(pre_ev, 1)
                for c in range(4):
                    act.wait_ge(pre_mm, 2 + c)
                    act.activation(qiT[:, c, :], psum[:, 2 + c, 0:SEQ], ACT.Copy).then_inc(pre_ev, 1)
                    if c % 2 == 0:
                        a_upper(act, c // 2, c // 2, 0, 0)
                act.wait_ge(pre_mm, 6)
                act.activation(wi[:, :, :], psum[:, 1, 0:TC * IDX_HEADS].rearrange("p (a h) -> p a h", a=TC), ACT.Copy,
                               scale=IDX_HEADS ** -0.5).then_inc(pre_ev, 1)
                for n in range(TC * IDX_HEADS):
                    a = TC - 1 - n // IDX_HEADS
                    act.wait_ge(s_mm, n + 1)
                    wait(act, s_acc, n - 1)
                    act.activation(rel[:, n % 2, 0:P * (a + 1)], psum[:, n % 2, 0:P * (a + 1)], ACT.Relu,
                                   scale=IDX_HD ** -0.5).then_inc(s_relu, 1)
                act.wait_ge(pre_mm, 7)
                act.activation(kT[:, :], psum[:, 6, 0:SEQ], ACT.Copy).then_inc(pre_ev, 1)
                act.wait_ge(pre_mm, 8)
                act.activation(v_a[:, :, :], psum[:, 7, 0:TC * A_HD].rearrange("p (a e) -> p a e", a=TC), ACT.Copy).then_inc(pre_ev, 1)
                for i in range(2):
                    act.wait_ge(pre_mm, 9 + i)
                    act.activation(q_a[:, 0, i, :], psum[:, 4 + i, 0:SEQ], ACT.Copy)

            @block.vector
            def _(dve):
                steps = [0]

                def link(ins):
                    steps[0] += 1
                    ins.then_inc(tk, 1)
                    dve.wait_ge(tk, steps[0])

                dve.wait_ge(x_upper, 1)
                dve.tensor_tensor(xTl[:, :, :], xT[:, :, :], xTh[:, :, :].bitcast(F32), ALU.subtract)
                for j in range(2):
                    a_lower(dve, j, j, 0, 0)
                dve.wait_ge(pre_ev, 6)
                dve.wait_ge(c_in, 32)
                for ai in range(TC):
                    a = TC - 1 - ai
                    n_keys = P * (a + 1)
                    sc = score[:, a, 0:n_keys]
                    for hd in range(IDX_HEADS):
                        n = ai * IDX_HEADS + hd
                        dve.wait_ge(s_relu, n + 1)
                        if hd == 0:
                            dve.tensor_scalar(sc, rel[:, n % 2, 0:n_keys], wi[:, a, hd:hd + 1], None, ALU.mult).then_inc(s_acc, 1)
                        else:
                            dve.wait_ge(s_acc, n)
                            dve.scalar_tensor_tensor(out=sc, in0=rel[:, n % 2, 0:n_keys], scalar=wi[:, a, hd:hd + 1], in1=sc,
                                                     op0=ALU.mult, op1=ALU.add).then_inc(s_acc, 1)
                    dve.wait_ge(s_acc, (ai + 1) * IDX_HEADS)
                    dg = score[:, a, a * P:a * P + P]
                    link(dve.tensor_tensor(dg, dg, causal[:, :], ALU.add))
                    for rnd in range(TOPK_KEYS // 8):
                        link(dve.max(best[:, a, :], sc))
                        link(dve.match_replace(sc, best[:, a, :], sc, TAKEN))
                    dst = sel[:, a * P:a * P + n_keys]
                    link(dve.tensor_scalar(sc, sc, TAKEN, -MASKED, ALU.is_equal, ALU.mult))
                    link(dve.tensor_scalar(dst, sc, MASKED, None, ALU.add))

        prelude_scope.close()
        spent[:] = made
        sem = all_sem
        wo_a = t["a_w_o"][0].rearrange("(u c p) n -> u p c n", c=2, p=P)
        sel_used = sem("bias_sel_ready")

        def a_pair(sp, pr_done, j, b):
            sp.wait_ge(pr_done, 2 * j - 2)
            load_q(sp, j, b)
            sp.wait_ge(sel_used, 2 * j - 2)
            sp.dma_start(bias_in_a[:, b, :, SEQ:LINE], bias_tile(0, 1, j, P)[:, 0]).then_inc(bias_in[b], 16)
            sp.dma_start(bias_in_a[:, b, :, 0:SEQ], bias_tile(0, 1, j, SEQ)[:, 0]).then_inc(bias_in[b], 16)

        def a_first(sp, pr_done):
            for j in (2, 3):
                a_pair(sp, pr_done, j, j % 2)

        def a_loop(sp, pr_done, stt_done):
            with sp.Fori(1, STEPS // 2 - 1) as it:
                for b in range(2):
                    a_pair(sp, pr_done, 2 * it + 2 + b, b)

        def a_pool(pool, stt_done):
            def combine(j, b, half, first):
                pool.wait_ge(bias_in[b], 32 * half + 32)
                if not first:
                    pool.wait_ge(stt_done, 2 * j - 2)
                for c in range(2):
                    pool.tensor_tensor(bias_sel[:, b, c, :], bias_in_a[:, b, c, ::-1], sel[:, :], ALU.add).then_inc(sel_used, 1)
            combine(0, 0, 0, True)
            combine(1, 1, 0, True)
            with pool.Fori(0, STEPS // 2 - 1) as it:
                combine(2 * it + 2, 0, it + 1, False)
                combine(2 * it + 3, 1, it + 1, False)

        raw_in = [[sem(f"raw{l}_in{i}") for i in range(6)] for l in range(DEPTH)]
        gate_in = [[sem(f"gate{l}_in{i}") for i in range(2)] for l in range(DEPTH)]
        load_e = [expert_loads(l, raw_in[l]) for l in range(DEPTH)]

        def prefetch(l):
            def f(sp):
                for n, ring_set in ((0, 1), (1, 0)):
                    for i in range(3):
                        load_e[l](sp, n, n, 3 * ring_set + i)
            return f

        a2 = Arena("a2", mark)
        attention(
            "a_", 1, scale_a, 2, a_project, a_first, a_loop, prefetch(0),
            bias_ready=lambda dve, j, b, half: dve.wait_ge(sel_used, 2 * j + 2),
            bias_of=lambda b, c: bias_sel[:, b, c, :],
            q_of=lambda b, c, g, a: q_a[:, b, c, a * P:a * P + P],
            k_of=lambda b, c, g, a: kT[:, 0:P * (a + 1)],
            v_of=lambda b, c, g, s: v_a[:, s, :],
            evac_piece=lambda act, b, i: act.activation(q_a[:, b, i, :], psum[:, i % 2, 0:SEQ], ACT.Copy),
            o_step=lambda OT, c: OT[:, c * SEQ:(c + 1) * SEQ],
            o_chunks=A_HEADS, wo_view=lambda u: wo_a[u], wo_units=A_HEADS // 2,
            ar=a2, far=a2, upper=a_upper, lower=a_lower, upper_at={("head", 0): [(2, 0)]}, lower_at={1: [(2, 0)]},
            first_lowers=(), second_logits=0, extra_pool=a_pool,
            first_done=True, w_hi_at=wq_hi_at, w_hi_size=8 * UNIT)

        def router_of(l):
            return (t["moe_w_router"][l].rearrange("(p k) e -> p k e", k=KC), t["moe_bias"][l])

        def ln_rows(l, i):
            return (t["ln_g"][l, i], t["ln_b"][l, i])

        def norm_arena(tag, start):
            return Arena(tag)("xT", [P, KC, SEQ]), Arena(tag + "s", start=start)

        xF, ar = norm_arena("n0", behind_weights)
        norm("n0_", ln_rows(0, 0), xF, ar, router=router_of(0), gates=gates_d[0], **SharedSplit(0, load_e[0], raw_in[0]).hooks())

        G = len(B_GROUPS)
        WB = KC * G * P
        rawB = raw[:, :, :].rearrange("p u n -> p (u n)")[:, 0:3 * WB].rearrange("p (s k g c) -> p s k g c", s=3, k=KC, g=G)
        rawB_low = raw_low[:, :, :].rearrange("p u n -> p (u n)")[:, 0:3 * WB].rearrange("p (s n) -> p s n", s=3)
        wb_in = [sem(f"wb_in{i}") for i in range(3)]
        wb_upper = [sem(f"wb_upper{i}") for i in range(3)]
        wb_lower = [sem(f"wb_lower{i}") for i in range(3)]
        bias_b_in = [sem(f"bias_b_in{i}") for i in range(2)]

        def load_b(eng, j, i):
            eng.dma_start(rawB[:, i, :, :, :].rearrange("p k g c -> p (k g c)"), t["b_w_in_parts"][j, i]).then_inc(wb_in[i], 16)

        def first_b(sp, taken):
            for i, units in enumerate(((0, 1), (1, 2), (3, 4))):
                for u in units:
                    sp.wait_ge(*taken[u])
                load_b(sp, 0, i)

        experts(0, load_e[0], raw_in[0], gate_in[0], gates_d[0], load_after=first_b)

        ar = Arena("b")
        far = Arena("b_far", start=xh_at - arena_at)
        wb_hi_at = ar.at
        wb_hi = ar("w_hi", [P, 3, WB], F32R)

        def b_upper(act, j, b, half, i):
            act.wait_ge(wb_in[i], 16 * j + 16)
            act.activation(wb_hi[:, i, :], rawB[:, i, :, :, :].rearrange("p k g c -> p (k g c)"), ACT.Copy).then_inc(wb_upper[i], 1)

        def b_lower(dve, j, b, half, i):
            dve.wait_ge(wb_upper[i], j + 1)
            dve.tensor_tensor(rawB_low[:, i, :], rawB[:, i, :, :, :].rearrange("p k g c -> p (k g c)"),
                              wb_hi[:, i, :].bitcast(F32), ALU.subtract).then_inc(wb_lower[i], 1)

        def b_split_first(eng, part, parts):
            for i in parts:
                part(eng, 0, 0, 0, i)

        xF = Arena("n1x", start=12 * WB)("xT", [P, KC, SEQ])
        norm("n1_", ln_rows(0, 1), xF, Arena("n1s", start=behind_weights),
             act_first=lambda act: b_split_first(act, b_upper, (0,)), act_second=lambda act: b_split_first(act, b_upper, (1, 2)),
             pool_work=lambda pool: b_split_first(pool, b_lower, (0, 1)))

        qk = ar("qk", [P, 2, 2, G, SEQ])
        vb = ar("v", [P, 2, TC, G * P])
        bias_b = ar("bias", [P, 2, 2, G, LINE])

        def load_bias(sp, j, b):
            for c in range(2):
                for lo_, n_ in ((0, SEQ), (SEQ, P)):
                    src = bias_tile(1, G, j, n_)[:, :, c]
                    sp.dma_start(bias_b[:, b, c, :, lo_:lo_ + n_], src).then_inc(bias_b_in[b], 16)

        def b_weights(sp, pr_done, j):
            for i in range(3):
                sp.wait_ge(pr_done, 8 * j - 8 + (3, 6, 8)[i])
                load_b(sp, j, i)

        def b_first(sp, pr_done):
            for j in range(2):
                load_bias(sp, j, j)
            b_weights(sp, pr_done, 1)

        def b_loop(sp, pr_done, stt_done):
            with sp.Fori(0, STEPS // 2 - 1) as it:
                for b in range(2):
                    j = 2 * it + 2 + b
                    b_weights(sp, pr_done, j)
                    sp.wait_ge(stt_done, 2 * j - 2)
                    load_bias(sp, j, b)

        def b_project(pe, j, b, half, i):
            part = i // 3
            if i in (0, 3, 6):
                pe.wait_ge(wb_lower[part], j + 1)
            for step, (w, x) in enumerate(((wb_hi[:, part, :], xTh), (wb_hi[:, part, :], xTl), (rawB_low[:, part, :], xTh))):
                wk = w.rearrange("p (k n) -> p k n", k=KC)
                for k in range(KC):
                    flags = dict(start=(step == 0 and k == 0), stop=(step == 2 and k == KC - 1))
                    if i < 6:
                        last = pe.matmul(psum[:, i % 2, 0:SEQ], wk[:, k, (i % 3) * P:(i % 3) * P + P], x[:, k, :], **flags)
                    else:
                        last = pe.matmul(psum[:, i % 2, 0:G * P], x[:, k, (i - 6) * P:(i - 5) * P], wk[:, k, :], **flags)
            return last

        def b_evac(act, b, i):
            if i < 6:
                return act.activation(qk[:, b, i // 3, i % 3, :], psum[:, i % 2, 0:SEQ], ACT.Copy)
            return act.activation(vb[:, b, i - 6, :], psum[:, i % 2, 0:G * P], ACT.Copy)

        wo_b = t["b_w_o"][0].rearrange("(u c p) n -> u p c n", c=2, p=P)
        attention(
            "b_", G, B_HD ** -0.5, 8, b_project, b_first, b_loop, prefetch(1),
            bias_ready=lambda dve, j, b, half: dve.wait_ge(bias_b_in[b], 64 * half + 64),
            bias_of=lambda b, c: bias_b[:, b, c, :, ::-1],
            q_of=lambda b, c, g, a: qk[c * B_HD:(c + 1) * B_HD, b, 0, g, a * P:a * P + P],
            k_of=lambda b, c, g, a: qk[c * B_HD:(c + 1) * B_HD, b, 1, g, 0:P * (a + 1)],
            v_of=lambda b, c, g, s: vb[:, b, s, g * P + c * B_HD:g * P + (c + 1) * B_HD],
            evac_piece=b_evac,
            o_step=lambda OT, c: OT[c * B_HD:(c + 1) * B_HD, 0:SEQ],
            o_chunks=B_HEADS // 2, wo_view=lambda u: wo_b[u], wo_units=B_HEADS // 4, ar=ar, far=far,
            upper=b_upper, lower=b_lower, upper_at={0: [(1, 1)], 1: [(1, 2)], 4: [(2, 0)]},
            lower_at={0: [(1, 1), (1, 2)], 1: [(2, 0)]}, second_logits=2,
            first_lowers=((0, 0, 0, 2), (1, 1, 0, 0)), w_hi_at=wb_hi_at, w_hi_size=12 * WB)

        xF, ar = norm_arena("n2", behind_weights)
        norm("n2_", ln_rows(1, 0), xF, ar, router=router_of(1), gates=gates_d[1], **SharedSplit(1, load_e[1], raw_in[1]).hooks())
        experts(1, load_e[1], raw_in[1], gate_in[1], gates_d[1])
        xF, ar = norm_arena("n3", behind_weights)
        norm("n3_", ln_rows(1, 1), xF, ar, final=True)


def t5_bucket(dist):
    exact = REL_BUCKETS // 2
    if dist < exact:
        return dist
    large = exact + int(math.log(dist / exact) / math.log(REL_MAX_DIST / exact) * (REL_BUCKETS - exact))
    return min(large, REL_BUCKETS - 1)


def bucket_table():
    hot = np.zeros((REL_BUCKETS + 1, 1 + len(B_GROUPS), LINE), np.float32)
    for g, (window, dil) in enumerate(((SEQ, 1),) + B_GROUPS):
        for m in range(LINE):
            dist = m - (P - 1)
            reach = SEQ if g == 0 else window // dil
            ok = dist >= 0 and dist % dil == 0 and dist // dil <= reach
            hot[t5_bucket(dist) if ok else REL_BUCKETS, g, m] = 1.0
    return hot


def kernel(**inputs):
    import concourse.bacc as bacc
    from concourse.bass_utils import run_bass_kernel_spmd

    a = {n: np.ascontiguousarray(inputs[n]) for n in
         ("x", "rel_bias", "a_w_o", "b_w_o", "ln_g", "ln_b", "moe_w_router", "moe_bias", "moe_w_gate", "moe_w_up",
          "moe_w_down", "moe_ws_gate", "moe_ws_up", "moe_ws_down")}

    def chunked(w):
        return np.ascontiguousarray(w.reshape(P, KC * w.shape[1]))

    a["x_T"] = np.ascontiguousarray(np.asarray(inputs["x"])[0].T.reshape(P, KC, SEQ))
    w = np.asarray(inputs["a_w_in"])[0]
    nq, nk = A_HEADS * A_HD, A_HEADS * A_HD + 2 * A_HD
    a["a_w_q"] = np.stack([chunked(w[:, j * 256:(j + 1) * 256]) for j in range(STEPS)])
    ni = IDX_HEADS * IDX_HD
    a["a_w_in_parts"] = np.stack([chunked(w[:, nk:nk + 256]), chunked(w[:, nk + 256:nk + 512]), chunked(w[:, nq:nk])])
    ki = w[:, nk + ni:nk + ni + IDX_HD]
    a["a_w_ki"] = chunked(np.concatenate([ki, ki, w[:, nk + ni + IDX_HD:]], axis=1))
    wb = np.asarray(inputs["b_w_in"])[0].reshape(P, KC, len(B_GROUPS), 3, STEPS, P)
    a["b_w_in_parts"] = np.ascontiguousarray(wb.transpose(4, 3, 0, 1, 2, 5)).reshape(STEPS, 3, P, -1)
    a["hot"] = bucket_table()
    a["ident"] = np.eye(P, dtype=np.float32)
    a["causal"] = np.where(np.arange(P)[None, :] <= np.arange(P)[:, None], 0.0, MASKED).astype(np.float32)
    earlier = (np.arange(N_GROUPS)[None, :] < np.arange(N_GROUPS)[:, None]).astype(np.float32)
    a["tri"] = np.ascontiguousarray(np.broadcast_to(earlier, (P, N_GROUPS, N_GROUPS)))

    upto = np.arange(P)
    a["before"] = np.stack([(upto[:, None] < upto[None, :]), np.ones((P, P), bool)], axis=1).astype(np.float32)
    a["slot_no"] = np.ascontiguousarray(np.broadcast_to(np.arange(SLOTS, dtype=np.float32), (P, SLOTS)))

    nc = bacc.Bacc("TRN2", target_bir_lowering=False, num_devices=1)
    t = {n: nc.dram_tensor(f"in_{n}", v.shape, mybir.dt.from_np(v.dtype), kind="ExternalInput").ap() for n, v in a.items()}
    out = nc.dram_tensor("out", (1, SEQ, D_MODEL), F32, kind="ExternalOutput").ap()
    build(nc, t, out)
    r = run_bass_kernel_spmd(nc, [{f"in_{n}": v for n, v in a.items()}], core_ids=[0])
    return r.results[0]["out"]
```
